# Optimizing a Trainium2 kernel written in Bass

```python
import numpy as np
import jax
import jax.numpy as jnp
from jax import lax
import jax, jax.numpy as jnp

D_MODEL = 1024
BATCH = 1
SEQ = 256
DEPTH = 1

D_RNN = 1344
RNN_BLOCKS = 16
RNN_BLOCK_W = D_RNN // RNN_BLOCKS
RNN_CONV_W = 4
LRU_C = 8.0
N_HEADS = 16
N_KV = 4
HEAD_DIM = 64
GROUP = N_HEADS // N_KV
CMP_LEN = 32
CMP_STRIDE = 16
CMP_HIDDEN = 128
SEL_LEN = 64
N_SELECT = 16
WINDOW = 512
Q_BLOCK = 64
D_FF = 3 * D_MODEL
FFN_CONV_W = 3
EPS = 1e-6
NEG = -1e30
FORCE = 1e6


def rms_norm(x, g):
    x32 = x.astype(jnp.float32)
    y = x32 * lax.rsqrt(jnp.mean(x32 * x32, axis=-1, keepdims=True) + EPS)
    return (y * g.astype(jnp.float32)).astype(x.dtype)

def causal_dwconv(x, w, b):
    k = w.shape[0]
    y = lax.conv_general_dilated(x, w[:, None, :].astype(x.dtype), window_strides=(1,),
                                 padding=[(k - 1, 0)], dimension_numbers=('NWC', 'WIO', 'NWC'),
                                 feature_group_count=x.shape[-1])
    return y + b.astype(x.dtype)

def masked_softmax(s, mask):
    p = jax.nn.softmax(jnp.where(mask, s, NEG), axis=-1)
    return p * mask

def rg_lru(x, w_a, b_a, w_x, b_x, lam):
    bsz, s, _ = x.shape
    xb = x.reshape(bsz, s, RNN_BLOCKS, RNN_BLOCK_W)
    r = jax.nn.sigmoid(jnp.einsum('bsnc,ncd->bsnd', xb, w_a).reshape(bsz, s, D_RNN) + b_a)
    i = jax.nn.sigmoid(jnp.einsum('bsnc,ncd->bsnd', xb, w_x).reshape(bsz, s, D_RNN) + b_x)
    log_a = LRU_C * r.astype(jnp.float32) * jax.nn.log_sigmoid(lam.astype(jnp.float32))
    a = jnp.exp(log_a)
    u = jnp.sqrt(-jnp.expm1(2.0 * log_a)) * (i * x).astype(jnp.float32)

    def combine(lhs, rhs):
        a1, b1 = lhs
        a2, b2 = rhs
        return a1 * a2, a2 * b1 + b2

    _, h = lax.associative_scan(combine, (a, u), axis=1)
    return h.astype(x.dtype)

def compress(kv, pe, w1, w2):
    bsz, s, g, hd = kv.shape
    nc = (s - CMP_LEN) // CMP_STRIDE + 1
    pos = np.arange(nc)[:, None] * CMP_STRIDE + np.arange(CMP_LEN)[None, :]
    blocks = kv[:, pos] + pe[None, None, :, None, :]
    blocks = blocks.transpose(0, 3, 1, 2, 4).reshape(bsz, g, nc, CMP_LEN * hd)
    return jax.nn.gelu(blocks @ w1) @ w2

def overlap_matrix(nc, ns):
    i = np.arange(nc)[:, None]
    j = np.arange(ns)[None, :]
    lo = np.maximum(i * CMP_STRIDE, j * SEL_LEN)
    hi = np.minimum(i * CMP_STRIDE + CMP_LEN, (j + 1) * SEL_LEN)
    return jnp.asarray(np.maximum(hi - lo, 0) / CMP_STRIDE, dtype=jnp.float32)

def nsa(q, kc, vc, ks, vs, kw, vw, gates, q_norm_g, k_cmp_norm_g, k_slc_norm_g, k_win_norm_g,
        cmp_pe_k, cmp_w1_k, cmp_w2_k, cmp_pe_v, cmp_w1_v, cmp_w2_v):
    bsz, s, _ = q.shape
    f32 = jnp.float32
    scale = HEAD_DIM ** -0.5

    def heads(t, n):
        return t.reshape(bsz, s, n, HEAD_DIM)

    qh = rms_norm(heads(q, N_HEADS), q_norm_g)
    qh = qh.reshape(bsz, s, N_KV, GROUP, HEAD_DIM).transpose(0, 2, 3, 1, 4)
    k_cmp = rms_norm(compress(heads(kc, N_KV), cmp_pe_k, cmp_w1_k, cmp_w2_k), k_cmp_norm_g)
    v_cmp = compress(heads(vc, N_KV), cmp_pe_v, cmp_w1_v, cmp_w2_v)
    nc = k_cmp.shape[2]
    ns = s // SEL_LEN
    k_slc = rms_norm(heads(ks, N_KV), k_slc_norm_g).transpose(0, 2, 1, 3).reshape(bsz, N_KV, ns, SEL_LEN, HEAD_DIM)
    v_slc = heads(vs, N_KV).transpose(0, 2, 1, 3).reshape(bsz, N_KV, ns, SEL_LEN, HEAD_DIM)
    pad = ((0, 0), (0, 0), (WINDOW, 0), (0, 0))
    k_win = jnp.pad(rms_norm(heads(kw, N_KV), k_win_norm_g).transpose(0, 2, 1, 3), pad)
    v_win = jnp.pad(heads(vw, N_KV).transpose(0, 2, 1, 3), pad)
    g = jax.nn.sigmoid(gates).reshape(bsz, s, N_KV, GROUP, 3).transpose(0, 2, 3, 1, 4)
    overlap = overlap_matrix(nc, ns)
    cmp_end = np.arange(nc) * CMP_STRIDE + CMP_LEN - 1
    n_top = min(N_SELECT, ns)
    gather = jax.vmap(jax.vmap(lambda blk, ix: blk[ix]))
    jb = jnp.arange(ns)

    def block(qi):
        st = qi * Q_BLOCK
        t = st + jnp.arange(Q_BLOCK)
        qb = lax.dynamic_slice_in_dim(qh, st, Q_BLOCK, axis=3)
        gb = lax.dynamic_slice_in_dim(g, st, Q_BLOCK, axis=3)
        sc = jnp.einsum('bgrqd,bgcd->bgrqc', qb, k_cmp).astype(f32) * scale
        p_cmp = masked_softmax(sc, cmp_end[None, :] <= t[:, None])
        o_cmp = jnp.einsum('bgrqc,bgcd->bgrqd', p_cmp.astype(v_cmp.dtype), v_cmp)
        imp = jnp.einsum('bgrqc,cn->bgqn', p_cmp, overlap)
        cur = t // SEL_LEN
        causal_b = jb[None, :] <= cur[:, None]
        forced = (jb[None, :] == 0) | (jb[None, :] == cur[:, None]) | (jb[None, :] == cur[:, None] - 1)
        rank = jnp.where(causal_b, jnp.where(forced, FORCE, imp), -FORCE)
        _, idx = lax.top_k(rank, n_top)
        kg = gather(k_slc, idx)
        vg = gather(v_slc, idx)
        kpos = idx[..., None] * SEL_LEN + jnp.arange(SEL_LEN)
        ok = (idx <= cur[:, None])[..., None] & (kpos <= t[:, None, None])
        sc = jnp.einsum('bgrqd,bgqnld->bgrqnl', qb, kg).astype(f32) * scale
        p = masked_softmax(sc.reshape(bsz, N_KV, GROUP, Q_BLOCK, n_top * SEL_LEN),
                           ok.reshape(bsz, N_KV, 1, Q_BLOCK, n_top * SEL_LEN))
        o_slc = jnp.einsum('bgrqm,bgqmd->bgrqd', p.astype(vg.dtype),
                           vg.reshape(bsz, N_KV, Q_BLOCK, n_top * SEL_LEN, HEAD_DIM))
        kwb = lax.dynamic_slice_in_dim(k_win, st, WINDOW + Q_BLOCK, axis=2)
        vwb = lax.dynamic_slice_in_dim(v_win, st, WINDOW + Q_BLOCK, axis=2)
        kp = st - WINDOW + jnp.arange(WINDOW + Q_BLOCK)
        okw = (kp[None, :] <= t[:, None]) & (kp[None, :] > t[:, None] - WINDOW) & (kp[None, :] >= 0)
        sc = jnp.einsum('bgrqd,bgkd->bgrqk', qb, kwb).astype(f32) * scale
        pw = masked_softmax(sc, okw)
        o_win = jnp.einsum('bgrqk,bgkd->bgrqd', pw.astype(vwb.dtype), vwb)
        return gb[..., 0:1] * o_cmp + gb[..., 1:2] * o_slc + gb[..., 2:3] * o_win

    out = lax.map(block, jnp.arange(s // Q_BLOCK))
    return out.transpose(1, 0, 4, 2, 3, 5).reshape(bsz, s, N_HEADS * HEAD_DIM)

def first_inputs(seed: int = 0) -> dict:
    key = jax.random.key(seed)
    k = jax.random.split(key, 28)

    def nrm(kk, shape, scale):
        return jax.random.normal(kk, shape, jnp.float32) * scale

    d, hd = D_MODEL, HEAD_DIM
    n_in = 2 * D_RNN + N_HEADS * hd + 6 * N_KV * hd + 3 * N_HEADS + 2 * d
    u = jax.random.uniform(k[9], (D_RNN,), jnp.float32, 0.9, 0.999)
    sg = u ** (1.0 / LRU_C)
    lam = jnp.log(sg) - jnp.log1p(-sg)
    return {
        'x': nrm(k[0], (BATCH, SEQ, d), 1.0),
        'norm1_g': 1.0 + nrm(k[1], (d,), 0.02),
        'w_in': nrm(k[2], (d, n_in), d ** -0.5),
        'rnn_conv_w': nrm(k[3], (RNN_CONV_W, D_RNN), RNN_CONV_W ** -0.5),
        'rnn_conv_b': nrm(k[4], (D_RNN,), 0.02),
        'rg_w_a': nrm(k[5], (RNN_BLOCKS, RNN_BLOCK_W, RNN_BLOCK_W), RNN_BLOCK_W ** -0.5),
        'rg_b_a': nrm(k[6], (D_RNN,), 0.02),
        'rg_w_x': nrm(k[7], (RNN_BLOCKS, RNN_BLOCK_W, RNN_BLOCK_W), RNN_BLOCK_W ** -0.5),
        'rg_b_x': nrm(k[8], (D_RNN,), 0.02),
        'lru_lambda': lam,
        'w_rnn_out': nrm(k[10], (D_RNN, d), D_RNN ** -0.5),
        'q_norm_g': 1.0 + nrm(k[11], (hd,), 0.02),
        'k_cmp_norm_g': 1.0 + nrm(k[12], (hd,), 0.02),
        'k_slc_norm_g': 1.0 + nrm(k[13], (hd,), 0.02),
        'k_win_norm_g': 1.0 + nrm(k[14], (hd,), 0.02),
        'cmp_pe_k': nrm(k[15], (CMP_LEN, hd), 0.1),
        'cmp_w1_k': nrm(k[16], (CMP_LEN * hd, CMP_HIDDEN), (CMP_LEN * hd) ** -0.5),
        'cmp_w2_k': nrm(k[17], (CMP_HIDDEN, hd), CMP_HIDDEN ** -0.5),
        'cmp_pe_v': nrm(k[18], (CMP_LEN, hd), 0.1),
        'cmp_w1_v': nrm(k[19], (CMP_LEN * hd, CMP_HIDDEN), (CMP_LEN * hd) ** -0.5),
        'cmp_w2_v': nrm(k[20], (CMP_HIDDEN, hd), CMP_HIDDEN ** -0.5),
        'w_attn_out': nrm(k[21], (N_HEADS * hd, d), (N_HEADS * hd) ** -0.5),
        'w_out': nrm(k[22], (d, d), d ** -0.5),
        'norm2_g': 1.0 + nrm(k[23], (d,), 0.02),
        'w_up': nrm(k[24], (d, 2 * D_FF), d ** -0.5),
        'ffn_conv_w': nrm(k[25], (FFN_CONV_W, 2 * D_FF), FFN_CONV_W ** -0.5),
        'ffn_conv_b': nrm(k[26], (2 * D_FF,), 0.02),
        'w_down': nrm(k[27], (D_FF, d), D_FF ** -0.5),
    }

def first_block(x, norm1_g, w_in, rnn_conv_w, rnn_conv_b, rg_w_a, rg_b_a, rg_w_x, rg_b_x, lru_lambda,
              w_rnn_out, q_norm_g, k_cmp_norm_g, k_slc_norm_g, k_win_norm_g, cmp_pe_k, cmp_w1_k, cmp_w2_k,
              cmp_pe_v, cmp_w1_v, cmp_w2_v, w_attn_out, w_out, norm2_g, w_up, ffn_conv_w, ffn_conv_b, w_down):
    kvw = N_KV * HEAD_DIM
    sizes = [D_RNN, D_RNN, N_HEADS * HEAD_DIM] + [kvw] * 6 + [3 * N_HEADS, D_MODEL, D_MODEL]
    splits = np.cumsum(sizes)[:-1].tolist()
    for _ in range(DEPTH):
        h = rms_norm(x, norm1_g)
        proj = h @ w_in
        (rx, rgate, q, kc, vc, ks, vs, kw, vw, nsa_g, mg_rnn, mg_attn) = jnp.split(proj, splits, axis=-1)
        hr = rg_lru(causal_dwconv(rx, rnn_conv_w, rnn_conv_b), rg_w_a, rg_b_a, rg_w_x, rg_b_x, lru_lambda)
        y_rnn = (hr * jax.nn.gelu(rgate)) @ w_rnn_out
        o = nsa(q, kc, vc, ks, vs, kw, vw, nsa_g, q_norm_g, k_cmp_norm_g, k_slc_norm_g, k_win_norm_g,
                cmp_pe_k, cmp_w1_k, cmp_w2_k, cmp_pe_v, cmp_w1_v, cmp_w2_v)
        y_attn = o @ w_attn_out
        x = x + (jax.nn.sigmoid(mg_rnn) * y_rnn + jax.nn.sigmoid(mg_attn) * y_attn) @ w_out
        up = causal_dwconv(rms_norm(x, norm2_g) @ w_up, ffn_conv_w, ffn_conv_b)
        gate, val = jnp.split(up, 2, axis=-1)
        x = x + (jax.nn.gelu(gate) * val) @ w_down
    return x


N_ATTN_HEADS = D_MODEL // (2 * HEAD_DIM)
N_GMLP_GROUPS = D_MODEL // (2 * HEAD_DIM)
ATTN_WIDTH = N_ATTN_HEADS * HEAD_DIM
GMLP_WIDTH = N_GMLP_GROUPS * HEAD_DIM
MIX_WIDTH = ATTN_WIDTH + GMLP_WIDTH
IN_PROJ_WIDTH = 3 * ATTN_WIDTH + 2 * GMLP_WIDTH
MOBA_BLOCK = 256
MOBA_TOPK = 3
Q_CHUNK = 128
GMLP_CHUNK = 128
ROPE_THETA = 10000.0
FFN_HIDDEN = -(-(8 * D_MODEL) // (3 * 256)) * 256
DEEPNORM_ALPHA = (2 * DEPTH) ** 0.25
DEEPNORM_BETA = (8 * DEPTH) ** -0.25
LN_EPS = 1e-5
RMS_EPS = 1e-6
NEG_INF = -1e30


def layer_norm(x, g, b):
    xf = x.astype(jnp.float32)
    mu = jnp.mean(xf, axis=-1, keepdims=True)
    var = jnp.mean(jnp.square(xf - mu), axis=-1, keepdims=True)
    return ((xf - mu) * lax.rsqrt(var + LN_EPS) * g.astype(jnp.float32) + b.astype(jnp.float32)).astype(x.dtype)

def rms_norm_2(x, g):
    xf = x.astype(jnp.float32)
    ms = jnp.mean(jnp.square(xf), axis=-1, keepdims=True)
    return (xf * lax.rsqrt(ms + RMS_EPS) * g.astype(jnp.float32)).astype(x.dtype)

def rope(t, pos):
    inv_freq = ROPE_THETA ** (-jnp.arange(0, HEAD_DIM, 2, dtype=jnp.float32) / HEAD_DIM)
    ang = pos.astype(jnp.float32)[:, None] * inv_freq[None, :]
    ang = jnp.concatenate([ang, ang], axis=-1)
    cos = jnp.cos(ang).astype(t.dtype)
    sin = jnp.sin(ang).astype(t.dtype)
    t1, t2 = t[..., : HEAD_DIM // 2], t[..., HEAD_DIM // 2:]
    rot = jnp.concatenate([-t2, t1], axis=-1)
    return t * cos + rot * sin

def moba_attention(q, k, v):
    B, H, S, hd = q.shape
    nb = -(-S // MOBA_BLOCK)
    pad = nb * MOBA_BLOCK - S
    kb = jnp.pad(k, ((0, 0), (0, 0), (0, pad), (0, 0))).reshape(B, H, nb, MOBA_BLOCK, hd)
    vb = jnp.pad(v, ((0, 0), (0, 0), (0, pad), (0, 0))).reshape(B, H, nb, MOBA_BLOCK, hd)
    pos = jnp.arange(S, dtype=jnp.int32)
    own = pos // MOBA_BLOCK
    own_idx = jnp.broadcast_to(own[None, None, :, None], (B, H, S, 1)).astype(jnp.int32)
    n_sel = min(MOBA_TOPK, nb - 1)
    if n_sel > 0:
        k_mean = jnp.mean(kb.astype(jnp.float32), axis=3)
        gate = jnp.einsum('bhsd,bhnd->bhsn', q.astype(jnp.float32), k_mean)
        past = jnp.arange(nb, dtype=jnp.int32)[None, :] < own[:, None]
        gate = jnp.where(past[None, None], gate, NEG_INF)
        _, sel = lax.top_k(gate, n_sel)
        idx = jnp.concatenate([sel.astype(jnp.int32), own_idx], axis=-1)
    else:
        idx = own_idx
    nsb = idx.shape[-1]
    n_chunks = S // Q_CHUNK
    q_c = q.reshape(B, H, n_chunks, Q_CHUNK, hd).transpose(2, 0, 1, 3, 4)
    idx_c = idx.reshape(B, H, n_chunks, Q_CHUNK, nsb).transpose(2, 0, 1, 3, 4)
    pos_c = pos.reshape(n_chunks, Q_CHUNK)
    b_ix = jnp.arange(B)[:, None, None, None]
    h_ix = jnp.arange(H)[None, :, None, None]
    key_off = jnp.arange(MOBA_BLOCK, dtype=jnp.int32)
    slot_own = jnp.arange(nsb) == nsb - 1
    scale = HEAD_DIM ** -0.5

    def attend(args):
        qc, ic, pc = args
        kg = kb[b_ix, h_ix, ic]
        vg = vb[b_ix, h_ix, ic]
        s = jnp.einsum('bhqd,bhqnkd->bhqnk', qc, kg).astype(jnp.float32) * scale
        own_c = pc // MOBA_BLOCK
        valid_blk = slot_own | (ic < own_c[:, None])
        key_pos = ic[..., None] * MOBA_BLOCK + key_off
        mask = valid_blk[..., None] & (key_pos <= pc[:, None, None])
        s = jnp.where(mask, s, NEG_INF)
        p = jax.nn.softmax(s.reshape(B, H, Q_CHUNK, nsb * MOBA_BLOCK), axis=-1)
        p = p.reshape(B, H, Q_CHUNK, nsb, MOBA_BLOCK).astype(vg.dtype)
        return jnp.einsum('bhqnk,bhqnkd->bhqd', p, vg)

    out = lax.map(attend, (q_c, idx_c, pos_c))
    return out.transpose(1, 2, 0, 3, 4).reshape(B, H, S, hd)

def spatial_gating(u, z, ln_g, ln_b, w_s, b_s):
    B, S, G, dg = z.shape
    z = layer_norm(z, ln_g, ln_b)
    nc = S // GMLP_CHUNK
    zc = z.reshape(B, nc, GMLP_CHUNK, G, dg)
    tril = jnp.tril(jnp.ones((GMLP_CHUNK, GMLP_CHUNK), dtype=bool))
    w = jnp.where(tril[None], w_s, jnp.zeros_like(w_s))
    mixed = jnp.einsum('gij,bcjgd->bcigd', w, zc) + b_s.T[None, None, :, :, None]
    return u * mixed.reshape(B, S, G, dg)

def hybrid_mixer(x, w_in, attn_out_g, gmlp_out_g, gmlp_ln_g, gmlp_ln_b, w_spatial, b_spatial, w_out):
    B, S, _ = x.shape
    h = x @ w_in
    A, G = ATTN_WIDTH, GMLP_WIDTH
    q, k, v, u, z = jnp.split(h, [A, 2 * A, 3 * A, 3 * A + G], axis=-1)

    def heads(t):
        return t.reshape(B, S, N_ATTN_HEADS, HEAD_DIM).transpose(0, 2, 1, 3)

    pos = jnp.arange(S, dtype=jnp.int32)
    qh = rope(heads(q), pos)
    kh = rope(heads(k), pos)
    attn = moba_attention(qh, kh, heads(v)).transpose(0, 2, 1, 3).reshape(B, S, A)

    u = jax.nn.gelu(u, approximate=False).reshape(B, S, N_GMLP_GROUPS, HEAD_DIM)
    z = jax.nn.gelu(z, approximate=False).reshape(B, S, N_GMLP_GROUPS, HEAD_DIM)
    sg = spatial_gating(u, z, gmlp_ln_g, gmlp_ln_b, w_spatial, b_spatial).reshape(B, S, G)

    merged = jnp.concatenate([rms_norm_2(attn, attn_out_g), rms_norm_2(sg, gmlp_out_g)], axis=-1)
    return merged @ w_out

def swiglu_ffn(x, w_gate, w_up, w_down):
    return (jax.nn.silu(x @ w_gate) * (x @ w_up)) @ w_down

def second_inputs(seed: int = 0) -> dict:
    key = jax.random.key(seed)
    ks = jax.random.split(key, 16)
    nrm = jax.random.normal
    f32 = jnp.float32
    x = nrm(ks[0], (BATCH, SEQ, D_MODEL), f32)
    w_in = nrm(ks[1], (DEPTH, D_MODEL, IN_PROJ_WIDTH), f32) * D_MODEL ** -0.5
    attn_out_g = 1.0 + 0.1 * nrm(ks[2], (DEPTH, ATTN_WIDTH), f32)
    gmlp_out_g = 1.0 + 0.1 * nrm(ks[3], (DEPTH, GMLP_WIDTH), f32)
    gmlp_ln_g = 1.0 + 0.1 * nrm(ks[4], (DEPTH, N_GMLP_GROUPS, HEAD_DIM), f32)
    gmlp_ln_b = 0.02 * nrm(ks[5], (DEPTH, N_GMLP_GROUPS, HEAD_DIM), f32)
    w_spatial = nrm(ks[6], (DEPTH, N_GMLP_GROUPS, GMLP_CHUNK, GMLP_CHUNK), f32) * GMLP_CHUNK ** -0.5
    b_spatial = 1.0 + 0.1 * nrm(ks[7], (DEPTH, N_GMLP_GROUPS, GMLP_CHUNK), f32)
    w_out = nrm(ks[8], (DEPTH, MIX_WIDTH, D_MODEL), f32) * (MIX_WIDTH ** -0.5 * DEEPNORM_BETA)
    ln1_g = 1.0 + 0.1 * nrm(ks[9], (DEPTH, D_MODEL), f32)
    ln1_b = 0.02 * nrm(ks[10], (DEPTH, D_MODEL), f32)
    w_gate = nrm(ks[11], (DEPTH, D_MODEL, FFN_HIDDEN), f32) * D_MODEL ** -0.5
    w_up = nrm(ks[12], (DEPTH, D_MODEL, FFN_HIDDEN), f32) * D_MODEL ** -0.5
    w_down = nrm(ks[13], (DEPTH, FFN_HIDDEN, D_MODEL), f32) * (FFN_HIDDEN ** -0.5 * DEEPNORM_BETA)
    ln2_g = 1.0 + 0.1 * nrm(ks[14], (DEPTH, D_MODEL), f32)
    ln2_b = 0.02 * nrm(ks[15], (DEPTH, D_MODEL), f32)
    return {"x": x, "w_in": w_in, "attn_out_g": attn_out_g, "gmlp_out_g": gmlp_out_g,
            "gmlp_ln_g": gmlp_ln_g, "gmlp_ln_b": gmlp_ln_b, "w_spatial": w_spatial,
            "b_spatial": b_spatial, "w_out": w_out, "ln1_g": ln1_g, "ln1_b": ln1_b,
            "w_gate": w_gate, "w_up": w_up, "w_down": w_down, "ln2_g": ln2_g, "ln2_b": ln2_b}

def second_block(x, w_in, attn_out_g, gmlp_out_g, gmlp_ln_g, gmlp_ln_b, w_spatial, b_spatial,
              w_out, ln1_g, ln1_b, w_gate, w_up, w_down, ln2_g, ln2_b):
    for l in range(DEPTH):
        mix = hybrid_mixer(x, w_in[l], attn_out_g[l], gmlp_out_g[l], gmlp_ln_g[l], gmlp_ln_b[l],
                           w_spatial[l], b_spatial[l], w_out[l])
        x = layer_norm(DEEPNORM_ALPHA * x + mix, ln1_g[l], ln1_b[l])
        ffn = swiglu_ffn(x, w_gate[l], w_up[l], w_down[l])
        x = layer_norm(DEEPNORM_ALPHA * x + ffn, ln2_g[l], ln2_b[l])
    return x


def setup_inputs(seed=0):
    out = dict(first_inputs(seed))
    for name, value in second_inputs(seed + 1).items():
        if name != "x":
            out[name + "_2"] = value
    return out


def reference(
    x, norm1_g, w_in, rnn_conv_w, rnn_conv_b, rg_w_a, rg_b_a, rg_w_x, rg_b_x, lru_lambda,
    w_rnn_out, q_norm_g, k_cmp_norm_g, k_slc_norm_g, k_win_norm_g, cmp_pe_k, cmp_w1_k, cmp_w2_k,
    cmp_pe_v, cmp_w1_v, cmp_w2_v, w_attn_out, w_out, norm2_g, w_up, ffn_conv_w, ffn_conv_b,
    w_down, w_in_2, attn_out_g_2, gmlp_out_g_2, gmlp_ln_g_2, gmlp_ln_b_2, w_spatial_2,
    b_spatial_2, w_out_2, ln1_g_2, ln1_b_2, w_gate_2, w_up_2, w_down_2, ln2_g_2, ln2_b_2,
):
    x = first_block(
        x, norm1_g, w_in, rnn_conv_w, rnn_conv_b, rg_w_a, rg_b_a, rg_w_x, rg_b_x, lru_lambda,
        w_rnn_out, q_norm_g, k_cmp_norm_g, k_slc_norm_g, k_win_norm_g, cmp_pe_k, cmp_w1_k,
        cmp_w2_k, cmp_pe_v, cmp_w1_v, cmp_w2_v, w_attn_out, w_out, norm2_g, w_up, ffn_conv_w,
        ffn_conv_b, w_down,
    )
    return second_block(
        x, w_in_2, attn_out_g_2, gmlp_out_g_2, gmlp_ln_g_2, gmlp_ln_b_2, w_spatial_2,
        b_spatial_2, w_out_2, ln1_g_2, ln1_b_2, w_gate_2, w_up_2, w_down_2, ln2_g_2, ln2_b_2,
    )


_drawn_inputs = setup_inputs


def setup_inputs(seed=0):
    import zlib

    import numpy as np

    out = dict(_drawn_inputs(seed))
    spreads = {}
    factors = {'norm1_g': 5.643,
     'rg_b_a': 21.36,
     'rg_b_x': 8.0,
     'q_norm_g': 8.0,
     'k_cmp_norm_g': 127.148,
     'k_slc_norm_g': 8.0,
     'k_win_norm_g': 8.0,
     'cmp_pe_k': 8.0,
     'cmp_pe_v': 19.032,
     'norm2_g': 11.162,
     'ffn_conv_b': 10.908,
     'gmlp_ln_g_2': 200.0,
     'gmlp_ln_b_2': 200.0,
     'ln1_b_2': 2.772,
     'ln2_b_2': 2.9,
     'rnn_conv_b': 3.199,
     'attn_out_g_2': 64.0,
     'gmlp_out_g_2': 64.0,
     'b_spatial_2': 64.0}
    for name, (base, spread) in spreads.items():
        noise = np.random.default_rng([zlib.crc32(name.encode()), seed]).standard_normal(out[name].shape)
        drawn = base * np.exp(spread * noise) if base else spread * noise
        out[name] = jnp.asarray(drawn.astype(out[name].dtype))
    for name, factor in factors.items():
        out[name] = (out[name] * factor).astype(out[name].dtype)
    return out
```

```python
import concourse.bass as bass
from concourse import mybir
from contextlib import ExitStack

F32 = mybir.dt.float32
F32R = mybir.dt.float32r
ACT = mybir.ActivationFunctionType
ALU = mybir.AluOpType
AX = mybir.AxisListType.X

P = 128
TOK = 256
NT = TOK // P
DM = 1024
KD = DM // P
D_RNN = 1344
RP = 112
NR = D_RNN // RP
RB = D_RNN // 16
RG = 3
NG = NR // RG
HD = 64
NH = 16
NKV = 4
CMP_STRIDE = 16
NC = 15
CP = 16
EPS = 1e-6
LN_EPS = 1e-5
NEG = -1e30
N_UP = 3 * DM // P
N_UP2 = 2816 // P
ALPHA = 2 ** 0.25
AW = 512
CHUNK = 2048
NRAW = 2
NSPL = 3
ADJ = ((0, 1), (0, 1, 2), (1, 2))
ADJ_LIST = [(to, ti) for to in range(RG) for ti in ADJ[to]]


def chunk_list():
    out = [("kv", i, CHUNK, True) for i in range(4)]
    out += [("cmp", i, CHUNK, True) for i in range(2)]
    out += [("gate", 0, KD * 3 * NH, True)]
    out += [("q", i, CHUNK, True) for i in range(4)]
    out += [("w1", i, CHUNK, False) for i in range(2)]
    for g in range(NG):
        out += [("rnn", RG * g + t, 2 * KD * RP, True) for t in range(RG)]
        out += [("mg", 2 * g, CHUNK, True), ("ri", g, 2 * len(ADJ_LIST) * RP, False), ("mg", 2 * g + 1, CHUNK, True)]
    out += [("ao", i, CHUNK, True) for i in range(4)]
    out += [("ro", i, NR * P, True) for i in range(8)]
    out += [("wo", i, CHUNK, True) for i in range(4)]
    out += ffn_order("up", N_UP, "dn")
    out += [("in2", i, CHUNK, True) for i in range(10)]
    out += [("wo2", i, CHUNK, True) for i in (1, 3, 0, 2)]
    out += ffn_order("up2", N_UP2, "dn2")
    return out


def ffn_order(up, n, down, lag=5):
    out, d = [], 0
    for i in range(n):
        out.append((up, i, CHUNK, True))
        if i >= 2 * d + lag:
            out.append((down, d, CHUNK, True))
            d += 1
    out += [(down, j, CHUNK, True) for j in range(d, n // 2)]
    return out


CHUNKS = chunk_list()
NCH = len(CHUNKS)
AT = {(kind, i): c for c, (kind, i, _, _) in enumerate(CHUNKS)}
OFFS = [sum(P * w for _, _, w, _ in CHUNKS[:c]) for c in range(NCH + 1)]
W0 = AT[("rnn", 0)]
SPLIT_NO = [sum(1 for x in CHUNKS[:c] if x[3]) for c in range(NCH)]
SPLITS = [c for c in range(NCH) if CHUNKS[c][3]]

COLS = {}
_n = 0
for _name, _w in (("cw", 4 * NR), ("cb", NR), ("ba", NR), ("bx", NR), ("lam", NR), ("fw", 3 * 2 * N_UP),
                  ("fb", 2 * N_UP), ("gq", 1), ("gkc", 1), ("gks", 1), ("gkw", 1), ("bs", 8),
                  ("pek", 16), ("pev", 16), ("w2k", HD), ("w2v", HD)):
    COLS[_name] = (_n, _n + _w)
    _n += _w
NCOLS = _n
CONSTS = {}
_n = 0
for _name, _w in (("ident", P), ("mask", 2 * P), ("cadd", NT * CP), ("c01", NT * CP), ("m8", 8), ("ind2", 2),
                  ("cos", NT * HD), ("sin", NT * HD)):
    CONSTS[_name] = (_n, _n + _w)
    _n += _w
NCONST = _n
NU = 16
NU2 = 4


def n_tile1(u):
    return sum(1 for x in range(u + 1) if (x >> 1) & 1)


def psum_uses(kinds_by_reader):
    uses, counts, seen = [], [], {"act": 0, "dve": 0, "m": 0}
    for c, (kind, _, _, _) in enumerate(CHUNKS):
        if kind in kinds_by_reader:
            reader, n = kinds_by_reader[kind]
            for _ in range(n):
                seen[reader] += 1
                uses.append(reader)
                counts.append(seen[reader])
    return uses, counts


MB_READERS = {"cmp": ("act", 1), "q": ("act", 1), "rnn": ("dve", 1), "mg": ("act", 1), "ri": ("act", RG),
              "ao": ("dve", 1), "ro": ("m", 1)}
MB_USES, MB_COUNTS = psum_uses(MB_READERS)
T0_NO = {}
for _c, (_kind, _i, _, _) in enumerate(CHUNKS):
    if (_kind in ("kv", "wo", "in2") and _i % 2 or _kind == "wo2" and _i % 2 == 0
            or _kind == "dn" and _i == N_UP // 2 - 1 or _kind == "dn2" and _i == N_UP2 // 2 - 1):
        T0_NO[_c] = len(T0_NO)
MB_NO = {}
_n = 0
for _c, (_kind, _i, _, _) in enumerate(CHUNKS):
    if _kind in MB_READERS:
        MB_NO[_c] = _n
        _n += MB_READERS[_kind][1]


def two_block_program(nc, A_w, A_x, A_cols, A_consts, A_g1, A_g2, A_og, A_gln, A_ln1, A_ln2, A_ws, A_out):
    ctx = ExitStack()
    with ctx:
        base = -(-nc.sbuf_base // 64) * 64
        top = [base]

        def put(name, shape, dt=F32, at=None):
            size = 4
            for n in shape[1:]:
                size *= n
            off = top[0] if at is None else at
            if at is None:
                top[0] += -(-size // 32) * 32
            return nc.alloc_sbuf_tensor_at(name, list(shape), dt, offset=off)

        def sem(name):
            return ctx.enter_context(nc.semaphore(name))

        RAW = put("RAW", [P, NRAW, CHUNK])
        WH = put("WH", [P, NSPL, CHUNK], F32R)
        WL = put("WL", [P, NSPL, CHUNK], F32R)
        a_at = top[0]
        AH = put("AH", [P, NR, TOK], F32R)
        AL = put("AL", [P, NR, TOK], F32R)
        BH = put("BH", [P, KD, TOK], F32R)
        BL = put("BL", [P, KD, TOK], F32R)
        CH = put("CH", [P, KD, TOK], F32R)
        CL = put("CL", [P, KD, TOK], F32R)
        CV = put("CV", [P, NCOLS])
        CN = put("CN", [P, NCONST])
        st_at = top[0]
        top[0] += 2816
        pr = -(-top[0] // 64) * 64
        st = [st_at]

        def small(name, cols):
            off = st[0]
            st[0] += 4 * cols
            assert st[0] <= st_at + 2816
            return nc.alloc_sbuf_tensor_at(name, [P, cols], F32, offset=off, align_bytes=4)

        def col(name, j=0, n=1, parts=P):
            lo = COLS[name][0] + j
            return CV[0:parts, lo:lo + n]

        def const(name):
            return CN[:, CONSTS[name][0]:CONSTS[name][1]]

        ident = const("ident")

        half = small("half", 64)
        ssx = small("ssx", 2)
        rsx = small("rsx", 2)
        kss = small("kss", 16)
        krs = small("krs", 16)
        qss = small("qss", NT * NH)
        rq = small("rq", NT * NH)
        gts = small("gts", NT * 3 * NH)
        gk = small("gk", 3)
        hba = small("hba", NR)
        hbx = small("hbx", NR)
        c4 = small("c4", NR)
        l1 = small("l1", NR)
        l2 = small("l2", NR)
        l3 = small("l3", NR)
        cbk = small("cbk", 2)
        css = small("css", 1)
        crs = small("crs", 1)
        cmx = small("cmx", NT * NH)
        csm = small("csm", NT * NH)
        crw = small("crw", NT * NH)
        mx = small("mx", 8)
        nb = small("nb", 8)
        rs = small("rs", 8)
        ri_ = small("ri_", 8)
        wt = small("wt", 8)
        rs2 = small("rs2", 16)
        ri2 = small("ri2", 16)
        ss1 = small("ss1", 4)
        ss1s = small("ss1s", 2)
        rs1 = small("rs1", 2)
        pmean = small("pmean", 16)
        zss = small("zss", 16)
        zrs = small("zrs", 16)
        oss = small("oss", 4)
        ors = small("ors", 4)
        ysum = small("ysum", 8)
        ymean = small("ymean", 4)
        yss = small("yss", 4)
        yrs = small("yrs", 4)
        tmp = small("tmp", 80)

        XC = put("XC", [RP, 2, RG, TOK], at=pr)
        RGT = put("RGT", [RP, 2, RG, TOK], at=pr + 6144)
        TR = put("TR", [RP, RG, TOK], at=pr + 12288)
        TI = put("TI", [RP, RG, TOK], at=pr + 15360)
        AA = put("AA", [RP, RG, TOK], at=pr + 18432)
        QT = put("QT", [P, KD, TOK], at=pr + 21504)
        KT = put("KT", [P, 2, NKV, TOK], at=pr + 29696)
        V = put("V", [P, NT, 2, 256], at=pr + 37888)
        SM = put("SM", [P, 2, 4, TOK], at=pr + 41984)
        PT = put("PT", [P, 2, NT, 4, P], at=pr + 50176)
        MG = put("MG", [P, 16, TOK], at=pr + 58368)
        VB = put("VB", [P, 2, 8, HD], at=pr + 74752)
        PC = put("PC", [P, 2, TOK], at=pr + 78848)
        assert pr + 80896 <= nc.sbuf_usable_end
        X0 = put("X0", [P, NT, DM], at=pr + 58368)
        XN = put("XN", [P, NT, DM], at=pr + 66560)
        G1R = put("G1R", [P, DM], at=pr + 41984)
        KSQ = put("KSQ", [P, 2, 256], at=pr + 66560)
        KN = put("KN", [P, 2, NT, 4, 2, HD], at=pr + 50176)
        SK = put("SK", [P, 2, NKV, TOK], at=pr)
        QSQ = put("QSQ", [P, 2, TOK], at=pr + 12288)
        HK = put("HK", [P, 2, NKV, CP], at=pr + 18432)
        HVX = put("HVX", [P, NH, CP], at=pr + 18944)
        SC = put("SC", [P, NT, NH, CP], at=pr + 72704)
        KNC = put("KNC", [NKV * CP, 2, HD], at=pr + 70656)
        KCZ = put("KCZ", [P, NKV, 2, CP], at=pr + 71168)
        X1 = put("X1", [P, NT, DM], at=pr)
        XN2 = put("XN2", [P, NT, DM], at=pr + 21504)
        G2R = put("G2R", [P, DM], at=pr + 29696)
        JK = put("JK", [P, 4, 512], at=pr + 33792)
        CG = put("CG", [P, 4, 2, TOK], at=pr + 37888)
        RQK = put("RQK", [P, 2, NT, AW], at=pr + 8192)
        RT = put("RT", [P, 2, 2, AW], at=pr + 21504)
        QK2 = put("QK2", [P, 2, 4, TOK], at=pr + 29696)
        V2 = put("V2", [P, NT, AW], at=pr + 37888)
        U2 = put("U2", [P, NT, AW], at=pr + 41984)
        Z2 = put("Z2", [P, NT, AW], at=pr + 46080)
        SM2 = put("SM2", [P, 2, 4, TOK], at=pr + 50176)
        PT2 = put("PT2", [P, 2, NT, 4, P], at=pr + 58368)
        OGR = put("OGR", [P, 2 * AW], at=pr + 66560)
        GLN = put("GLN", [P, 2, AW], at=pr + 70656)
        MR = put("MR", [P, NT, DM], at=pr + 21504)
        LN1 = put("LN1", [P, 2, DM], at=a_at)
        WS = put("WS", [P, 8, P], at=a_at + 8192)
        ZT = put("ZT", [P, NT, AW], at=a_at + 12288)
        ZQ = put("ZQ", [P, NT, AW], at=a_at + 16384)
        X3 = put("X3", [P, NT, DM], at=pr + 8192)
        LN2 = put("LN2", [P, 2, DM], at=pr + 66560)
        SG = put("SG", [P, 4, TOK], at=pr + 37888)
        YJ = put("YJ", [P, NT, DM], at=pr + 50176)

        PS = ctx.enter_context(nc.psum_tensor("PS", [P, 8, 512], F32))

        raw_in = [sem(f"raw_in{i}") for i in range(NRAW)]
        x_in = [sem(f"x_in{t}") for t in range(NT)]
        w_hi, w_lo, chunk_done, tile0_done, ri_part, y_gain, x_again, vec_in, g1_in = (sem(n) for n in (
            "w_hi", "w_lo", "chunk_done", "tile0_done", "ri_part", "y_gain", "x_again", "vec_in", "g1_in"))
        g2_in, og_in, gln_in, ln1_in, ln2_in, ws_in, out_done, act_own, dve_own = (sem(n) for n in (
            "g2_in", "og_in", "gln_in", "ln1_in", "ln2_in", "ws_in", "out_done", "act_own", "dve_own"))
        pool_own, x_sq, x_rstd, xn_ready, xt_done, xt_hi, xt_lo, k_sq, k_ss = (sem(n) for n in (
            "pool_own", "x_sq", "x_rstd", "xn_ready", "xt_done", "xt_hi", "xt_lo", "k_sq", "k_ss"))
        k_rstd, kn_ready, kt_done, kt_copied, gk_ready, mb_act, mb_dve, gate_tanh = (sem(n) for n in (
            "k_rstd", "kn_ready", "kt_done", "kt_copied", "gk_ready", "mb_act", "mb_dve", "gate_tanh"))
        gate_ready, qss_done, qss_copied, rq_ready, lam_exp, lam_abs, c4_ready = (sem(n) for n in (
            "gate_ready", "qss_done", "qss_copied", "rq_ready", "lam_exp", "lam_abs", "c4_ready"))
        pe_part, cb_copied, hk_ready, hk_zero, hvx_ready, kc_done, kc_sq, kc_rstd = (sem(n) for n in (
            "pe_part", "cb_copied", "hk_ready", "hk_zero", "hvx_ready", "kc_done", "kc_sq", "kc_rstd"))
        knc_ready, kct_done, kcz_ready, vb_ready, sc_done, sc_sub, sc_exp, pc_ready = (sem(n) for n in (
            "knc_ready", "kct_done", "kcz_ready", "vb_ready", "sc_done", "sc_sub", "sc_exp", "pc_ready"))
        pct_done, pct_copied, qk_done, s_read, nb_ready, exp_done, p_ready, t_done = (sem(n) for n in (
            "pct_done", "pct_copied", "qk_done", "s_read", "nb_ready", "exp_done", "p_ready", "t_done"))
        pt0_copied, pt1_copied, pv_done, o_hi, o_lo, rnn_g, la_ready = (sem(n) for n in (
            "pt0_copied", "pt1_copied", "pv_done", "o_hi", "o_lo", "rnn_g", "la_ready"))
        ix_ready, sq_ready, w_ready, root_ready, scan_ready, g_hi, g_lo, m_ready = (sem(n) for n in (
            "ix_ready", "sq_ready", "w_ready", "root_ready", "scan_ready", "g_hi", "g_lo", "m_ready"))
        m_hi, m_lo, x1_ready, x1_sq, x1_ss, x1_rstd, xn2_ready, xt2_done, xt2_hi = (sem(n) for n in (
            "m_hi", "m_lo", "x1_ready", "x1_sq", "x1_ss", "x1_rstd", "xn2_ready", "xt2_done", "xt2_hi"))
        xt2_lo, up_taps, up_conv, up_gelu, up_prod, up_hi, up_lo, x2_ready, xt3_done = (sem(n) for n in (
            "xt2_lo", "up_taps", "up_conv", "up_gelu", "up_prod", "up_hi", "up_lo", "x2_ready", "xt3_done"))
        xt3_hi, xt3_lo, rope_parts, roped, v2_copied, u_ready, z_ready, qkt_done = (sem(n) for n in (
            "xt3_hi", "xt3_lo", "rope_parts", "roped", "v2_copied", "u_ready", "z_ready", "qkt_done"))
        qkt_copied, qk2_done, s2_read, nb2_ready, exp2_done, t2_done, pt20_copied = (sem(n) for n in (
            "qkt_copied", "qk2_done", "s2_read", "nb2_ready", "exp2_done", "t2_done", "pt20_copied"))
        pt21_copied, pv2_done, z_mean, z_sq, z_ss, z_rstd, zn_ready, ws_ready = (sem(n) for n in (
            "pt21_copied", "pv2_done", "z_mean", "z_sq", "z_ss", "z_rstd", "zn_ready", "ws_ready"))
        mix_done, os_ready, os_ss, os_rstd, mr_ready, mrt_done, mrt_hi, mrt_lo = (sem(n) for n in (
            "mix_done", "os_ready", "os_ss", "os_rstd", "mr_ready", "mrt_done", "mrt_hi", "mrt_lo"))
        y_mean, y_sq, y_rstd, y_ln, xt4_done, xt4_hi, xt4_lo, up2_silu, up2_prod = (sem(n) for n in (
            "y_mean", "y_sq", "y_rstd", "y_ln", "xt4_done", "xt4_hi", "xt4_lo", "up2_silu", "up2_prod"))
        up2_hi, up2_lo, z_gain = (sem(n) for n in (
            "up2_hi", "up2_lo", "z_gain"))

        def wait_tile(eng, c, t):
            if t == 0:
                eng.wait_ge(tile0_done, T0_NO[c] + 1)
            else:
                eng.wait_ge(chunk_done, c + 1)

        def wait_mb(eng, c, n=0):
            if CHUNKS[c][0] == "ri" and n < RG - 1:
                eng.wait_ge(ri_part, (RG - 1) * CHUNKS[c][1] + n + 1)
            else:
                eng.wait_ge(chunk_done, c + 1)
            return (MB_NO[c] + n) % 2

        def raw(c):
            return RAW[:, c % NRAW, 0:CHUNKS[c][2]]

        def slot(c):
            return SPLIT_NO[c] % NSPL

        def f32(ap):
            return ap.bitcast(F32)

        def s_view(bank, qt):
            nk = P * (qt + 1)
            return PS[:, bank:bank + 2, 0:2 * nk].rearrange("p b (r k) -> p b r k", r=2)

        def sm_view(buf, u, qt):
            return buf[:, u % 2, :, 0:P * (qt + 1)].rearrange("p (b r) k -> p b r k", b=2)

        def heads4(t, first):
            return t[:, first:first + 4].rearrange("p (r b) -> p b r", b=2)

        XT_BANKS = {0: (0, 1, 2, 3), 2: (6, 7, 0, 1), 3: (6, 7, 0, 1), "m": (6, 7, 6, 7), 4: (4, 5, 6, 7)}
        UP_BANKS = (0, 1, 6, 7)
        UP2_BANKS = (4, 5, 6, 7)
        IN2_BANKS = (2, 4, 6, 4, 6)

        block = ctx.enter_context(nc.Block())

        @block.sync
        def _(eng):
            for t in range(NT):
                eng.dma_start(X0[:, t, :], A_x[t * P:(t + 1) * P, :]).then_inc(x_in[t], 16)
            eng.dma_start(G1R[:, :], A_g1.partition_broadcast(P)).then_inc(g1_in, 16)
            eng.dma_start(CN[:, :], A_consts).then_inc(vec_in, 16)
            eng.dma_start(CV[:, :], A_cols).then_inc(vec_in, 16)
            for c in range(NCH):
                if c >= NRAW:
                    if CHUNKS[c - NRAW][3]:
                        eng.wait_ge(w_lo, SPLIT_NO[c - NRAW] + 1)
                    else:
                        eng.wait_ge(chunk_done, c - NRAW + 1)
                eng.dma_start(raw(c), A_w[OFFS[c]:OFFS[c + 1]].rearrange("(p n) -> p n", p=P))\
                   .then_inc(raw_in[c % NRAW], 16)
            for t in range(NT):
                eng.wait_ge(y_ln, NT + t + 1)
                eng.dma_start(A_out[t * P:(t + 1) * P, :], X3[:, t, :]).then_inc(out_done, 16)
            eng.wait_ge(out_done, 16 * NT)

        @block.gpsimd
        def _(eng):
            own = [0]

            def link(ins):
                own[0] += 1
                ins.then_inc(pool_own, 1)
                eng.wait_ge(pool_own, own[0])

            used = [0]

            def power(out, ss, n, mean_of, eps, ready):
                t = tmp[0:out.shape[0], used[0]:used[0] + n]
                used[0] += n
                link(eng.tensor_scalar(t, ss, 1.0 / mean_of, eps, ALU.mult, ALU.add))
                eng.tensor_tensor(out, t, half[0:out.shape[0], 0:n], ALU.pow).then_inc(ready, 1)

            link(eng.memset(half[:, :], -0.5))
            for t in range(NT):
                eng.wait_ge(x_sq, t + 1)
                power(rsx[:, t:t + 1], ssx[:, t:t + 1], 1, DM, EPS, x_rstd)
            for b in range(2):
                eng.wait_ge(k_ss, 2 * b + 2)
                power(krs[:, 8 * b:8 * b + 8], kss[:, 8 * b:8 * b + 8], 8, HD, EPS, k_rstd)
            eng.wait_ge(qss_copied, 1)
            power(rq[:, :], qss[:, :], NT * NH, 1.0, HD * EPS, rq_ready)
            eng.wait_ge(kc_sq, 1)
            power(crs[0:NKV * CP, :], css[0:NKV * CP, :], 1, HD, EPS, kc_rstd)
            eng.wait_ge(x1_ss, 1)
            power(rs1[:, :], ss1s[:, :], 2, DM, EPS, x1_rstd)
            for i in range(4):
                b, t = divmod(i, 2)
                eng.wait_ge(rope_parts, i + 1)
                eng.tensor_tensor(RQK[:, b, t, :], RT[:, i % 2, 0, :], RT[:, i % 2, 1, :], ALU.add).then_inc(roped, 1)
            eng.wait_ge(ws_in, 16)
            eng.affine_select(out=WS[:, :, :], in_=WS[:, :, :], compare_op=ALU.is_ge, fill=0.0, base=0,
                              pattern=[[0, 8], [1, P]], channel_multiplier=-1).then_inc(ws_ready, 1)
            eng.wait_ge(z_ss, 1)
            power(zrs[:, :], zss[:, :], 16, HD, LN_EPS, z_rstd)
            eng.wait_ge(os_ss, NT)
            power(ors[:, 2:4], oss[:, 2:4], 2, AW, EPS, os_rstd)
            eng.wait_ge(os_ss, 2 * NT)
            power(ors[:, 0:2], oss[:, 0:2], 2, AW, EPS, os_rstd)
            for n in range(2):
                for t in range(NT):
                    eng.wait_ge(y_sq, NT * n + t + 1)
                    j = NT * n + t
                    power(yrs[:, j:j + 1], yss[:, j:j + 1], 1, DM, LN_EPS, y_rstd)

        @block.scalar
        def _(eng):
            own = [0]

            def link(ins):
                own[0] += 1
                ins.then_inc(act_own, 1)
                eng.wait_ge(act_own, own[0])

            def split(c):
                if c >= NCH or not CHUNKS[c][3]:
                    return
                s = SPLIT_NO[c]
                eng.wait_ge(raw_in[c % NRAW], 16 * (c // NRAW + 1))
                if s >= NSPL:
                    eng.wait_ge(chunk_done, SPLITS[s - NSPL] + 1)
                eng.activation(WH[:, s % NSPL, 0:CHUNKS[c][2]], raw(c), ACT.Copy).then_inc(w_hi, 1)

            def evict_hi(H, banks, done, hi, kps=range(4), first=0):
                for n, kp in enumerate(kps):
                    eng.wait_ge(done, first + n + 1)
                    eng.activation(H[:, 2 * kp:2 * kp + 2, :].rearrange("p k t -> p (k t)"), PS[:, banks[kp], :],
                                   ACT.Copy).then_inc(hi, 1)

            def unit_exp(u):
                g, qt, br = u >> 2, (u >> 1) & 1, u & 1
                eng.wait_ge(nb_ready, u + 1)
                for i in range(4):
                    r = 2 * (i % 2) + i // 2
                    h = NH * qt + 4 * g + r
                    s = SM[:, u % 2, i, 0:P * (qt + 1)]
                    last = eng.activation(s, s, ACT.Exp, bias=nb[:, 4 * (u % 2) + i:4 * (u % 2) + i + 1],
                                          scale=rq[:, h:h + 1], accum_out=rs[:, 4 * (u % 2) + r:4 * (u % 2) + r + 1])
                last.then_inc(exp_done, 1)

            def unit_pt(u):
                eng.wait_ge(t_done, u + 1)
                if u >= 2:
                    eng.wait_ge(pv_done, u - 1)
                eng.activation(PT[:, u % 2, 0, :, :].rearrange("p h q -> p (h q)"), PS[:, 4, :], ACT.Copy)\
                   .then_inc(pt0_copied, 1)

            def o_first(v):
                g, qt = v >> 1, v & 1
                eng.wait_ge(pv_done, 2 * v + 2)
                eng.activation(CH[:, 2 * g:2 * g + 2, qt * P:(qt + 1) * P],
                               PS[:, 6 + v % 2, 0:256].rearrange("p (k q) -> p k q", k=2), ACT.Copy).then_inc(o_hi, 1)

            def window(w):
                if w == 0:
                    eng.wait_ge(kc_done, 1)
                    eng.activation(KSQ[0:NKV * CP, 0, 0:HD], PS[0:NKV * CP, 4, 0:HD], ACT.Square,
                                   accum_out=css[0:NKV * CP, :]).then_inc(kc_sq, 1)
                if w == 1:
                    eng.wait_ge(kct_done, 1)
                    eng.wait_ge(gk_ready, 1)
                    eng.wait_ge(hk_zero, 2)
                    for b in range(2):
                        last = eng.activation(KCZ[64 * b:64 * b + 64, :, b, :],
                                              PS[64 * b:64 * b + 64, 5, 0:NKV * CP].rearrange("p (g c) -> p g c", g=NKV),
                                              ACT.Copy, scale=gk[64 * b:64 * b + 64, 0:1])
                    last.then_inc(kcz_ready, 1)
                if w == 2:
                    eng.wait_ge(sc_sub, 1)
                    eng.activation(SC[:, :, :, :], SC[:, :, :, :], ACT.Exp).then_inc(sc_exp, 1)
                if w == 4:
                    eng.wait_ge(pct_done, 1)
                    eng.activation(PC[:, :, :].rearrange("p a q -> p (a q)"), PS[:, 6, :], ACT.Copy).then_inc(pct_copied, 1)
                if 0 <= w - 2 < NU:
                    unit_exp(w - 2)
                if 0 <= w - 4 < NU:
                    unit_pt(w - 4)
                if 0 <= w - 5 < NU and (w - 5) % 2:
                    o_first((w - 5) // 2)
                G, j = (w - 5) // 6, (w - 5) % 6
                if w >= 5 and G < NG:
                    if j == 0:
                        eng.wait_ge(la_ready, G + 1)
                        link(eng.activation(AA[:, :, :], TR[:, :, :], ACT.Exp))
                        eng.activation(TR[:, :, :], TR[:, :, :], ACT.Tanh)
                        eng.wait_ge(ix_ready, G + 1)
                        eng.activation(XC[:, G % 2, :, :], AA[:, :, :], ACT.Square).then_inc(sq_ready, 1)
                    if j == 1:
                        eng.wait_ge(w_ready, G + 1)
                        eng.activation(XC[:, G % 2, :, :], TR[:, :, :], ACT.Sqrt, scale=-0.25).then_inc(root_ready, 1)
                        eng.wait_ge(rnn_g, RG * (G + 1))
                        eng.activation(RGT[:, G % 2, :, :], RGT[:, G % 2, :, :], ACT.Gelu_apprx_tanh)\
                           .then_inc(root_ready, 1)
                    if j == 2:
                        eng.wait_ge(scan_ready, G + 1)
                        eng.activation(AH[0:RP, RG * G:RG * G + RG, :], XC[:, G % 2, :, :], ACT.Copy).then_inc(g_hi, 1)

            def unit2_exp(u):
                hg, qt = u >> 1, u & 1
                eng.wait_ge(nb2_ready, u + 1)
                for i in range(4):
                    h = 8 * qt + 4 * hg + 2 * (i % 2) + i // 2
                    s = SM2[:, u % 2, i, 0:P * (qt + 1)]
                    last = eng.activation(s, s, ACT.Exp, bias=nb[:, 4 * (u % 2) + i:4 * (u % 2) + i + 1],
                                          scale=HD ** -0.5, accum_out=rs2[:, h:h + 1])
                last.then_inc(exp2_done, 1)

            def unit2_pt(u):
                eng.wait_ge(t2_done, u + 1)
                if u >= 2:
                    eng.wait_ge(pv2_done, u - 1)
                eng.activation(PT2[:, u % 2, 0, :, :].rearrange("p h q -> p (h q)"), PS[:, 2, :], ACT.Copy)\
                   .then_inc(pt20_copied, 1)

            def side(c):
                kind, i, _, _ = CHUNKS[c]
                if kind == "kv":
                    if i % 2 == 0:
                        return
                    br = i // 2
                    for t in range(NT):
                        wait_tile(eng, c, t)
                        eng.activation(V[:, t, br, :], PS[:, 4 + 2 * br + t, 256:512], ACT.Copy)
                        if 2 * br + t >= 2:
                            eng.wait_ge(k_ss, 2 * br + t - 1)
                        eng.activation(KSQ[:, t, :], PS[:, 4 + 2 * br + t, 0:256], ACT.Square).then_inc(k_sq, 1)
                if kind == "cmp":
                    bank = wait_mb(eng, c)
                    for j in range(2):
                        for h in range(2):
                            src = PS[64 * h:64 * h + 64, bank, 256 * j:256 * j + 256]
                            eng.activation(SK[0:64, i, 2 * j + h, :], src, ACT.Copy)
                            last = eng.activation(SK[64:128, i, 2 * j + h, 0:TOK - 1], src[:, 1:TOK], ACT.Copy)
                    last.then_inc(mb_act, 1)
                    if i == 0:
                        eng.wait_ge(lam_abs, 1)
                        eng.activation(l2[0:RP, :], l1[0:RP, :], ACT.Exp, scale=-1.0).then_inc(lam_exp, 1)
                if kind == "gate":
                    eng.wait_ge(chunk_done, c + 1)
                    eng.activation(gts[:, :], PS[:, 4, 0:NT * 3 * NH], ACT.Tanh, scale=0.5).then_inc(gate_tanh, 1)
                if kind == "q":
                    bank = wait_mb(eng, c)
                    eng.activation(QT[:, 2 * i:2 * i + 2, :].rearrange("p k t -> p (k t)"), PS[:, bank, :], ACT.Copy)
                    if i:
                        eng.wait_ge(qss_done, i)
                    eng.activation(QSQ[:, :, :].rearrange("p k t -> p (k t)"), PS[:, bank, :], ACT.Square)\
                       .then_inc(mb_act, 1)
                if kind == "w1":
                    eng.wait_ge(pe_part, i + 1)
                    eng.activation(cbk[:, i:i + 1], PS[:, 2 + i, 64:65], ACT.Copy).then_inc(cb_copied, 1)
                    eng.wait_ge(cb_copied, i + 1)
                    eng.wait_ge(chunk_done, c + 1)
                    eng.wait_ge(hk_zero, 1)
                    eng.activation(HK[:, i, :, 0:NC], PS[:, 2 + i, 0:NKV * NC].rearrange("p (g c) -> p g c", g=NKV),
                                   ACT.Gelu_apprx_tanh, bias=cbk[:, i:i + 1]).then_inc(hk_ready, 1)
                if kind == "rnn":
                    bank = wait_mb(eng, c)
                    G, t = divmod(i, RG)
                    if G >= 2:
                        eng.wait_ge(g_lo, G - 1)
                    eng.activation(XC[:, G % 2, t, :], PS[0:RP, bank, 0:256], ACT.Identity,
                                   bias=col("cb", i, parts=RP), scale=col("cw", 3 * NR + i, parts=RP))
                    eng.activation(RGT[:, G % 2, t, :], PS[0:RP, bank, 256:512], ACT.Copy).then_inc(rnn_g, 1)
                if kind == "mg":
                    bank = wait_mb(eng, c)
                    eng.activation(MG[:, 2 * i:2 * i + 2, :].rearrange("p k t -> p (k t)"), PS[:, bank, :], ACT.Tanh,
                                   scale=0.5).then_inc(mb_act, 1)
                if kind == "ri":
                    if i >= 1:
                        eng.wait_ge(scan_ready, i)
                    for t in range(RG):
                        bank = wait_mb(eng, c, t)
                        n = RG * i + t
                        eng.activation(TR[:, t, :], PS[0:RP, bank, 0:256], ACT.Tanh, bias=hba[0:RP, n:n + 1], scale=0.5)
                        eng.activation(TI[:, t, :], PS[0:RP, bank, 256:512], ACT.Tanh, bias=hbx[0:RP, n:n + 1],
                                       scale=0.5).then_inc(mb_act, 1)
                if kind == "ro":
                    if i == 0:
                        eng.wait_ge(g_lo, NG)
                        eng.wait_ge(scan_ready, NG)
                        eng.dma_start(X1[:, :, :], A_x.rearrange("(t p) d -> p t d", p=P)).then_inc(x_again, 16)
                        eng.wait_ge(qk_done, NU)
                        eng.dma_start(G2R[:, :], A_g2.partition_broadcast(P)).then_inc(g2_in, 16)
                    eng.wait_ge(m_ready, i + 1)
                    eng.activation(BH[:, i, :], MG[:, i, :], ACT.Copy).then_inc(m_hi, 1)
                if kind == "wo" and i % 2:
                    for t in range(NT):
                        n = i // 2
                        eng.wait_ge(x1_ready, NT * n + t + 1)
                        eng.activation(JK[:, 2 * n + t, :], X1[:, t, 512 * n:512 * n + 512], ACT.Square,
                                       accum_out=ss1[:, 2 * t + n:2 * t + n + 1]).then_inc(x1_sq, 1)
                    if i == 3:
                        evict_hi(CH, XT_BANKS[2], xt2_done, xt2_hi)
                if kind == "up":
                    up_taps_of(i)
                    if i >= 1:
                        up_gelu_of(i - 1)
                    if i >= 2:
                        up_first(i - 2)
                    if i == N_UP - 1:
                        up_gelu_of(i)
                        up_first(i - 1)
                        up_first(i)
                if kind == "dn" and i == N_UP // 2 - 1:
                    for a, b, s in ((LN1, A_ln1, ln1_in), (OGR, A_og, og_in), (GLN, A_gln, gln_in)):
                        if a is LN1:
                            eng.wait_ge(chunk_done, c + 1)
                            eng.dma_start(WS[:, :, :], A_ws).then_inc(ws_in, 16)
                        flat = a[:, :] if a is OGR else a[:, :, :].rearrange("p a n -> p (a n)")
                        eng.dma_start(flat, b.partition_broadcast(P)).then_inc(s, 16)
                    evict_hi(BH, XT_BANKS[3], xt3_done, xt3_hi)
                if kind == "in2":
                    if i == 2:
                        eng.wait_ge(qkt_done, 1)
                        eng.activation(QK2[:, 0, :, :], PS[:, 0:2, :].rearrange("p b (j t) -> p (b j) t", j=2), ACT.Copy)\
                           .then_inc(qkt_copied, 1)
                    if i == 4:
                        eng.wait_ge(qkt_done, 2)
                        eng.activation(QK2[:, 1, :, :], PS[:, 2:4, :].rearrange("p b (j t) -> p (b j) t", j=2), ACT.Copy)\
                           .then_inc(qkt_copied, 1)
                    if i == 5:
                        for t in range(NT):
                            wait_tile(eng, c, t)
                            eng.activation(V2[:, t, :], PS[:, IN2_BANKS[2] + t, :], ACT.Copy).then_inc(v2_copied, 1)
                        unit2_exp(0)
                    if i == 6:
                        unit2_pt(0)
                        unit2_exp(1)
                    if i == 7:
                        for t in range(NT):
                            wait_tile(eng, c, t)
                            eng.activation(Z2[:, t, :], PS[:, IN2_BANKS[3] + t, :], ACT.Gelu).then_inc(z_ready, 1)
                        unit2_pt(1)
                        for t in range(NT):
                            eng.wait_ge(z_mean, t + 1)
                            eng.activation(ZQ[:, t, :], ZT[:, t, :], ACT.Square).then_inc(z_sq, 1)
                        unit2_exp(2)
                    if i == 8:
                        unit2_pt(2)
                        unit2_exp(3)
                    if i == 9:
                        for t in range(NT):
                            wait_tile(eng, c, t)
                            eng.activation(U2[:, t, :], PS[:, IN2_BANKS[4] + t, :], ACT.Gelu).then_inc(u_ready, 1)
                        unit2_pt(3)
                        for part in (1, 0):
                            for t in range(NT):
                                eng.wait_ge(os_ready, NT * (1 - part) + t + 1)
                                eng.activation(YJ[:, t, AW * part:AW * part + AW], MR[:, t, AW * part:AW * part + AW], ACT.Square,
                                               accum_out=oss[:, 2 * part + t:2 * part + t + 1]).then_inc(os_ss, 1)
                        evict_hi(CH, XT_BANKS["m"], mrt_done, mrt_hi, kps=(2, 3))
                if kind == "wo2" and i == 3:
                    evict_hi(CH, XT_BANKS["m"], mrt_done, mrt_hi, kps=(0, 1), first=2)
                if kind == "wo2" and i == 2:
                    norm_squares(0)
                    eng.wait_ge(os_rstd, 2)
                    eng.wait_ge(mr_ready, 4)
                    eng.dma_start(LN2[:, :, :].rearrange("p a n -> p (a n)"), A_ln2.partition_broadcast(P))\
                       .then_inc(ln2_in, 16)
                    evict_hi(BH, XT_BANKS[4], xt4_done, xt4_hi)
                if kind == "up2":
                    up2_silu_of(i)
                    if i >= 1:
                        up2_first(i - 1)
                    if i == N_UP2 - 1:
                        up2_first(i)
                if kind == "dn2" and i == N_UP2 // 2 - 1:
                    norm_squares(1)

            def norm_squares(n):
                for t in range(NT):
                    j = NT * n + t
                    eng.wait_ge(y_mean, j + 1)
                    eng.activation(YJ[:, t, :], (X1 if n == 0 else X3)[:, t, :], ACT.Square, bias=ymean[:, j:j + 1],
                                   accum_out=yss[:, j:j + 1]).then_inc(y_sq, 1)

            def up_taps_of(i):
                eng.wait_ge(chunk_done, AT["up", i] + 1)
                if i >= 4:
                    eng.wait_ge(up_lo, i - 3)
                for v in range(2):
                    f = N_UP * v + i
                    last = eng.activation(CG[:, i % 4, v, :], PS[:, UP_BANKS[i % 4], 256 * v:256 * v + 256], ACT.Identity,
                                          bias=col("fb", f), scale=col("fw", 2 * 2 * N_UP + f))
                last.then_inc(up_taps, 1)

            def up_gelu_of(i):
                eng.wait_ge(up_conv, i + 1)
                eng.activation(CG[:, i % 4, 0, :], CG[:, i % 4, 0, :], ACT.Gelu_apprx_tanh).then_inc(up_gelu, 1)

            def up_first(i):
                eng.wait_ge(up_prod, i + 1)
                if i >= NR:
                    eng.wait_ge(chunk_done, AT["dn", (i - NR) // 2] + 1)
                eng.activation(AH[:, i % NR, :], CG[:, i % 4, 0, :], ACT.Copy).then_inc(up_hi, 1)

            def up2_silu_of(i):
                eng.wait_ge(chunk_done, AT["up2", i] + 1)
                if i >= 4:
                    eng.wait_ge(up2_lo, i - 3)
                eng.activation(SG[:, i % 4, :], PS[:, UP2_BANKS[i % 4], 0:256], ACT.Silu).then_inc(up2_silu, 1)

            def up2_first(i):
                eng.wait_ge(up2_prod, i + 1)
                if i >= NR:
                    eng.wait_ge(chunk_done, AT["dn2", (i - NR) // 2] + 1)
                eng.activation(AH[:, i % NR, :], SG[:, i % 4, :], ACT.Copy).then_inc(up2_hi, 1)

            for t in range(NT):
                eng.wait_ge(x_in[t], 16)
                eng.activation(XN[:, t, :], X0[:, t, :], ACT.Square, accum_out=ssx[:, t:t + 1]).then_inc(x_sq, 1)
            split(0)
            evict_hi(BH, XT_BANKS[0], xt_done, xt_hi)
            split(1)
            for c in range(NCH):
                if CHUNKS[c][3]:
                    split(c + 2)
                    side(c)
                else:
                    side(c)
                    split(c + 2)
                if c >= W0:
                    window(c - W0)

        @block.vector
        def _(eng):
            own = [0]

            def link(ins):
                own[0] += 1
                ins.then_inc(dve_own, 1)
                eng.wait_ge(dve_own, own[0])

            def split(c):
                if c >= NCH or not CHUNKS[c][3]:
                    return
                s = SPLIT_NO[c]
                eng.wait_ge(w_hi, s + 1)
                eng.tensor_tensor(WL[:, s % NSPL, 0:CHUNKS[c][2]], raw(c), f32(WH[:, s % NSPL, 0:CHUNKS[c][2]]),
                                  ALU.subtract).then_inc(w_lo, 1)

            def evict_lo(H, L, banks, hi, lo, kps=range(4), first=0):
                for n, kp in enumerate(kps):
                    eng.wait_ge(hi, first + n + 1)
                    eng.tensor_tensor(L[:, 2 * kp:2 * kp + 2, :].rearrange("p k t -> p (k t)"), PS[:, banks[kp], :],
                                      f32(H[:, 2 * kp:2 * kp + 2, :].rearrange("p k t -> p (k t)")),
                                      ALU.subtract).then_inc(lo, 1)

            def unit_scores(u):
                g, qt, br = u >> 2, (u >> 1) & 1, u & 1
                eng.wait_ge(qk_done, u + 1)
                if u >= 2:
                    eng.wait_ge(t_done, u - 1)
                nk = P * (qt + 1)
                mask = const("mask")[:, 2 * P - nk:2 * P].unsqueeze(1).unsqueeze(1).broadcast_to([P, 2, 2, nk])
                eng.tensor_tensor(sm_view(SM, u, qt), s_view(2, qt), mask, ALU.add).then_inc(s_read, 1)
                eng.wait_ge(s_read, u + 1)
                m = mx[:, 4 * (u % 2):4 * (u % 2) + 4]
                link(eng.tensor_reduce(m, SM[:, u % 2, :, 0:nk], AX, ALU.max, negate=True))
                q = heads4(rq[:, NH * qt:NH * qt + NH], 4 * g)
                eng.tensor_tensor(nb[:, 4 * (u % 2):4 * (u % 2) + 4].rearrange("p (b r) -> p b r", b=2),
                                  m.rearrange("p (b r) -> p b r", b=2), q, ALU.mult).then_inc(nb_ready, 1)

            def unit_norm(u):
                g, qt, br = u >> 2, (u >> 1) & 1, u & 1
                eng.wait_ge(exp_done, u + 1)
                o = 4 * (u % 2)
                link(eng.reciprocal(ri_[:, o:o + 4], rs[:, o:o + 4]))
                gate = gts[:, 48 * qt + 12 * g + br + 1:48 * qt + 12 * g + br + 11:3]
                link(eng.tensor_tensor(wt[:, o:o + 4], ri_[:, o:o + 4], gate, ALU.mult))
                s = sm_view(SM, u, qt)
                w = heads4(wt, o).unsqueeze(3).broadcast_to([P, 2, 2, P * (qt + 1)])
                eng.tensor_tensor(s, s, w, ALU.mult).then_inc(p_ready, 1)

            def unit_pt(u):
                if (u >> 1) & 1:
                    eng.wait_ge(t_done, u + 1)
                    if u >= 2:
                        eng.wait_ge(pv_done, u - 1)
                    eng.tensor_copy(PT[:, u % 2, 1, :, :].rearrange("p h q -> p (h q)"), PS[:, 5, :])\
                       .then_inc(pt1_copied, 1)

            def o_second(v):
                g, qt = v >> 1, v & 1
                eng.wait_ge(o_hi, v + 1)
                eng.tensor_tensor(CL[:, 2 * g:2 * g + 2, qt * P:(qt + 1) * P],
                                  PS[:, 6 + v % 2, 0:256].rearrange("p (k q) -> p k q", k=2),
                                  f32(CH[:, 2 * g:2 * g + 2, qt * P:(qt + 1) * P]), ALU.subtract).then_inc(o_lo, 1)

            def window(w):
                if w == 0:
                    for T in range(2):
                        eng.wait_ge(kc_done, 3)
                        last = eng.tensor_tensor(
                            VB[:, T, :, :], PS[:, 7, 64 * T:64 * T + 64].unsqueeze(1).broadcast_to([P, 8, HD]),
                            const("m8").unsqueeze(2).broadcast_to([P, 8, HD]), ALU.mult)
                        last.then_inc(vb_ready, 1)
                    eng.wait_ge(kc_rstd, 1)
                    eng.tensor_tensor(KNC[:, :, :],
                                      PS[0:NKV * CP, 4, 0:HD].unsqueeze(1).broadcast_to([NKV * CP, 2, HD]),
                                      crs[0:NKV * CP, 0:1].unsqueeze(1).broadcast_to([NKV * CP, 2, HD]),
                                      ALU.mult).then_inc(knc_ready, 1)
                if w == 2:
                    eng.wait_ge(sc_done, 1)
                    eng.wait_ge(rq_ready, 1)
                    hs = [P, NH, CP]

                    def per_head(t, tt):
                        return t[:, NH * tt:NH * tt + NH].unsqueeze(2).broadcast_to(hs)

                    for tt in range(NT):
                        m = const("cadd")[:, CP * tt:CP * tt + CP].unsqueeze(1).broadcast_to(hs)
                        link(eng.tensor_tensor(SC[:, tt, :, :],
                                               PS[:, 5, 256 * tt:256 * tt + 256].rearrange("p (h c) -> p h c", h=NH),
                                               m, ALU.add))
                    link(eng.tensor_reduce(cmx[:, :], SC[:, :, :, :].rearrange("p a h c -> p (a h) c"), AX, ALU.max))
                    for tt in range(NT):
                        link(eng.tensor_tensor(SC[:, tt, :, :], SC[:, tt, :, :], per_head(cmx, tt), ALU.subtract))
                        ins = eng.tensor_tensor(SC[:, tt, :, :], SC[:, tt, :, :], per_head(rq, tt), ALU.mult)
                        if tt == 0:
                            link(ins)
                    ins.then_inc(sc_sub, 1)
                if w == 3:
                    eng.wait_ge(sc_exp, 1)
                    eng.wait_ge(gate_ready, 1)
                    link(eng.tensor_reduce(csm[:, :], SC[:, :, :, :].rearrange("p a h c -> p (a h) c"), AX, ALU.add))
                    link(eng.reciprocal(crw[:, :], csm[:, :]))
                    link(eng.tensor_tensor(crw[:, :], crw[:, :], gts[:, 0:NT * 3 * NH:3], ALU.mult))
                    hs = [P, NH, CP]
                    for tt in range(NT):
                        m = const("c01")[:, CP * tt:CP * tt + CP].unsqueeze(1).broadcast_to(hs)
                        link(eng.tensor_tensor(SC[:, tt, :, :], SC[:, tt, :, :], m, ALU.mult))
                        ins = eng.tensor_tensor(SC[:, tt, :, :], SC[:, tt, :, :],
                                                crw[:, NH * tt:NH * tt + NH].unsqueeze(2).broadcast_to(hs), ALU.mult)
                        if tt == 0:
                            link(ins)
                    ins.then_inc(pc_ready, 1)
                if 0 <= w - 2 < NU:
                    unit_scores(w - 2)
                if 0 <= w - 3 < NU:
                    unit_norm(w - 3)
                if 0 <= w - 4 < NU:
                    unit_pt(w - 4)
                if 0 <= w - 5 < NU and (w - 5) % 2:
                    o_second((w - 5) // 2)
                G, j = (w - 4) // 6, (w - 4) % 6
                if w >= 4 and G < NG:
                    x = XC[:, G % 2, :, :]
                    if j == 0:
                        eng.wait_ge(mb_act, MB_COUNTS[MB_NO[AT["ri", G]] + RG - 1])
                        if G == 0:
                            eng.wait_ge(c4_ready, 1)
                        eng.scalar_tensor_tensor(TR[:, :, :], TR[:, :, :], 1.0,
                                                 c4[0:RP, RG * G:RG * G + RG].unsqueeze(2).broadcast_to([RP, RG, TOK]),
                                                 ALU.add, ALU.mult).then_inc(la_ready, 1)
                        eng.scalar_tensor_tensor(TI[:, :, :], TI[:, :, :], 1.0, x, ALU.add, ALU.mult).then_inc(ix_ready, 1)
                    if j == 1:
                        eng.wait_ge(sq_ready, G + 1)
                        eng.scalar_tensor_tensor(TR[:, :, :], x, 1.0, TR[:, :, :], ALU.add, ALU.mult)\
                           .then_inc(w_ready, 1)
                        link(eng.memset(AA[:, :, 0:1], 0.0))
                    if j == 2:
                        eng.wait_ge(root_ready, 2 * G + 1)
                        link(eng.tensor_tensor(TI[:, :, :], x, TI[:, :, :], ALU.mult))
                        flat = [b.rearrange("p k t -> p (k t)") for b in (TR[:, :, :], AA[:, :, :], TI[:, :, :])]
                        link(eng.tensor_tensor_scan(flat[0], flat[1], flat[2], 0.0, ALU.mult, ALU.add))
                    if j == 3:
                        eng.wait_ge(root_ready, 2 * G + 2)
                        eng.tensor_tensor(x, TR[:, :, :], RGT[:, G % 2, :, :], ALU.mult).then_inc(scan_ready, 1)
                    if j == 4:
                        eng.wait_ge(g_hi, G + 1)
                        eng.tensor_tensor(AL[0:RP, RG * G:RG * G + RG, :], x, f32(AH[0:RP, RG * G:RG * G + RG, :]),
                                          ALU.subtract).then_inc(g_lo, 1)

            def side(c):
                kind, i, _, _ = CHUNKS[c]
                if kind == "kv" and i % 2:
                    br = i // 2
                    for t in range(NT):
                        eng.wait_ge(k_sq, 2 * br + t + 1)
                        o = 8 * br + 4 * t
                        eng.tensor_reduce(kss[:, o:o + 4], KSQ[:, t, :].rearrange("p (g d) -> p g d", g=4), AX, ALU.add)\
                           .then_inc(k_ss, 1)
                    eng.wait_ge(k_rstd, br + 1)
                    for t in range(NT):
                        o = 8 * br + 4 * t
                        src = PS[:, 4 + 2 * br + t, 0:256].rearrange("p (g d) -> p g d", g=4)
                        eng.tensor_tensor(KN[:, br, t, :, :, :], src.unsqueeze(2).broadcast_to([P, 4, 2, HD]),
                                          krs[:, o:o + 4].unsqueeze(2).unsqueeze(2).broadcast_to([P, 4, 2, HD]),
                                          ALU.mult).then_inc(kn_ready, 1)
                if kind == "kv" and i == 0:
                    eng.wait_ge(vec_in, 32)
                    for n, name in enumerate(("gkc", "gks", "gkw")):
                        last = eng.tensor_tensor(gk[:, n:n + 1], col(name), col("gq"), ALU.mult)
                    last.then_inc(gk_ready, 1)
                    eng.tensor_scalar(hba[:, :], col("ba", n=NR), 0.5, None, ALU.mult)
                    eng.tensor_scalar(hbx[:, :], col("bx", n=NR), 0.5, None, ALU.mult)
                    eng.scalar_tensor_tensor(l1[:, :], col("lam", n=NR), -1.0, col("lam", n=NR), ALU.mult, ALU.max)\
                       .then_inc(lam_abs, 1)
                if kind == "cmp" and i == 0:
                    eng.memset(HK[:, :, :, :], 0.0).then_inc(hk_zero, 1)
                    eng.memset(KCZ[:, :, :, :], 0.0).then_inc(hk_zero, 1)
                if kind == "cmp" and i == 1:
                    eng.wait_ge(lam_exp, 1)
                    z, s, p, q = (t[0:RP, :] for t in (l2, l1, l3, c4))
                    link(eng.tensor_scalar(s, z, 2.0, None, ALU.add))
                    link(eng.reciprocal(p, s))
                    link(eng.tensor_tensor(s, p, z, ALU.mult))
                    link(eng.tensor_tensor(z, s, s, ALU.mult))
                    link(eng.tensor_scalar(p, z, 1.0 / 17, None, ALU.mult))
                    for k in range(7, 0, -1):
                        link(eng.scalar_tensor_tensor(p, p, 1.0 / (2 * k + 1), z, ALU.add, ALU.mult))
                    link(eng.scalar_tensor_tensor(p, p, 1.0, s, ALU.add, ALU.mult))
                    link(eng.tensor_scalar(q, col("lam", n=NR, parts=RP), 4.0, 0.0, ALU.mult, ALU.min))
                    eng.scalar_tensor_tensor(q, p, -8.0, q, ALU.mult, ALU.add).then_inc(c4_ready, 1)
                if kind == "gate":
                    eng.wait_ge(gate_tanh, 1)
                    eng.tensor_scalar(gts[:, :], gts[:, :], 0.5, 0.5, ALU.mult, ALU.add).then_inc(gate_ready, 1)
                if kind == "cmp":
                    eng.wait_ge(kt_done, i + 1)
                    eng.wait_ge(gk_ready, 1)
                    bank = (2, 6)[i]
                    eng.tensor_scalar(KT[:, i, :, :], PS[:, bank:bank + 2, :].rearrange("p b (g t) -> p (b g) t", g=2),
                                      gk[:, 1 + i:2 + i], None, ALU.mult).then_inc(kt_copied, 1)
                if kind == "w1" and i == 0:
                    eng.wait_ge(qss_done, 4)
                    eng.tensor_copy(qss[:, :], PS[:, 5, 0:NT * NH]).then_inc(qss_copied, 1)
                if kind == "w1" and i == 1:
                    eng.wait_ge(hk_ready, 2)
                    for g in range(NKV):
                        last = eng.tensor_copy(HVX[:, 4 * g:4 * g + 4, :],
                                               HK[:, 1, g, :].unsqueeze(1).broadcast_to([P, 4, CP]))
                    last.then_inc(hvx_ready, 1)
                if kind == "rnn":
                    bank = wait_mb(eng, c)
                    G, t = divmod(i, RG)
                    eng.wait_ge(rnn_g, i + 1)
                    for s in range(1, 4):
                        o = XC[:, G % 2, t, s:TOK]
                        ins = eng.scalar_tensor_tensor(o, PS[0:RP, bank, 0:TOK - s],
                                                       col("cw", (3 - s) * NR + i, parts=RP), o, ALU.mult, ALU.add)
                        if s < 3:
                            link(ins)
                    ins.then_inc(mb_dve, 1)
                if kind == "ao":
                    bank = wait_mb(eng, c)
                    t = MG[:, 8 + 2 * i:10 + 2 * i, :].rearrange("p k t -> p (k t)")
                    eng.scalar_tensor_tensor(t, t, 1.0, PS[:, bank, :], ALU.add, ALU.mult).then_inc(mb_dve, 1)
                if kind == "ro":
                    bank = wait_mb(eng, c)
                    t = MG[:, i, :]
                    link(eng.scalar_tensor_tensor(t, t, 1.0, PS[:, bank, 0:256], ALU.add, ALU.mult))
                    eng.tensor_tensor(t, t, MG[:, 8 + i, :], ALU.add).then_inc(m_ready, 1)
                    if i >= 1:
                        m_second(i - 1)
                    if i == 7:
                        m_second(7)
                if kind == "wo" and i % 2:
                    n = i // 2
                    if n == 0:
                        eng.wait_ge(x_again, 16)
                    for t in range(NT):
                        wait_tile(eng, c, t)
                        o = X1[:, t, 512 * n:512 * n + 512]
                        eng.scalar_tensor_tensor(o, PS[:, 2 + 2 * n + t, :], 0.5, o, ALU.mult, ALU.add)\
                           .then_inc(x1_ready, 1)
                    if i == 3:
                        eng.wait_ge(x1_sq, 4)
                        eng.tensor_tensor(ss1s[:, :], ss1[:, 0:4:2], ss1[:, 1:4:2], ALU.add).then_inc(x1_ss, 1)
                        eng.wait_ge(x1_rstd, 1)
                        eng.wait_ge(g2_in, 16)
                        for t in range(NT):
                            eng.scalar_tensor_tensor(XN2[:, t, :], X1[:, t, :], rs1[:, t:t + 1], G2R[:, :], ALU.mult,
                                                     ALU.mult).then_inc(xn2_ready, 1)
                        evict_lo(CH, CL, XT_BANKS[2], xt2_hi, xt2_lo)
                if kind == "up":
                    up_taps_of(i)
                    if i >= 1:
                        up_product(i - 1)
                    if i >= 2:
                        up_second(i - 2)
                    if i == N_UP - 1:
                        up_product(i)
                        up_second(i - 1)
                        up_second(i)
                if kind == "dn" and i == N_UP // 2 - 1:
                    for t in range(NT):
                        wait_tile(eng, c, t)
                        for n in range(2):
                            o = X1[:, t, 512 * n:512 * n + 512]
                            ins = eng.tensor_tensor(o, PS[:, 2 + 2 * t + n, :], o, ALU.add)
                        ins.then_inc(x2_ready, 1)
                    evict_lo(BH, BL, XT_BANKS[3], xt3_hi, xt3_lo)
                if kind == "in2":
                    if i in (1, 3):
                        b = i // 2
                        for t in range(NT):
                            wait_tile(eng, c, t)
                            j = 2 * b + t
                            if j >= 2:
                                eng.wait_ge(roped, j - 1)
                            src = PS[:, IN2_BANKS[b] + t, :].rearrange("p (h d) -> p h d", h=8)
                            cos = const("cos")[:, HD * t:HD * t + HD].unsqueeze(1).broadcast_to([P, 8, HD])
                            sin = const("sin")[:, HD * t:HD * t + HD]
                            eng.tensor_tensor(RT[:, j % 2, 0, :].rearrange("p (h d) -> p h d", h=8), src, cos, ALU.mult)
                            o = RT[:, j % 2, 1, :].rearrange("p (h d) -> p h d", h=8)
                            hf = HD // 2
                            for a, z in ((0, hf), (hf, 0)):
                                ins = eng.tensor_tensor(o[:, :, a:a + hf], src[:, :, z:z + hf],
                                                        sin[:, a:a + hf].unsqueeze(1).broadcast_to([P, 8, hf]), ALU.mult)
                            ins.then_inc(rope_parts, 1)
                    if i == 5:
                        unit2_scores(0)
                    if i == 6:
                        unit2_scores(1)
                    if i == 7:
                        for t in range(NT):
                            eng.wait_ge(z_ready, t + 1)
                            z = Z2[:, t, :].rearrange("p (g d) -> p g d", g=8)
                            pm = pmean[:, 8 * t:8 * t + 8]
                            link(eng.tensor_reduce(pm, z, AX, ALU.add))
                            link(eng.tensor_scalar(pm, pm, 1.0 / HD, None, ALU.mult))
                            eng.tensor_tensor(ZT[:, t, :].rearrange("p (g d) -> p g d", g=8), z,
                                              pm.unsqueeze(2).broadcast_to([P, 8, HD]), ALU.subtract).then_inc(z_mean, 1)
                        unit2_pt(1)
                        unit2_scores(2)
                        for t in range(NT):
                            eng.wait_ge(z_sq, t + 1)
                            ins = eng.tensor_reduce(zss[:, 8 * t:8 * t + 8], ZQ[:, t, :].rearrange("p (g d) -> p g d", g=8),
                                                    AX, ALU.add)
                        ins.then_inc(z_ss, 1)
                        eng.wait_ge(gln_in, 16)
                        for t in range(NT):
                            eng.tensor_tensor(ZT[:, t, :], ZT[:, t, :], GLN[:, 0, :], ALU.mult).then_inc(z_gain, 1)
                    if i == 8:
                        unit2_scores(3)
                        eng.wait_ge(z_rstd, 1)
                        eng.wait_ge(z_gain, NT)
                        for t in range(NT):
                            z = ZT[:, t, :].rearrange("p (g d) -> p g d", g=8)
                            link(eng.tensor_tensor(z, z, zrs[:, 8 * t:8 * t + 8].unsqueeze(2).broadcast_to([P, 8, HD]),
                                                   ALU.mult))
                            eng.tensor_tensor(ZT[:, t, :], ZT[:, t, :], GLN[:, 1, :], ALU.add).then_inc(zn_ready, 1)
                    if i == 9:
                        unit2_pt(3)
                        eng.wait_ge(mix_done, 1)
                        eng.wait_ge(u_ready, NT)
                        for t in range(NT):
                            for g in range(8):
                                ins = eng.scalar_tensor_tensor(
                                    MR[:, t, AW + HD * g:AW + HD * g + HD],
                                    PS[:, 6 + g // 4, P * (g % 4) + HD * t:P * (g % 4) + HD * t + HD],
                                    col("bs", g), U2[:, t, HD * g:HD * g + HD], ALU.add, ALU.mult)
                            ins.then_inc(os_ready, 1)
                        for t in range(NT):
                            eng.wait_ge(exp2_done, NU2)
                            eng.wait_ge(pv2_done, NU2)
                            if t == 0:
                                link(eng.reciprocal(ri2[:, :], rs2[:, :]))
                            eng.tensor_tensor(MR[:, t, 0:AW].rearrange("p (h d) -> p h d", h=8),
                                              PS[:, 4 + t, :].rearrange("p (h d) -> p h d", h=8),
                                              ri2[:, 8 * t:8 * t + 8].unsqueeze(2).broadcast_to([P, 8, HD]),
                                              ALU.mult).then_inc(os_ready, 1)
                        eng.wait_ge(og_in, 16)
                        for part in (1, 0):
                            eng.wait_ge(os_rstd, 2 - part)
                            for t in range(NT):
                                eng.wait_ge(os_ready, NT * (2 - part))
                                m = MR[:, t, AW * part:AW * part + AW]
                                eng.scalar_tensor_tensor(m, m, ors[:, 2 * part + t:2 * part + t + 1],
                                                         OGR[:, AW * part:AW * part + AW], ALU.mult, ALU.mult)\
                                   .then_inc(mr_ready, 1)
                        evict_lo(CH, CL, XT_BANKS["m"], mrt_hi, mrt_lo, kps=(2, 3))
                if kind == "wo2" and i == 3:
                    evict_lo(CH, CL, XT_BANKS["m"], mrt_hi, mrt_lo, kps=(0, 1), first=2)
                if kind == "wo2" and i == 2:
                    layer_norm(0)
                    evict_lo(BH, BL, XT_BANKS[4], xt4_hi, xt4_lo)
                if kind == "up2":
                    up2_product(i)
                    if i >= 1:
                        up2_second(i - 1)
                    if i == N_UP2 - 1:
                        up2_second(i)
                if kind == "dn2" and i == N_UP2 // 2 - 1:
                    layer_norm(1)

            def m_second(i):
                eng.wait_ge(m_hi, i + 1)
                eng.tensor_tensor(BL[:, i, :], MG[:, i, :], f32(BH[:, i, :]), ALU.subtract).then_inc(m_lo, 1)

            def up_taps_of(i):
                eng.wait_ge(up_taps, i + 1)
                for s in (1, 2):
                    for v in range(2):
                        f = N_UP * v + i
                        o = CG[:, i % 4, v, s:TOK]
                        ins = eng.scalar_tensor_tensor(o, PS[:, UP_BANKS[i % 4], 256 * v:256 * v + TOK - s],
                                                       col("fw", (2 - s) * 2 * N_UP + f), o, ALU.mult, ALU.add)
                        if s == 1:
                            link(ins)
                ins.then_inc(up_conv, 1)

            def up_product(i):
                eng.wait_ge(up_gelu, i + 1)
                eng.tensor_tensor(CG[:, i % 4, 0, :], CG[:, i % 4, 0, :], CG[:, i % 4, 1, :], ALU.mult)\
                   .then_inc(up_prod, 1)

            def up_second(i):
                eng.wait_ge(up_hi, i + 1)
                eng.tensor_tensor(AL[:, i % NR, :], CG[:, i % 4, 0, :], f32(AH[:, i % NR, :]), ALU.subtract)\
                   .then_inc(up_lo, 1)

            def up2_product(i):
                eng.wait_ge(up2_silu, i + 1)
                eng.tensor_tensor(SG[:, i % 4, :], PS[:, UP2_BANKS[i % 4], 256:512], SG[:, i % 4, :], ALU.mult)\
                   .then_inc(up2_prod, 1)

            def up2_second(i):
                eng.wait_ge(up2_hi, i + 1)
                eng.tensor_tensor(AL[:, i % NR, :], SG[:, i % 4, :], f32(AH[:, i % NR, :]), ALU.subtract)\
                   .then_inc(up2_lo, 1)

            def unit2_scores(u):
                hg, qt = u >> 1, u & 1
                eng.wait_ge(qk2_done, u + 1)
                if u >= 2:
                    eng.wait_ge(t2_done, u - 1)
                nk = P * (qt + 1)
                mask = const("mask")[:, 2 * P - nk:2 * P].unsqueeze(1).unsqueeze(1).broadcast_to([P, 2, 2, nk])
                eng.tensor_tensor(sm_view(SM2, u, qt), s_view(0, qt), mask, ALU.add).then_inc(s2_read, 1)
                eng.wait_ge(s2_read, u + 1)
                m = mx[:, 4 * (u % 2):4 * (u % 2) + 4]
                link(eng.tensor_reduce(m, SM2[:, u % 2, :, 0:nk], AX, ALU.max, negate=True))
                eng.tensor_scalar(nb[:, 4 * (u % 2):4 * (u % 2) + 4], m, HD ** -0.5, None, ALU.mult)\
                   .then_inc(nb2_ready, 1)

            def unit2_pt(u):
                if u & 1:
                    eng.wait_ge(t2_done, u + 1)
                    if u >= 2:
                        eng.wait_ge(pv2_done, u - 1)
                    eng.tensor_copy(PT2[:, u % 2, 1, :, :].rearrange("p h q -> p (h q)"), PS[:, 3, :])\
                       .then_inc(pt21_copied, 1)

            def layer_norm(n):
                y, gained = (X1, X3) if n == 0 else (X3, X1)
                gains, gains_in = ((LN1, ln1_in), (LN2, ln2_in))[n]

                def gain(t):
                    j = NT * n + t
                    eng.wait_ge(y_mean, j + 1)
                    eng.scalar_tensor_tensor(gained[:, t, :], y[:, t, :], ymean[:, j:j + 1], gains[:, 0, :],
                                             ALU.add, ALU.mult).then_inc(y_gain, 1)

                def finish(t):
                    j = NT * n + t
                    eng.wait_ge(y_rstd, j + 1)
                    eng.wait_ge(y_gain, j + 1)
                    eng.scalar_tensor_tensor(X3[:, t, :], gained[:, t, :], yrs[:, j:j + 1], gains[:, 1, :],
                                             ALU.mult, ALU.add).then_inc(y_ln, 1)

                for t in range(NT):
                    j = NT * n + t
                    for h in range(2):
                        wait_tile(eng, AT["wo2", 2 * h] if n == 0 else NCH - 1, t)
                        o = y[:, t, 512 * h:512 * h + 512]
                        k = 4 * n + 2 * t + h
                        link(eng.scalar_tensor_tensor(o, o, ALPHA, PS[:, 2 * t + h, :], ALU.mult, ALU.add,
                                                      accum_out=ysum[:, k:k + 1]))
                    m = ymean[:, j:j + 1]
                    k = 4 * n + 2 * t
                    link(eng.tensor_tensor(m, ysum[:, k:k + 1], ysum[:, k + 1:k + 2], ALU.add))
                    eng.tensor_scalar(m, m, -1.0 / DM, None, ALU.mult).then_inc(y_mean, 1)
                    if t == 0:
                        eng.wait_ge(gains_in, 16)
                        gain(0)
                finish(0)
                gain(1)
                finish(1)

            eng.wait_ge(g1_in, 16)
            for t in range(NT):
                eng.wait_ge(x_rstd, t + 1)
                eng.scalar_tensor_tensor(XN[:, t, :], X0[:, t, :], rsx[:, t:t + 1], G1R[:, :], ALU.mult, ALU.mult)\
                   .then_inc(xn_ready, 1)
            split(0)
            evict_lo(BH, BL, XT_BANKS[0], xt_hi, xt_lo)
            split(1)
            for c in range(NCH):
                if CHUNKS[c][3]:
                    split(c + 2)
                    side(c)
                else:
                    side(c)
                    split(c + 2)
                if c >= W0:
                    window(c - W0)

        @block.tensor
        def _(eng):
            def transposes(src, banks, ready, done, kps=range(4), first=0):
                for t in range(NT):
                    eng.wait_ge(ready, first + t + 1)
                    for kp in kps:
                        for kk in range(2):
                            k = 2 * kp + kk
                            o = PS[:, banks[kp], 256 * kk + P * t:256 * kk + P * t + P]
                            last = eng.transpose(o, src[:, t, P * k:P * k + P], ident)
                        if t == NT - 1:
                            last.then_inc(done, 1)

            def f_tile(out, c, col0, m, H, L, nk=KD, parts=P, lo_ready=None):
                s = slot(c)
                for k in range(nk):
                    if lo_ready is not None and k % 2 == 0:
                        eng.wait_ge(lo_ready, k // 2 + 1)
                    lo_, hi_ = col0 + k * m, col0 + k * m + m
                    wh, wl = WH[0:parts, s, lo_:hi_], WL[0:parts, s, lo_:hi_]
                    eng.matmul(out, wh, H[0:parts, k, :], start=(k == 0), stop=False)
                    eng.matmul(out, wh, L[0:parts, k, :], start=False, stop=False)
                    last = eng.matmul(out, wl, H[0:parts, k, :], start=False, stop=(k == nk - 1))
                return last

            def t_part(out, c, cols, ks, H, L, t, start, stop):
                s = slot(c)
                for n, (k, lo_) in enumerate(ks):
                    wh, wl = WH[:, s, lo_:lo_ + cols], WL[:, s, lo_:lo_ + cols]
                    h, l = H[:, k, P * t:P * t + P], L[:, k, P * t:P * t + P]
                    eng.matmul(out, h, wh, start=(start and n == 0), stop=False)
                    eng.matmul(out, h, wl, start=False, stop=False)
                    last = eng.matmul(out, l, wh, start=False, stop=(stop and n == len(ks) - 1))
                return last

            def t_half(c, banks, i, H, L, first_half=0):
                for t in range(NT):
                    last = t_part(PS[:, banks[t], :], c, 512, [(4 * (i % 2) + k, 512 * k) for k in range(4)], H, L, t,
                                  i % 2 == first_half, i % 2 != first_half)
                    if i % 2 != first_half and t == 0:
                        last.then_inc(tile0_done, 1)
                return last

            def mb_bank(m):
                if m >= 2:
                    reader, n = MB_USES[m - 2], MB_COUNTS[m - 2]
                    eng.wait_ge({"act": mb_act, "dve": mb_dve, "m": m_ready}[reader], n)
                return m % 2

            def unit_qk(u):
                g, qt, br = u >> 2, (u >> 1) & 1, u & 1
                if u >= 1:
                    eng.wait_ge(s_read, u)
                nk = P * (qt + 1)
                for r in range(4):
                    h = 4 * g + r
                    o = 64 * (h % 2)
                    out = PS[:, 2 + r % 2, nk * (r // 2):nk * (r // 2) + nk]
                    last = eng.matmul(out, QT[o:o + 64, h // 2, P * qt:P * qt + P], KT[o:o + 64, br, g, 0:nk],
                                      start=True, stop=True)
                last.then_inc(qk_done, 1)

            def unit_t(u):
                qt = (u >> 1) & 1
                eng.wait_ge(p_ready, u + 1)
                if u >= 1:
                    eng.wait_ge(pt0_copied, u)
                    if n_tile1(u - 1):
                        eng.wait_ge(pt1_copied, n_tile1(u - 1))
                for kt in range(qt + 1):
                    for i in range(4):
                        last = eng.transpose(PS[:, 4 + kt, P * i:P * i + P], SM[:, u % 2, i, P * kt:P * kt + P], ident)
                last.then_inc(t_done, 1)

            def unit_pv(u):
                g, qt, br = u >> 2, (u >> 1) & 1, u & 1
                v = u >> 1
                bank = 6 + v % 2
                if br == 0:
                    if v == 0:
                        eng.wait_ge(pct_copied, 1)
                        eng.wait_ge(vb_ready, 2)
                    if v >= 2:
                        eng.wait_ge(o_lo, v - 1)
                    for pp in range(2):
                        j = 2 * (g % 2) + pp
                        eng.matmul(PS[:, bank, P * pp:P * pp + P],
                                   VB[:, g // 2, 2 * j:2 * j + 2, :].rearrange("p h d -> p (h d)"),
                                   PC[:, g // 2, P * qt:P * qt + P], start=(pp == 0), stop=False, skip_group_check=True)
                eng.wait_ge(pt0_copied, u + 1)
                if qt:
                    eng.wait_ge(pt1_copied, n_tile1(u))
                for kt in range(qt + 1):
                    for b in range(2):
                        last = eng.matmul(PS[64 * b:64 * b + 64, bank, 0:256], V[:, kt, br, HD * g:HD * g + HD],
                                          PT[:, u % 2, kt, 2 * b:2 * b + 2, :].rearrange("p r q -> p (r q)"),
                                          start=False, stop=(br == 1 and kt == qt), skip_group_check=True)
                last.then_inc(pv_done, 1)

            def window(w):
                if w == 0:
                    eng.wait_ge(hk_ready, 2)
                    eng.wait_ge(hk_zero, 1)
                    eng.wait_ge(gate_tanh, 1)
                    eng.matmul(PS[0:NKV * CP, 4, 0:HD], HK[:, 0, :, :].rearrange("p g c -> p (g c)"), col("w2k", n=HD),
                               start=True, stop=True).then_inc(kc_done, 1)
                    eng.wait_ge(hvx_ready, 1)
                    eng.wait_ge(kt_copied, 2)
                    for T in range(2):
                        eng.matmul(PS[:, 7, 64 * T:64 * T + 64], HVX[:, 8 * T:8 * T + 8, :].rearrange("p h c -> p (h c)"),
                                   col("w2v", n=HD), start=True, stop=True).then_inc(kc_done, 1)
                if w == 1:
                    eng.wait_ge(knc_ready, 1)
                    eng.wait_ge(qss_copied, 1)
                    eng.transpose(PS[:, 5, 0:NKV * CP], KNC[:, :, :].rearrange("p a d -> p (a d)"),
                                  ident[0:NKV * CP, 0:NKV * CP]).then_inc(kct_done, 1)
                if w == 2:
                    eng.wait_ge(kcz_ready, 1)
                    for tt in range(NT):
                        for j in range(KD):
                            last = eng.matmul(PS[:, 5, 256 * tt + 32 * j:256 * tt + 32 * j + 32],
                                              QT[:, j, P * tt:P * tt + P],
                                              KCZ[:, j // 2, :, :].rearrange("p a c -> p (a c)"), start=True, stop=True)
                    last.then_inc(sc_done, 1)
                if 0 <= w - 2 < NU:
                    unit_qk(w - 2)
                if w == 4:
                    eng.wait_ge(pc_ready, 1)
                    for T in range(2):
                        for tt in range(NT):
                            last = eng.transpose(PS[:, 6, 256 * T + P * tt:256 * T + P * tt + P],
                                                 SC[:, tt, 8 * T:8 * T + 8, :].rearrange("p h c -> p (h c)"), ident)
                    last.then_inc(pct_done, 1)
                if 0 <= w - 4 < NU:
                    unit_t(w - 4)
                if 0 <= w - 5 < NU:
                    unit_pv(w - 5)

            def unit2_qk(u):
                hg, qt = u >> 1, u & 1
                if u == 0:
                    eng.wait_ge(qkt_copied, 2)
                else:
                    eng.wait_ge(s2_read, u)
                nk = P * (qt + 1)
                for r in range(4):
                    h = 4 * hg + r
                    o = 64 * (h % 2)
                    out = PS[:, r % 2, nk * (r // 2):nk * (r // 2) + nk]
                    last = eng.matmul(out, QK2[o:o + 64, 0, h // 2, P * qt:P * qt + P], QK2[o:o + 64, 1, h // 2, 0:nk],
                                      start=True, stop=True)
                last.then_inc(qk2_done, 1)

            def unit2_t(u):
                qt = u & 1
                eng.wait_ge(exp2_done, u + 1)
                if u >= 1:
                    eng.wait_ge(pt20_copied, u)
                if u // 2:
                    eng.wait_ge(pt21_copied, u // 2)
                for kt in range(qt + 1):
                    for i in range(4):
                        last = eng.transpose(PS[:, 2 + kt, P * i:P * i + P], SM2[:, u % 2, i, P * kt:P * kt + P], ident)
                last.then_inc(t2_done, 1)

            def unit2_pv(u):
                hg, qt = u >> 1, u & 1
                eng.wait_ge(pt20_copied, u + 1)
                if qt:
                    eng.wait_ge(pt21_copied, u // 2 + 1)
                if u == 0:
                    eng.wait_ge(z_ready, NT)
                    eng.wait_ge(v2_copied, NT)
                for i in range(4):
                    h = 4 * hg + 2 * (i % 2) + i // 2
                    for kt in range(qt + 1):
                        last = eng.matmul(PS[:, 4 + qt, HD * h:HD * h + HD], PT2[:, u % 2, kt, i, :],
                                          V2[:, kt, HD * h:HD * h + HD], start=(kt == 0), stop=(kt == qt))
                last.then_inc(pv2_done, 1)

            def transpose_heads(b, bank):
                for j in range(4):
                    for t in range(NT):
                        eng.wait_ge(roped, NT * b + t + 1)
                        last = eng.transpose(PS[:, bank + j // 2, 256 * (j % 2) + P * t:256 * (j % 2) + P * t + P],
                                             RQK[:, b, t, P * j:P * j + P], ident)
                last.then_inc(qkt_done, 1)

            def main(c):
                kind, i, _, is_split = CHUNKS[c]
                if is_split:
                    eng.wait_ge(w_lo, SPLIT_NO[c] + 1)
                else:
                    eng.wait_ge(raw_in[c % NRAW], 16 * (c // NRAW + 1))
                if kind == "kv":
                    eng.wait_ge(xt_lo, (2, 4)[i > 0])
                    b = 4 + 2 * (i // 2)
                    last = t_half(c, (b, b + 1), i, BH, BL)
                if kind == "cmp":
                    m = MB_NO[c]
                    bank = mb_bank(m)
                    for j in range(2):
                        last = f_tile(PS[:, bank, 256 * j:256 * j + 256], c, 1024 * j, P, BH, BL)
                if kind == "gate":
                    eng.wait_ge(kn_ready, 2)
                    eng.wait_ge(k_sq, 2)
                    for t in range(NT):
                        last = t_part(PS[:, 4, 48 * t:48 * t + 48], c, 48, [(k, 48 * k) for k in range(KD)], BH, BL, t,
                                      True, True)
                if kind == "q":
                    bank = mb_bank(MB_NO[c])
                    for j in range(2):
                        last = f_tile(PS[:, bank, 256 * j:256 * j + 256], c, 1024 * j, P, BH, BL)
                if kind == "w1":
                    if i == 0:
                        eng.wait_ge(kt_copied, 1)
                        eng.wait_ge(mb_act, 2)
                        eng.wait_ge(vec_in, 32)
                    w = raw(c).rearrange("p (l n) -> p l n", l=16)
                    for l in range(16):
                        ins = eng.matmul(PS[:, 2 + i, 64:65], w[:, l, :], col(("pek", "pev")[i], l),
                                         start=(l == 0), stop=(l == 15))
                    ins.then_inc(pe_part, 1)
                    eng.wait_ge(cb_copied, i + 1)
                    for l in range(16):
                        last = eng.matmul(PS[:, 2 + i, 0:NKV * NC], w[:, l, :],
                                         SK[:, i, :, 2 * l:2 * l + CMP_STRIDE * (NC - 1) + 1:CMP_STRIDE],
                                         start=(l == 0), stop=(l == 15))
                if kind == "rnn":
                    bank = mb_bank(MB_NO[c])
                    for j in range(2):
                        last = f_tile(PS[0:RP, bank, 256 * j:256 * j + 256], c, KD * RP * j, RP, BH, BL)
                if kind == "mg":
                    bank = mb_bank(MB_NO[c])
                    for j in range(2):
                        last = f_tile(PS[:, bank, 256 * j:256 * j + 256], c, 1024 * j, P, BH, BL)
                if kind == "ri":
                    eng.wait_ge(mb_dve, RG * (i + 1))
                    for t in range(RG):
                        bank = mb_bank(MB_NO[c] + t)
                        for which in range(2):
                            for n, ti in enumerate(ADJ[t]):
                                e = len(ADJ_LIST) * which + ADJ_LIST.index((t, ti))
                                last = eng.matmul(PS[0:RP, bank, 256 * which:256 * which + 256],
                                                  raw(c)[0:RP, RP * e:RP * e + RP], XC[:, i % 2, ti, :],
                                                  start=(n == 0), stop=(n == len(ADJ[t]) - 1))
                        if t < RG - 1:
                            last.then_inc(ri_part, 1)
                if kind == "ao":
                    if i == 0:
                        eng.wait_ge(o_lo, 8)
                    bank = mb_bank(MB_NO[c])
                    for j in range(2):
                        last = f_tile(PS[:, bank, 256 * j:256 * j + 256], c, 1024 * j, P, CH, CL)
                if kind == "ro":
                    if i == 0:
                        eng.wait_ge(g_lo, NG)
                    bank = mb_bank(MB_NO[c])
                    last = f_tile(PS[:, bank, 0:256], c, 0, P, AH, AL, nk=NR, parts=RP)
                if kind == "wo":
                    if i % 2 == 0:
                        eng.wait_ge(m_lo, 4)
                    else:
                        eng.wait_ge(m_lo, 8)
                    b = 2 + 2 * (i // 2)
                    last = t_half(c, (b, b + 1), i, BH, BL)
                if kind == "up":
                    if i == 0:
                        eng.wait_ge(xt2_lo, 4)
                    if i >= 4:
                        eng.wait_ge(up_conv, i - 3)
                    for v in range(2):
                        last = f_tile(PS[:, UP_BANKS[i % 4], 256 * v:256 * v + 256], c, 1024 * v, P, CH, CL)
                if kind in ("dn", "dn2"):
                    first_bank, lo_s, n_all = (2, up_lo, N_UP // 2) if kind == "dn" else (0, up2_lo, N_UP2 // 2)
                    eng.wait_ge(lo_s, 2 * i + 2)
                    for t in range(NT):
                        for n in range(2):
                            last = t_part(PS[:, first_bank + 2 * t + n, :], c, 512,
                                          [((2 * i + k) % NR, 1024 * k + 512 * n) for k in range(2)], AH, AL, t,
                                          i == 0, i == n_all - 1)
                        if i == n_all - 1 and t == 0:
                            last.then_inc(tile0_done, 1)
                if kind == "in2":
                    b = i // 2
                    eng.wait_ge(xt3_lo, (2, 4)[i > 0])
                    if i == 0:
                        eng.wait_ge(x2_ready, NT)
                    if i == 6:
                        eng.wait_ge(rope_parts, 4)
                    if i == 8:
                        eng.wait_ge(v2_copied, NT)
                    last = t_half(c, (IN2_BANKS[b], IN2_BANKS[b] + 1), i, BH, BL)
                if kind == "wo2":
                    if i == 1:
                        eng.wait_ge(mrt_lo, 2)
                        eng.wait_ge(pt21_copied, NU2 // 2)
                    if i == 0:
                        eng.wait_ge(mrt_lo, 4)
                    last = t_half(c, (i // 2, 2 + i // 2), i, CH, CL, first_half=1)
                if kind == "up2":
                    if i == 0:
                        eng.wait_ge(xt4_lo, 4)
                    if i >= 4:
                        eng.wait_ge(up2_prod, i - 3)
                    for v in range(2):
                        last = f_tile(PS[:, UP2_BANKS[i % 4], 256 * v:256 * v + 256], c, 1024 * v, P, BH, BL)

                last.then_inc(chunk_done, 1)

            def q_sums(i):
                eng.wait_ge(mb_act, MB_COUNTS[MB_NO[AT["q", i]]])
                for j in range(2):
                    for tt in range(NT):
                        h = 2 * (2 * i + j)
                        last = eng.matmul(PS[:, 5, NH * tt + h:NH * tt + h + 2], QSQ[:, j, P * tt:P * tt + P],
                                          const("ind2"), start=True, stop=True)
                last.then_inc(qss_done, 1)

            def after(c):
                kind, i, _, _ = CHUNKS[c]
                if kind == "cmp":
                    eng.wait_ge(kn_ready, 2 * i + 2)
                    for g in range(NKV):
                        for t in range(NT):
                            o = 256 * (g % 2) + P * t
                            last = eng.transpose(PS[:, (2, 6)[i] + g // 2, o:o + P],
                                                 KN[:, i, t, g, :, :].rearrange("p a d -> p (a d)"), ident)
                    last.then_inc(kt_done, 1)
                if kind == "q" and i:
                    q_sums(i - 1)
                if kind == "wo" and i == 3:
                    transposes(XN2, XT_BANKS[2], xn2_ready, xt2_done)
                if kind == "dn" and i == N_UP // 2 - 1:
                    transposes(X1, XT_BANKS[3], x2_ready, xt3_done)
                if kind == "in2":
                    if i == 2:
                        transpose_heads(0, 0)
                    if i == 4:
                        eng.wait_ge(rope_parts, 2)
                        transpose_heads(1, 2)
                    if i == 5:
                        unit2_qk(0)
                    if i == 6:
                        unit2_t(0)
                        unit2_qk(1)
                    if i == 7:
                        unit2_t(1)
                        unit2_qk(2)
                    if i == 8:
                        unit2_pv(0)
                        unit2_t(2)
                        unit2_qk(3)
                        unit2_pv(1)
                    if i == 9:
                        unit2_t(3)
                        unit2_pv(2)
                        eng.wait_ge(zn_ready, NT)
                        eng.wait_ge(ws_ready, 1)
                        eng.wait_ge(u_ready, NT)
                        for g in range(8):
                            last = eng.matmul(PS[:, 6 + g // 4, P * (g % 4):P * (g % 4) + P], WS[:, g, :],
                                              ZT[:, :, HD * g:HD * g + HD], start=True, stop=True)
                        last.then_inc(mix_done, 1)
                        unit2_pv(3)
                        transposes(MR, XT_BANKS["m"], mr_ready, mrt_done, kps=(2, 3))
                if kind == "wo2" and i == 3:
                    transposes(MR, XT_BANKS["m"], mr_ready, mrt_done, kps=(0, 1), first=NT)
                if kind == "wo2" and i == 2:
                    transposes(X3, XT_BANKS[4], y_ln, xt4_done)

            eng.wait_ge(vec_in, 32)
            transposes(XN, XT_BANKS[0], xn_ready, xt_done)
            for c in range(NCH):
                if CHUNKS[c][0] == "w1" and CHUNKS[c][1] == 0:
                    q_sums(3)
                main(c)
                after(c)
                if c >= W0:
                    window(c - W0)


def _f(w):
    return w.reshape(-1, P, w.shape[1]).transpose(1, 0, 2)


def kernel(**inputs):
    import numpy as np
    import concourse.bacc as bacc
    from concourse.bass_utils import run_bass_kernel_spmd as run

    a = {k: np.asarray(v) for k, v in inputs.items()}
    w_in = a["w_in"]
    kvw = NKV * HD
    sizes = [D_RNN, D_RNN, DM] + [kvw] * 6 + [3 * NH, DM, DM]
    offs = np.concatenate([[0], np.cumsum(sizes)])
    (rx, rgate, q, kc, vc, ks, vs, kw, vw, gates, mg_rnn, mg_attn) = (
        w_in[:, offs[n]:offs[n + 1]] for n in range(len(sizes)))
    mgs = np.concatenate([mg_rnn, mg_attn], 1)
    rows = []

    def f_pair(w0, w1):
        return np.concatenate([_f(w0).reshape(P, -1), _f(w1).reshape(P, -1)], 1)

    def t_half(w, i):
        n, kh = divmod(i, 2)
        return _f(w[512 * kh:512 * kh + 512, 512 * n:512 * n + 512]).reshape(P, -1)

    def tile(w, m, width=P):
        return w[:, width * m:width * m + width]

    def gates_blocks(g):
        out = np.zeros((P, 2, len(ADJ_LIST), RP), np.float32)
        span = RG * RP
        for which, w in enumerate((a["rg_w_a"], a["rg_w_x"])):
            dense = np.zeros((span, span), np.float32)
            for b in range(span // RB):
                dense[RB * b:RB * b + RB, RB * b:RB * b + RB] = w[g * (span // RB) + b]
            for e, (to, ti) in enumerate(ADJ_LIST):
                out[0:RP, which, e] = dense[RP * ti:RP * ti + RP, RP * to:RP * to + RP]
        return out.reshape(P, -1)

    for kind, i, width, _ in CHUNKS:
        if kind == "kv":
            r = t_half(np.concatenate([ks, vs, kw, vw], 1), i)
        elif kind == "cmp":
            w = (kc, vc)[i]
            r = f_pair(tile(w, 0), tile(w, 1))
        elif kind == "gate":
            r = _f(gates).reshape(P, -1)
        elif kind == "q":
            r = f_pair(tile(q, 2 * i), tile(q, 2 * i + 1))
        elif kind == "w1":
            r = _f(a[("cmp_w1_k", "cmp_w1_v")[i]]).reshape(P, -1)
        elif kind == "rnn":
            r = f_pair(tile(rx, i, RP), tile(rgate, i, RP))
        elif kind == "mg":
            r = f_pair(tile(mgs, 2 * i), tile(mgs, 2 * i + 1))
        elif kind == "ri":
            r = gates_blocks(i)
        elif kind == "ao":
            r = f_pair(tile(a["w_attn_out"], 2 * i), tile(a["w_attn_out"], 2 * i + 1))
        elif kind == "ro":
            r = np.zeros((P, NR, P), np.float32)
            r[0:RP] = tile(a["w_rnn_out"], i).reshape(NR, RP, P).transpose(1, 0, 2)
            r = r.reshape(P, -1)
        elif kind == "wo":
            r = t_half(a["w_out"], i)
        elif kind == "up":
            r = f_pair(tile(a["w_up"], i), tile(a["w_up"], N_UP + i))
        elif kind == "dn":
            r = _f(a["w_down"][256 * i:256 * i + 256]).reshape(P, -1)
        elif kind == "in2":
            r = t_half(a["w_in_2"][0], (i, i + 2 if i < 8 else i - 2)[i >= 6])
        elif kind == "wo2":
            r = t_half(a["w_out_2"][0], i)
        elif kind == "up2":
            r = f_pair(tile(a["w_gate_2"][0], i), tile(a["w_up_2"][0], i))
        elif kind == "dn2":
            r = _f(a["w_down_2"][0][256 * i:256 * i + 256]).reshape(P, -1)
        assert r.shape == (P, width), (kind, r.shape)
        rows.append(np.ascontiguousarray(r).reshape(-1))
    stream = np.concatenate(rows)

    cols = np.zeros((P, NCOLS), np.float32)

    def place(name, block):
        cols[0:block.shape[0], COLS[name][0]:COLS[name][0] + block.shape[1]] = block

    place("cw", a["rnn_conv_w"].reshape(4 * NR, RP).T)
    for name, key in (("cb", "rnn_conv_b"), ("ba", "rg_b_a"), ("bx", "rg_b_x"), ("lam", "lru_lambda")):
        place(name, a[key].reshape(NR, RP).T)
    place("fw", a["ffn_conv_w"].reshape(3 * 2 * N_UP, P).T)
    place("fb", a["ffn_conv_b"].reshape(2 * N_UP, P).T)
    for name, key in (("gq", "q_norm_g"), ("gkc", "k_cmp_norm_g"), ("gks", "k_slc_norm_g"), ("gkw", "k_win_norm_g")):
        place(name, np.concatenate([a[key], a[key]])[:, None])
    place("bs", a["b_spatial_2"][0].T)
    place("pek", a["cmp_pe_k"].reshape(16, P).T)
    place("pev", a["cmp_pe_v"].reshape(16, P).T)
    place("w2k", a["cmp_w2_k"])
    place("w2v", a["cmp_w2_v"])

    consts = np.zeros((P, NCONST), np.float32)

    def fixed(name, block):
        consts[:, CONSTS[name][0]:CONSTS[name][1]] = block

    pos = np.arange(TOK)
    fixed("ident", np.eye(P))
    fixed("mask", np.concatenate([np.zeros((P, P)), np.where(pos[None, :P] <= pos[:P, None], 0.0, NEG)], 1))
    ends = np.arange(CP) * CMP_STRIDE + 31
    seen = (ends[None, :] <= pos[:, None]) & (np.arange(CP) < NC)[None, :]
    seen = seen.reshape(NT, P, CP).transpose(1, 0, 2).reshape(P, -1)
    fixed("cadd", np.where(seen, 0.0, NEG))
    fixed("c01", seen.astype(np.float32))
    fixed("m8", (np.arange(P)[:, None] // CP == np.arange(8)[None, :]))
    fixed("ind2", (np.arange(P)[:, None] // HD == np.arange(2)[None, :]))
    inv = (np.float32(10000.0) ** (-np.arange(0, HD, 2, dtype=np.float32) / np.float32(HD))).astype(np.float32)
    ang = pos.astype(np.float32)[:, None] * inv[None, :]
    cos, sin = np.cos(ang).astype(np.float32), np.sin(ang).astype(np.float32)
    for name, t in (("cos", np.concatenate([cos, cos], 1)), ("sin", np.concatenate([-sin, sin], 1))):
        fixed(name, t.reshape(NT, P, HD).transpose(1, 0, 2).reshape(P, -1))

    def row(*keys):
        return np.concatenate([a[k].reshape(-1) for k in keys])

    arrays = {
        "w_stream": stream,
        "x": np.ascontiguousarray(a["x"].reshape(TOK, DM)),
        "cols": cols,
        "consts": consts,
        "g1": row("norm1_g"),
        "g2": row("norm2_g"),
        "og": row("attn_out_g_2", "gmlp_out_g_2"),
        "gln": row("gmlp_ln_g_2", "gmlp_ln_b_2"),
        "ln1": row("ln1_g_2", "ln1_b_2"),
        "ln2": row("ln2_g_2", "ln2_b_2"),
        "ws": np.ascontiguousarray(a["w_spatial_2"][0].transpose(2, 0, 1)),
    }
    nc = bacc.Bacc("TRN2", target_bir_lowering=False, num_devices=1)
    aps = [nc.dram_tensor("in_" + k, v.shape, F32, kind="ExternalInput").ap() for k, v in arrays.items()]
    out = nc.dram_tensor("out_y", (TOK, DM), F32, kind="ExternalOutput").ap()
    two_block_program(nc, *aps, out)
    r = run(nc, [{"in_" + k: v for k, v in arrays.items()}], core_ids=[0])
    return r.results[0]["out_y"].reshape(1, TOK, DM)
```

```python
import concourse.bass as bass
from concourse import mybir
from contextlib import ExitStack

F32 = mybir.dt.float32
F32R = mybir.dt.float32r
ACT = mybir.ActivationFunctionType
ALU = mybir.AluOpType
AX = mybir.AxisListType.X

P = 128
TOK = 256
NT = TOK // P
DM = 1024
KD = DM // P
D_RNN = 1344
RP = 112
NR = D_RNN // RP
RB = D_RNN // 16
RG = 3
NG = NR // RG
HD = 64
NH = 16
NKV = 4
CMP_STRIDE = 16
NC = 15
CP = 16
NGC = NKV * CP - 1
EPS = 1e-6
LN_EPS = 1e-5
NEG = -1e30
N_UP = 3 * DM // P
N_UP2 = 2816 // P
ALPHA = 2 ** 0.25
AW = 512
CHUNK = 2048
NRAW = 2
NSLOT = 3
ADJ = ((0, 1), (0, 1, 2), (1, 2))
ADJ_LIST = [(to, ti) for to in range(RG) for ti in ADJ[to]]


def chunk_list():
    out = [("kv", i, CHUNK, True) for i in range(4)]
    out += [("cmp", i, CHUNK, True) for i in range(2)]
    out += [("gate", 0, KD * 3 * NH, True)]
    out += [("q", i, CHUNK, True) for i in range(4)]
    out += [("w1", i, CHUNK, False) for i in range(2)]
    for g in range(NG):
        out += [("rnn", RG * g + t, 2 * KD * RP, True) for t in range(RG)]
        out += [("mg", 2 * g, CHUNK, True), ("ri", g, 2 * len(ADJ_LIST) * RP, False), ("mg", 2 * g + 1, CHUNK, True)]
    out += [("ao", i, CHUNK, True) for i in range(4)]
    out += [("ro", i, NR * P, True) for i in range(8)]
    out += [("wo", i, CHUNK, True) for i in range(4)]
    out += ffn_order("up", N_UP, "dn")
    out += [("in2", i, CHUNK, True) for i in range(10)]
    out += [("wo2", i, CHUNK, True) for i in (1, 3, 0, 2)]
    out += ffn_order("up2", N_UP2, "dn2")
    return out


def ffn_order(up, n, down, lag=5):
    out, d = [], 0
    for i in range(n):
        out.append((up, i, CHUNK, True))
        if i >= 2 * d + lag:
            out.append((down, d, CHUNK, True))
            d += 1
    out += [(down, j, CHUNK, True) for j in range(d, n // 2)]
    return out


CHUNKS = chunk_list()
NCH = len(CHUNKS)
AT = {(kind, i): c for c, (kind, i, _, _) in enumerate(CHUNKS)}
OFFS = [sum(P * w for _, _, w, _ in CHUNKS[:c]) for c in range(NCH + 1)]
W0 = AT[("rnn", 0)]
SPLIT_NO = [sum(1 for x in CHUNKS[:c] if x[3]) for c in range(NCH)]
PLAIN = [c for c in range(NCH) if not CHUNKS[c][3]]
LOAD_ORDER = sorted(range(NCH), key=lambda c: c + (0 if CHUNKS[c][3] else 1.5))



def arrival_slots():
    last, uses, out = [None] * (NRAW + 2), [0] * (NRAW + 2), {}
    for c, (kind, _, _, is_split) in enumerate(CHUNKS):
        if not is_split:
            continue
        slots = list(range(NRAW)) + [NRAW] * (kind in ("up", "dn")) + [NRAW + 1] * (kind in ("up2", "dn2"))
        slot = min(slots, key=lambda n: -1 if last[n] is None else last[n])
        out[c] = (slot, last[slot], uses[slot])
        last[slot] = SPLIT_NO[c]
        uses[slot] += 1
    return out


ARRIVAL = arrival_slots()

COLS = {}
_n = 0
for _name, _w in (("cw", 4 * NR), ("cb", NR), ("ba", NR), ("bx", NR), ("lam", NR), ("fw", 3 * 2 * N_UP),
                  ("fb", 2 * N_UP), ("gq", 1), ("gkc", 1), ("gks", 1), ("gkw", 1), ("bs", 8),
                  ("pek", 16), ("pev", 16), ("w2k", HD), ("w2v", HD)):
    COLS[_name] = (_n, _n + _w)
    _n += _w
NCOLS = _n
CONSTS = {}
_n = 0
for _name, _w in (("ident", P), ("mask", P), ("cadd", NT * CP), ("c01", NT * CP), ("m8", 8), ("ind2", 2),
                  ("cos", NT * HD), ("sin", NT * HD)):
    CONSTS[_name] = (_n, _n + _w)
    _n += _w
NCONST = _n
RG_LOG_A, RG_A, RG_SQUARES, RG_ROOTS, RG_SCAN, RG_SPLIT = 4, 5, 6, 7, 8, 9
SUMS_FIRST = (("wo", 3), ("dn", N_UP // 2 - 1), ("in2", 9), ("wo2", 2))
NU = 16
NU2 = 4


def n_tile1(u):
    return sum(1 for x in range(u + 1) if (x >> 1) & 1)


def rg_group(w, step):
    g, r = divmod(w - step, 2 * RG)
    return g if r == 0 and 0 <= g < NG else None


def psum_uses(kinds_by_reader):
    uses, counts, seen = [], [], {"act": 0, "dve": 0, "m": 0}
    for c, (kind, _, _, _) in enumerate(CHUNKS):
        if kind in kinds_by_reader:
            reader, n = kinds_by_reader[kind]
            for _ in range(n):
                seen[reader] += 1
                uses.append(reader)
                counts.append(seen[reader])
    return uses, counts


MB_READERS = {"cmp": ("act", 1), "q": ("act", 1), "rnn": ("dve", 1), "mg": ("act", 1), "ri": ("act", RG),
              "ao": ("dve", 1), "ro": ("m", 1)}
MB_USES, MB_COUNTS = psum_uses(MB_READERS)
T0_NO = {}
for _c, (_kind, _i, _, _) in enumerate(CHUNKS):
    if (_kind in ("kv", "wo", "in2") and _i % 2 or _kind == "wo2" and _i % 2 == 0
            or _kind == "dn" and _i == N_UP // 2 - 1 or _kind == "dn2" and _i == N_UP2 // 2 - 1):
        T0_NO[_c] = len(T0_NO)
MB_NO = {}
_n = 0
for _c, (_kind, _i, _, _) in enumerate(CHUNKS):
    if _kind in MB_READERS:
        MB_NO[_c] = _n
        _n += MB_READERS[_kind][1]


def two_block_program(nc, A_w, A_x, A_cols, A_consts, A_g1, A_g2, A_og, A_gln, A_ln1, A_ln2, A_ws, A_out):
    ctx = ExitStack()
    with ctx:
        base = -(-nc.sbuf_base // 64) * 64
        top = [base]

        def put(name, shape, dt=F32, at=None):
            size = 4
            for n in shape[1:]:
                size *= n
            off = top[0] if at is None else at
            if at is None:
                top[0] += -(-size // 32) * 32
            return nc.alloc_sbuf_tensor_at(name, list(shape), dt, offset=off)

        def sem(name):
            return ctx.enter_context(nc.semaphore(name))

        RAW = put("RAW", [P, NRAW, CHUNK])
        w_at = top[0]
        WH = put("WH", [P, NSLOT, CHUNK], F32R)
        WF = put("WF", [P, NSLOT, CHUNK], at=w_at)
        WL = put("WL", [P, NSLOT, CHUNK], F32R)
        a_at = top[0]
        AH = put("AH", [P, NR, TOK], F32R)
        AL = put("AL", [P, NR, TOK], F32R)
        BH = put("BH", [P, KD, TOK], F32R)
        BL = put("BL", [P, KD, TOK], F32R)
        CH = put("CH", [P, KD, TOK], F32R)
        CL = put("CL", [P, KD, TOK], F32R)
        CV = put("CV", [P, NCOLS])
        CN = put("CN", [P, NCONST])
        IDR = put("IDR", [P, P], F32R)
        MASKR = put("MASKR", [P, P], F32R)
        st_at = top[0]
        top[0] += 2816
        pr = -(-top[0] // 64) * 64
        st = [st_at]

        def small(name, cols):
            off = st[0]
            st[0] += 4 * cols
            assert st[0] <= st_at + 2816
            return nc.alloc_sbuf_tensor_at(name, [P, cols], F32, offset=off, align_bytes=4)

        def col(name, j=0, n=1, parts=P):
            lo = COLS[name][0] + j
            return CV[0:parts, lo:lo + n]

        def const(name):
            return CN[:, CONSTS[name][0]:CONSTS[name][1]]

        ident = const("ident")

        half = small("half", 64)
        ssx = small("ssx", 2)
        rsx = small("rsx", 2)
        kss = small("kss", 16)
        krs = small("krs", 16)
        qss = small("qss", NT * NH)
        rq = small("rq", NT * NH)
        gts = small("gts", NT * 3 * NH)
        gk = small("gk", 3)
        hba = small("hba", NR)
        hbx = small("hbx", NR)
        c4 = small("c4", NR)
        l1 = small("l1", NR)
        l2 = small("l2", NR)
        l3 = small("l3", NR)
        css = small("css", 1)
        crs = small("crs", 1)
        cmx = small("cmx", NT * NH)
        csm = small("csm", NT * NH)
        crw = small("crw", NT * NH)
        mx = small("mx", 8)
        nb = small("nb", 8)
        rs = small("rs", 8)
        ri_ = small("ri_", 8)
        wt = small("wt", 8)
        rs2 = small("rs2", 16)
        ri2 = small("ri2", 16)
        ss1 = small("ss1", 4)
        ss1s = small("ss1s", 2)
        rs1 = small("rs1", 2)
        pmean = small("pmean", 16)
        zss = small("zss", 16)
        zrs = small("zrs", 16)
        oss = small("oss", 4)
        ors = small("ors", 4)
        ysum = small("ysum", 8)
        ymean = small("ymean", 4)
        yss = small("yss", 4)
        yrs = small("yrs", 4)
        tmp = small("tmp", 80)

        XC = put("XC", [RP, 2, RG, TOK], at=pr)
        RGT = put("RGT", [RP, 2, RG, TOK], at=pr + 6144)
        TR = put("TR", [RP, RG, TOK], at=pr + 12288)
        TI = put("TI", [RP, RG, TOK], at=pr + 15360)
        AA = put("AA", [RP, RG, TOK], at=pr + 18432)
        QT = put("QT", [P, KD, TOK], at=pr + 21504)
        KT = put("KT", [P, 2, NKV, TOK], at=pr + 29696)
        V = put("V", [P, NT, 2, 256], at=pr + 37888)
        SM = put("SM", [P, 2, 4, TOK], at=pr + 41984)
        PT = put("PT", [P, 2, NT, 4, P], at=pr + 50176)
        MG = put("MG", [P, 16, TOK], at=pr + 58368)
        VB = put("VB", [P, 2, 8, HD], at=pr + 74752)
        PC = put("PC", [P, 2, TOK], at=pr + 78848)
        assert pr + 80896 <= nc.sbuf_usable_end
        X0 = put("X0", [P, NT, DM], at=pr + 58368)
        XN = put("XN", [P, NT, DM], at=pr + 66560)
        G1R = put("G1R", [P, DM], at=pr + 41984)
        KSQ = put("KSQ", [P, 2, 256], at=pr + 66560)
        KN = put("KN", [P, 2, NT, 4, 2, HD], at=pr + 50176)
        SK = put("SK", [P, 2, NKV, TOK], at=pr)
        QSQ = put("QSQ", [P, 2, TOK], at=pr + 12288)
        XW = put("XW", [P, 2, 16, NGC + 1], at=pr + 58368)
        GTT = put("GTT", [3 * NH, TOK], at=pr + 14336)
        HK = put("HK", [P, 2, NKV, CP], at=pr + 18432)
        HVX = put("HVX", [P, NH, CP], at=pr + 18944)
        HG = put("HG", [P, 2, P], at=pr + 19968)
        SC = put("SC", [P, NT, NH, CP], at=pr + 72704)
        KNC = put("KNC", [NKV * CP, 2, HD], at=pr + 70656)
        KCZ = put("KCZ", [P, NKV, 2, CP], at=pr + 71168)
        X1 = put("X1", [P, NT, DM], at=pr)
        XN2 = put("XN2", [P, NT, DM], at=pr + 21504)
        G2R = put("G2R", [P, DM], at=pr + 29696)
        JK = put("JK", [P, 4, 512], at=pr + 33792)
        CG = put("CG", [P, 4, 2, TOK], at=pr + 37888)
        RAW1 = put("RAW1", [P, CHUNK], at=pr + 46080)
        RQK = put("RQK", [P, 2, NT, AW], at=pr + 8192)
        RT = put("RT", [P, 2, 2, AW], at=pr + 21504)
        QK2 = put("QK2", [P, 2, 4, TOK], at=pr + 29696)
        V2 = put("V2", [P, NT, AW], at=pr + 37888)
        U2 = put("U2", [P, NT, AW], at=pr + 41984)
        Z2 = put("Z2", [P, NT, AW], at=pr + 46080)
        SM2 = put("SM2", [P, 2, 4, TOK], at=pr + 50176)
        PT2 = put("PT2", [P, 2, NT, 4, P], at=pr + 58368)
        OGR = put("OGR", [P, 2 * AW], at=pr + 66560)
        GLN = put("GLN", [P, 2, AW], at=pr + 70656)
        MR = put("MR", [P, NT, DM], at=pr + 21504)
        LN1 = put("LN1", [P, 2, DM], at=a_at)
        WS = put("WS", [P, 8, P], at=a_at + 8192)
        ZT = put("ZT", [P, NT, AW], at=a_at + 12288)
        ZQ = put("ZQ", [P, NT, AW], at=a_at + 16384)
        X3 = put("X3", [P, NT, DM], at=pr + 8192)
        LN2 = put("LN2", [P, 2, DM], at=pr + 66560)
        SG = put("SG", [P, 4, TOK], at=pr + 37888)
        RAW2 = put("RAW2", [P, CHUNK], at=pr + 29696)
        YJ = put("YJ", [P, NT, DM], at=pr + 50176)

        PS = ctx.enter_context(nc.psum_tensor("PS", [P, 8, 512], F32))

        raw_in = [sem(f"raw_in{i}") for i in range(NRAW + 2)]
        plain_in = [sem(f"plain_in{i}") for i in range(2)]
        x_in = [sem(f"x_in{t}") for t in range(NT)]
        w_hi, w_lo, chunk_done, tile0_done, ri_part, y_gain, x_again, const_in, g1_in = (sem(n) for n in (
            "w_hi", "w_lo", "chunk_done", "tile0_done", "ri_part", "y_gain", "x_again", "const_in", "g1_in"))
        g2_in, og_in, gln_in, ln1_in, ln2_in, ws_in, out_done, act_own, dve_own = (sem(n) for n in (
            "g2_in", "og_in", "gln_in", "ln1_in", "ln2_in", "ws_in", "out_done", "act_own", "dve_own"))
        pool_own, x_sq, x_rstd, xn_ready, xt_done, xt_hi, xt_lo, k_sq, k_ss = (sem(n) for n in (
            "pool_own", "x_sq", "x_rstd", "xn_ready", "xt_done", "xt_hi", "xt_lo", "k_sq", "k_ss"))
        k_rstd, kn_ready, kt_done, kt_copied, gk_ready, mb_act, mb_dve, gate_tanh = (sem(n) for n in (
            "k_rstd", "kn_ready", "kt_done", "kt_copied", "gk_ready", "mb_act", "mb_dve", "gate_tanh"))
        gate_ready, qss_done, qss_copied, rq_ready, lam_exp, lam_abs, c4_ready = (sem(n) for n in (
            "gate_ready", "qss_done", "qss_copied", "rq_ready", "lam_exp", "lam_abs", "c4_ready"))
        hg_ready, hgt_done, hk_ready, hk_zero, hvx_ready, kc_done, kc_sq, kc_rstd = (sem(n) for n in (
            "hg_ready", "hgt_done", "hk_ready", "hk_zero", "hvx_ready", "kc_done", "kc_sq", "kc_rstd"))
        knc_ready, kct_done, kcz_ready, vb_ready, sc_done, sc_sub, sc_exp, pc_ready = (sem(n) for n in (
            "knc_ready", "kct_done", "kcz_ready", "vb_ready", "sc_done", "sc_sub", "sc_exp", "pc_ready"))
        pct_done, pct_copied, qk_done, nb_ready, exp_done, p_ready, t_done = (sem(n) for n in (
            "pct_done", "pct_copied", "qk_done", "nb_ready", "exp_done", "p_ready", "t_done"))
        pt0_copied, pt1_copied, pv_done, o_hi, o_lo, rnn_g, la_ready = (sem(n) for n in (
            "pt0_copied", "pt1_copied", "pv_done", "o_hi", "o_lo", "rnn_g", "la_ready"))
        ix_ready, sq_ready, w_ready, root_ready, scan_ready, g_hi, g_lo, m_ready = (sem(n) for n in (
            "ix_ready", "sq_ready", "w_ready", "root_ready", "scan_ready", "g_hi", "g_lo", "m_ready"))
        m_hi, m_lo, x1_ready, x1_sq, x1_ss, x1_rstd, xn2_ready, xt2_done, xt2_hi = (sem(n) for n in (
            "m_hi", "m_lo", "x1_ready", "x1_sq", "x1_ss", "x1_rstd", "xn2_ready", "xt2_done", "xt2_hi"))
        xt2_lo, up_taps, up_conv, up_gelu, up_prod, up_hi, up_lo, x2_ready, xt3_done = (sem(n) for n in (
            "xt2_lo", "up_taps", "up_conv", "up_gelu", "up_prod", "up_hi", "up_lo", "x2_ready", "xt3_done"))
        xt3_hi, xt3_lo, rope_parts, roped, v2_copied, u_ready, z_ready, qkt_done = (sem(n) for n in (
            "xt3_hi", "xt3_lo", "rope_parts", "roped", "v2_copied", "u_ready", "z_ready", "qkt_done"))
        qkt_copied, qk2_done, nb2_ready, exp2_done, t2_done, pt20_copied = (sem(n) for n in (
            "qkt_copied", "qk2_done", "nb2_ready", "exp2_done", "t2_done", "pt20_copied"))
        pt21_copied, pv2_done, z_mean, z_sq, z_ss, z_rstd, zn_ready, ws_ready = (sem(n) for n in (
            "pt21_copied", "pv2_done", "z_mean", "z_sq", "z_ss", "z_rstd", "zn_ready", "ws_ready"))
        mix_done, os_ready, os_ss, os_rstd, mr_ready, mrt_done, mrt_hi, mrt_lo = (sem(n) for n in (
            "mix_done", "os_ready", "os_ss", "os_rstd", "mr_ready", "mrt_done", "mrt_hi", "mrt_lo"))
        y_mean, y_sq, y_rstd, y_ln, xt4_done, xt4_hi, xt4_lo, up2_silu, up2_prod = (sem(n) for n in (
            "y_mean", "y_sq", "y_rstd", "y_ln", "xt4_done", "xt4_hi", "xt4_lo", "up2_silu", "up2_prod"))
        up2_hi, up2_lo, z_gain, masks_ready, wt_ready, h_ready, xw_ready, col_in, gate_t_done, a_starts = (sem(n) for n in (
            "up2_hi", "up2_lo", "z_gain", "masks_ready", "wt_ready", "h_ready", "xw_ready", "col_in", "gate_t_done", "a_starts"))

        def wait_tile(eng, c, t):
            if t == 0:
                eng.wait_ge(tile0_done, T0_NO[c] + 1)
            else:
                eng.wait_ge(chunk_done, c + 1)

        def wait_mb(eng, c, n=0):
            if CHUNKS[c][0] == "ri" and n < RG - 1:
                eng.wait_ge(ri_part, (RG - 1) * CHUNKS[c][1] + n + 1)
            else:
                eng.wait_ge(chunk_done, c + 1)
            return (MB_NO[c] + n) % 2

        def raw(c):
            slot = ARRIVAL[c][0]
            return (RAW[:, slot, :] if slot < NRAW else (RAW1, RAW2)[slot - NRAW][:, :])[:, 0:CHUNKS[c][2]]

        def plain(c):
            return WF[:, c % NSLOT, 0:CHUNKS[c][2]]

        def f32(ap):
            return ap.bitcast(F32)

        def s_view(bank, qt):
            nk = P * (qt + 1)
            return PS[:, bank:bank + 2, 0:2 * nk].rearrange("p b (r k) -> p b r k", r=2)

        def sm_view(buf, u, qt):
            return buf[:, u % 2, :, 0:P * (qt + 1)].rearrange("p (b r) k -> p b r k", b=2)

        def heads4(t, first):
            return t[:, first:first + 4].rearrange("p (r b) -> p b r", b=2)

        XT_BANKS = {0: (0, 1, 2, 3), 2: (6, 7, 0, 1), 3: (6, 7, 0, 1), "m": (6, 7, 6, 7), 4: (4, 5, 6, 7)}
        UP_BANKS = (6, 7, 0, 1)
        UP2_BANKS = (4, 5, 6, 7)
        IN2_BANKS = (2, 4, 6, 4, 6)

        block = ctx.enter_context(nc.Block())

        @block.sync
        def _(eng):
            for t in range(NT):
                eng.dma_start(X0[:, t, :], A_x[t * P:(t + 1) * P, :]).then_inc(x_in[t], 16)
            eng.dma_start(G1R[:, :], A_g1.partition_broadcast(P)).then_inc(g1_in, 16)
            eng.dma_start(CN[:, :], A_consts).then_inc(const_in, 16)
            for c in LOAD_ORDER:
                if c == 1:
                    eng.dma_start(CV[:, :], A_cols).then_inc(col_in, 16)
                source = A_w[OFFS[c]:OFFS[c + 1]].rearrange("(p n) -> p n", p=P)
                if CHUNKS[c][3]:
                    slot, before, _ = ARRIVAL[c]
                    if before is not None:
                        eng.wait_ge(w_lo, before + 1)
                    elif slot == NRAW:
                        eng.wait_ge(pv_done, NU)
                    elif slot == NRAW + 1:
                        eng.wait_ge(qk2_done, NU2)
                    eng.dma_start(raw(c), source).then_inc(raw_in[slot], 16)
                else:
                    eng.wait_ge(chunk_done, c - NSLOT + 1)
                    eng.dma_start(plain(c), source).then_inc(plain_in[PLAIN.index(c) % 2], 16)
            for n in range(2 * NT):
                t, h = divmod(n, 2)
                cols = slice(512 * h, 512 * h + 512)
                eng.wait_ge(y_ln, 2 * NT + n + 1)
                eng.dma_start(A_out[t * P:(t + 1) * P, cols], X3[:, t, cols]).then_inc(out_done, 16)
            eng.wait_ge(out_done, 16 * 2 * NT)

        @block.gpsimd
        def _(eng):
            own = [0]

            def link(ins):
                own[0] += 1
                ins.then_inc(pool_own, 1)
                eng.wait_ge(pool_own, own[0])

            used = [0]

            def power(out, ss, n, mean_of, eps, ready):
                t = tmp[0:out.shape[0], used[0]:used[0] + n]
                used[0] += n
                link(eng.tensor_scalar(t, ss, 1.0 / mean_of, eps, ALU.mult, ALU.add))
                eng.tensor_tensor(out, t, half[0:out.shape[0], 0:n], ALU.pow).then_inc(ready, 1)

            link(eng.memset(half[:, :], -0.5))
            for t in range(NT):
                eng.wait_ge(x_sq, t + 1)
                power(rsx[:, t:t + 1], ssx[:, t:t + 1], 1, DM, EPS, x_rstd)
            for b in range(2):
                eng.wait_ge(k_ss, 2 * b + 2)
                power(krs[:, 8 * b:8 * b + 8], kss[:, 8 * b:8 * b + 8], 8, HD, EPS, k_rstd)
            eng.wait_ge(qss_copied, 1)
            power(rq[:, :], qss[:, :], NT * NH, 1.0, HD * EPS, rq_ready)
            eng.wait_ge(kc_sq, 1)
            power(crs[0:NKV * CP, :], css[0:NKV * CP, :], 1, HD, EPS, kc_rstd)
            for u in range(NU):
                qt = (u >> 1) & 1
                eng.wait_ge(wt_ready, u + 1)
                s = sm_view(SM, u, qt)
                w = heads4(wt, 4 * (u % 2)).unsqueeze(3).broadcast_to([P, 2, 2, P * (qt + 1)])
                eng.tensor_tensor(s, s, w, ALU.mult).then_inc(p_ready, 1)
            for t in range(NT):
                eng.wait_ge(x1_ss, t + 1)
                power(rs1[:, t:t + 1], ss1s[:, t:t + 1], 1, DM, EPS, x1_rstd)
            for i in range(4):
                b, t = divmod(i, 2)
                eng.wait_ge(rope_parts, i + 1)
                eng.tensor_tensor(RQK[:, b, t, :], RT[:, i % 2, 0, :], RT[:, i % 2, 1, :], ALU.add).then_inc(roped, 1)
            eng.wait_ge(ws_in, 16)
            eng.affine_select(out=WS[:, :, :], in_=WS[:, :, :], compare_op=ALU.is_ge, fill=0.0, base=0,
                              pattern=[[0, 8], [1, P]], channel_multiplier=-1).then_inc(ws_ready, 1)
            eng.wait_ge(z_ss, 1)
            power(zrs[:, :], zss[:, :], 16, HD, LN_EPS, z_rstd)
            for n, j in enumerate((2, 3, 0, 1)):
                eng.wait_ge(os_ss, n + 1)
                power(ors[:, j:j + 1], oss[:, j:j + 1], 1, AW, EPS, os_rstd)
            for n in range(2):
                for t in range(NT):
                    eng.wait_ge(y_sq, NT * n + t + 1)
                    j = NT * n + t
                    power(yrs[:, j:j + 1], yss[:, j:j + 1], 1, DM, LN_EPS, y_rstd)

        @block.scalar
        def _(eng):
            own = [0]

            def link(ins):
                own[0] += 1
                ins.then_inc(act_own, 1)
                eng.wait_ge(act_own, own[0])

            def split(c):
                if c >= NCH or not CHUNKS[c][3]:
                    return
                slot, _, n = ARRIVAL[c]
                eng.wait_ge(raw_in[slot], 16 * (n + 1))
                if c >= NSLOT:
                    eng.wait_ge(chunk_done, c - NSLOT + 1)
                eng.activation(WH[:, c % NSLOT, 0:CHUNKS[c][2]], raw(c), ACT.Copy).then_inc(w_hi, 1)

            def evict_hi(H, banks, done, hi, kps=range(4), first=0):
                for n, kp in enumerate(kps):
                    eng.wait_ge(done, first + n + 1)
                    eng.activation(H[:, 2 * kp:2 * kp + 2, :].rearrange("p k t -> p (k t)"), PS[:, banks[kp], :],
                                   ACT.Copy).then_inc(hi, 1)

            def unit_exp(u):
                g, qt, br = u >> 2, (u >> 1) & 1, u & 1
                eng.wait_ge(nb_ready, u + 1)
                if u >= 2:
                    eng.wait_ge(t_done, u - 1)
                    eng.wait_ge(wt_ready, u - 1)
                nk = P * (qt + 1)
                for i in range(4):
                    r = 2 * (i % 2) + i // 2
                    h = NH * qt + 4 * g + r
                    last = eng.activation(SM[:, u % 2, i, 0:nk], PS[:, 2 + i // 2, nk * (i % 2):nk * (i % 2) + nk], ACT.Exp, bias=nb[:, 4 * (u % 2) + i:4 * (u % 2) + i + 1],
                                          scale=rq[:, h:h + 1], accum_out=rs[:, 4 * (u % 2) + r:4 * (u % 2) + r + 1])
                last.then_inc(exp_done, 1)

            def unit_pt(u):
                eng.wait_ge(t_done, u + 1)
                if u >= 2:
                    eng.wait_ge(pv_done, u - 1)
                eng.activation(PT[:, u % 2, 0, :, :].rearrange("p h q -> p (h q)"), PS[:, 4, :], ACT.Copy)\
                   .then_inc(pt0_copied, 1)

            def o_first(v):
                g, qt = v >> 1, v & 1
                eng.wait_ge(pv_done, 2 * v + 2)
                eng.activation(CH[:, 2 * g:2 * g + 2, qt * P:(qt + 1) * P],
                               PS[:, 6 + v % 2, 0:256].rearrange("p (k q) -> p k q", k=2), ACT.Copy).then_inc(o_hi, 1)

            def window(w):
                if w == 0:
                    eng.wait_ge(kc_done, 1)
                    eng.activation(KSQ[0:NKV * CP, 0, 0:HD], PS[0:NKV * CP, 4, 0:HD], ACT.Square,
                                   accum_out=css[0:NKV * CP, :]).then_inc(kc_sq, 1)
                if w == 1:
                    eng.wait_ge(kct_done, 1)
                    eng.wait_ge(gk_ready, 1)
                    eng.wait_ge(hk_zero, 3)
                    for b in range(2):
                        last = eng.activation(KCZ[64 * b:64 * b + 64, :, b, :],
                                              PS[64 * b:64 * b + 64, 5, 0:NKV * CP].rearrange("p (g c) -> p g c", g=NKV),
                                              ACT.Copy, scale=gk[64 * b:64 * b + 64, 0:1])
                    last.then_inc(kcz_ready, 1)
                if w == 4:
                    eng.wait_ge(pct_done, 1)
                    eng.activation(PC[:, :, :].rearrange("p a q -> p (a q)"), PS[:, 6, :], ACT.Copy).then_inc(pct_copied, 1)
                if 0 <= w - 4 < NU:
                    unit_pt(w - 4)
                if 0 <= w - 5 < NU and (w - 5) % 2:
                    o_first((w - 5) // 2)
                G = rg_group(w, RG_A)
                if G is not None:
                    eng.wait_ge(la_ready, G + 1)
                    link(eng.activation(AA[:, :, :], TR[:, :, :], ACT.Exp))
                    eng.activation(TR[:, :, :], TR[:, :, :], ACT.Tanh)
                    eng.wait_ge(ix_ready, G + 1)
                    eng.activation(XC[:, G % 2, :, :], AA[:, :, :], ACT.Square).then_inc(sq_ready, 1)
                G = rg_group(w, RG_ROOTS)
                if G is not None:
                    eng.wait_ge(w_ready, G + 1)
                    eng.activation(XC[:, G % 2, :, :], TR[:, :, :], ACT.Sqrt, scale=-0.25).then_inc(root_ready, 1)
                    eng.wait_ge(rnn_g, RG * (G + 1))
                    eng.activation(RGT[:, G % 2, :, :], RGT[:, G % 2, :, :], ACT.Gelu_apprx_tanh)\
                       .then_inc(root_ready, 1)

            def unit2_exp(u):
                hg, qt = u >> 1, u & 1
                eng.wait_ge(nb2_ready, u + 1)
                if u >= 2:
                    eng.wait_ge(t2_done, u - 1)
                nk = P * (qt + 1)
                for i in range(4):
                    h = 8 * qt + 4 * hg + 2 * (i % 2) + i // 2
                    last = eng.activation(SM2[:, u % 2, i, 0:nk], PS[:, i // 2, nk * (i % 2):nk * (i % 2) + nk], ACT.Exp, bias=nb[:, 4 * (u % 2) + i:4 * (u % 2) + i + 1],
                                          scale=HD ** -0.5, accum_out=rs2[:, h:h + 1])
                last.then_inc(exp2_done, 1)

            def unit2_pt(u):
                eng.wait_ge(t2_done, u + 1)
                if u >= 2:
                    eng.wait_ge(pv2_done, u - 1)
                eng.activation(PT2[:, u % 2, 0, :, :].rearrange("p h q -> p (h q)"), PS[:, 2, :], ACT.Copy)\
                   .then_inc(pt20_copied, 1)

            def side(c):
                kind, i, _, _ = CHUNKS[c]
                if kind == "kv":
                    if i % 2 == 0:
                        return
                    br = i // 2
                    for t in range(NT):
                        wait_tile(eng, c, t)
                        eng.activation(V[:, t, br, :], PS[:, 4 + 2 * br + t, 256:512], ACT.Copy)
                        if 2 * br + t >= 2:
                            eng.wait_ge(k_ss, 2 * br + t - 1)
                        eng.activation(KSQ[:, t, :], PS[:, 4 + 2 * br + t, 0:256], ACT.Square).then_inc(k_sq, 1)
                if kind == "cmp":
                    bank = wait_mb(eng, c)
                    for j in range(2):
                        for h in range(2):
                            src = PS[64 * h:64 * h + 64, bank, 256 * j:256 * j + 256]
                            eng.activation(SK[0:64, i, 2 * j + h, :], src, ACT.Copy)
                            last = eng.activation(SK[64:128, i, 2 * j + h, 0:TOK - 1], src[:, 1:TOK], ACT.Copy)
                    last.then_inc(mb_act, 1)
                    if i == 0:
                        eng.wait_ge(lam_abs, 1)
                        eng.activation(l2[0:RP, :], l1[0:RP, :], ACT.Exp, scale=-1.0).then_inc(lam_exp, 1)
                if kind == "gate":
                    eng.wait_ge(chunk_done, c + 1)
                    eng.activation(GTT[:, :], PS[0:3 * NH, 4, 0:TOK], ACT.Tanh, scale=0.5).then_inc(gate_tanh, 1)
                if kind == "q":
                    bank = wait_mb(eng, c)
                    eng.activation(QT[:, 2 * i:2 * i + 2, :].rearrange("p k t -> p (k t)"), PS[:, bank, :], ACT.Copy)
                    if i:
                        eng.wait_ge(qss_done, i)
                    eng.activation(QSQ[:, :, :].rearrange("p k t -> p (k t)"), PS[:, bank, :], ACT.Square)\
                       .then_inc(mb_act, 1)
                if kind == "w1":
                    eng.wait_ge(chunk_done, c + 1)
                    eng.activation(HG[0:NGC, i, :], PS[0:NGC, 2 + i, 0:P], ACT.Gelu_apprx_tanh)\
                       .then_inc(hg_ready, 1)
                if kind == "rnn":
                    bank = wait_mb(eng, c)
                    G, t = divmod(i, RG)
                    if G >= 2:
                        eng.wait_ge(g_lo, G - 1)
                    eng.activation(XC[:, G % 2, t, :], PS[0:RP, bank, 0:256], ACT.Identity,
                                   bias=col("cb", i, parts=RP), scale=col("cw", 3 * NR + i, parts=RP))
                    eng.activation(RGT[:, G % 2, t, :], PS[0:RP, bank, 256:512], ACT.Copy).then_inc(rnn_g, 1)
                if kind == "mg":
                    bank = wait_mb(eng, c)
                    eng.activation(MG[:, 2 * i:2 * i + 2, :].rearrange("p k t -> p (k t)"), PS[:, bank, :], ACT.Tanh,
                                   scale=0.5).then_inc(mb_act, 1)
                if kind == "ri":
                    if i >= 1:
                        eng.wait_ge(scan_ready, i)
                    for t in range(RG):
                        bank = wait_mb(eng, c, t)
                        n = RG * i + t
                        eng.activation(TR[:, t, :], PS[0:RP, bank, 0:256], ACT.Tanh, bias=hba[0:RP, n:n + 1], scale=0.5)
                        eng.activation(TI[:, t, :], PS[0:RP, bank, 256:512], ACT.Tanh, bias=hbx[0:RP, n:n + 1],
                                       scale=0.5).then_inc(mb_act, 1)
                        if t == 0 and 0 <= c - W0 - 3 < NU:
                            unit_exp(c - W0 - 3)
                if kind == "ro":
                    if i == 0:
                        eng.wait_ge(g_lo, NG)
                        eng.wait_ge(scan_ready, NG)
                        eng.dma_start(X1[:, :, :], A_x.rearrange("(t p) d -> p t d", p=P)).then_inc(x_again, 16)
                        eng.wait_ge(qk_done, NU)
                        eng.dma_start(G2R[:, :], A_g2.partition_broadcast(P)).then_inc(g2_in, 16)
                    if i >= 1:
                        m_first(i - 1)
                    if i == 7:
                        m_first(7)
                if kind == "wo" and i % 2:
                    for t in range(NT):
                        n = i // 2
                        eng.wait_ge(x1_ready, NT * n + t + 1)
                        eng.activation(JK[:, 2 * n + t, :], X1[:, t, 512 * n:512 * n + 512], ACT.Square,
                                       accum_out=ss1[:, 2 * t + n:2 * t + n + 1]).then_inc(x1_sq, 1)
                    if i == 3:
                        evict_hi(CH, XT_BANKS[2], xt2_done, xt2_hi)
                if kind == "up":
                    up_taps_of(i)
                    if i >= 1:
                        up_gelu_of(i - 1)
                    if i >= 2:
                        up_first(i - 2)
                    if i == N_UP - 1:
                        up_gelu_of(i)
                        up_first(i - 1)
                        up_first(i)
                if kind == "dn" and i == N_UP // 2 - 1:
                    for a, b, s in ((LN1, A_ln1, ln1_in), (OGR, A_og, og_in), (GLN, A_gln, gln_in)):
                        if a is LN1:
                            eng.wait_ge(chunk_done, c + 1)
                            eng.dma_start(WS[:, :, :], A_ws).then_inc(ws_in, 16)
                        flat = a[:, :] if a is OGR else a[:, :, :].rearrange("p a n -> p (a n)")
                        eng.dma_start(flat, b.partition_broadcast(P)).then_inc(s, 16)
                    evict_hi(BH, XT_BANKS[3], xt3_done, xt3_hi)
                if kind == "in2":
                    if i == 3:
                        eng.wait_ge(qkt_done, 1)
                        eng.activation(QK2[:, 0, :, :], PS[:, 0:2, :].rearrange("p b (j t) -> p (b j) t", j=2), ACT.Copy)\
                           .then_inc(qkt_copied, 1)
                    if i == 4:
                        eng.wait_ge(qkt_done, 2)
                        eng.activation(QK2[:, 1, :, :], PS[:, 2:4, :].rearrange("p b (j t) -> p (b j) t", j=2), ACT.Copy)\
                           .then_inc(qkt_copied, 1)
                    if i == 5:
                        for t in range(NT):
                            wait_tile(eng, c, t)
                            eng.activation(V2[:, t, :], PS[:, IN2_BANKS[2] + t, :], ACT.Copy).then_inc(v2_copied, 1)
                        unit2_exp(0)
                    if i == 6:
                        unit2_pt(0)
                        unit2_exp(1)
                    if i == 7:
                        for t in range(NT):
                            wait_tile(eng, c, t)
                            eng.activation(Z2[:, t, :], PS[:, IN2_BANKS[3] + t, :], ACT.Gelu).then_inc(z_ready, 1)
                        unit2_pt(1)
                        for t in range(NT):
                            eng.wait_ge(z_mean, t + 1)
                            eng.activation(ZQ[:, t, :], ZT[:, t, :], ACT.Square).then_inc(z_sq, 1)
                        unit2_exp(2)
                    if i == 8:
                        unit2_pt(2)
                        unit2_exp(3)
                    if i == 9:
                        for t in range(NT):
                            wait_tile(eng, c, t)
                            eng.activation(U2[:, t, :], PS[:, IN2_BANKS[4] + t, :], ACT.Gelu).then_inc(u_ready, 1)
                        unit2_pt(3)
                        split(c + 2)
                        for part in (1, 0):
                            for t in range(NT):
                                eng.wait_ge(os_ready, NT * (1 - part) + t + 1)
                                eng.activation(YJ[:, t, AW * part:AW * part + AW], MR[:, t, AW * part:AW * part + AW], ACT.Square,
                                               accum_out=oss[:, 2 * part + t:2 * part + t + 1]).then_inc(os_ss, 1)
                        evict_hi(CH, XT_BANKS["m"], mrt_done, mrt_hi, kps=(2, 3))
                if kind == "wo2" and i == 1:
                    evict_hi(CH, XT_BANKS["m"], mrt_done, mrt_hi, kps=(0, 1), first=2)
                if kind == "wo2" and i == 2:
                    norm_squares(0)
                    eng.wait_ge(mr_ready, 4)
                    eng.dma_start(LN2[:, :, :].rearrange("p a n -> p (a n)"), A_ln2.partition_broadcast(P))\
                       .then_inc(ln2_in, 16)
                    evict_hi(BH, XT_BANKS[4], xt4_done, xt4_hi)
                if kind == "up2":
                    up2_silu_of(i)
                    if i >= 1:
                        up2_first(i - 1)
                    if i == N_UP2 - 1:
                        up2_first(i)
                if kind == "dn2" and i == N_UP2 // 2 - 1:
                    norm_squares(1)

            def m_first(i):
                eng.wait_ge(m_ready, i + 1)
                eng.activation(BH[:, i, :], MG[:, i, :], ACT.Copy).then_inc(m_hi, 1)

            def norm_squares(n):
                for t in range(NT):
                    j = NT * n + t
                    eng.wait_ge(y_mean, j + 1)
                    eng.activation(YJ[:, t, :], (X1 if n == 0 else X3)[:, t, :], ACT.Square, bias=ymean[:, j:j + 1],
                                   accum_out=yss[:, j:j + 1]).then_inc(y_sq, 1)

            def up_taps_of(i):
                eng.wait_ge(chunk_done, AT["up", i] + 1)
                if i >= 4:
                    eng.wait_ge(up_lo, i - 3)
                for v in range(2):
                    f = N_UP * v + i
                    last = eng.activation(CG[:, i % 4, v, :], PS[:, UP_BANKS[i % 4], 256 * v:256 * v + 256], ACT.Identity,
                                          bias=col("fb", f), scale=col("fw", 2 * 2 * N_UP + f))
                last.then_inc(up_taps, 1)

            def up_gelu_of(i):
                eng.wait_ge(up_conv, i + 1)
                eng.activation(CG[:, i % 4, 0, :], CG[:, i % 4, 0, :], ACT.Gelu_apprx_tanh).then_inc(up_gelu, 1)

            def up_first(i):
                eng.wait_ge(up_prod, i + 1)
                if i >= NR:
                    eng.wait_ge(chunk_done, AT["dn", (i - NR) // 2] + 1)
                eng.activation(AH[:, i % NR, :], CG[:, i % 4, 0, :], ACT.Copy).then_inc(up_hi, 1)

            def up2_silu_of(i):
                eng.wait_ge(chunk_done, AT["up2", i] + 1)
                if i >= 4:
                    eng.wait_ge(up2_lo, i - 3)
                eng.activation(SG[:, i % 4, :], PS[:, UP2_BANKS[i % 4], 0:256], ACT.Silu).then_inc(up2_silu, 1)

            def up2_first(i):
                eng.wait_ge(up2_prod, i + 1)
                if i >= NR:
                    eng.wait_ge(chunk_done, AT["dn2", (i - NR) // 2] + 1)
                eng.activation(AH[:, i % NR, :], SG[:, i % 4, :], ACT.Copy).then_inc(up2_hi, 1)

            for t in range(NT):
                eng.wait_ge(x_in[t], 16)
                eng.activation(XN[:, t, :], X0[:, t, :], ACT.Square, accum_out=ssx[:, t:t + 1]).then_inc(x_sq, 1)
            evict_hi(BH, XT_BANKS[0], xt_done, xt_hi, kps=(0, 1))
            split(0)
            evict_hi(BH, XT_BANKS[0], xt_done, xt_hi, kps=(2, 3), first=2)
            split(1)
            eng.wait_ge(const_in, 16)
            eng.activation(IDR[:, :], ident, ACT.Copy)
            eng.activation(MASKR[:, :], const("mask"), ACT.Copy).then_inc(masks_ready, 1)
            for c in range(NCH):
                if CHUNKS[c][:2] != ("in2", 9):
                    split(c + 2)
                G = rg_group(c - W0, RG_SPLIT)
                if G is not None:
                    eng.wait_ge(scan_ready, G + 1)
                    eng.activation(AH[0:RP, RG * G:RG * G + RG, :], XC[:, G % 2, :, :], ACT.Copy).then_inc(g_hi, 1)
                if c - W0 == 3:
                    eng.wait_ge(sc_sub, 1)
                    eng.activation(SC[:, :, :, :], SC[:, :, :, :], ACT.Exp).then_inc(sc_exp, 1)
                if 0 <= c - W0 - 3 < NU and CHUNKS[c][0] != "ri":
                    unit_exp(c - W0 - 3)
                side(c)
                if c >= W0:
                    window(c - W0)

        @block.vector
        def _(eng):
            own = [0]

            def link(ins):
                own[0] += 1
                ins.then_inc(dve_own, 1)
                eng.wait_ge(dve_own, own[0])

            def split(c):
                if c >= NCH or not CHUNKS[c][3]:
                    return
                s = SPLIT_NO[c]
                eng.wait_ge(w_hi, s + 1)
                eng.tensor_tensor(WL[:, c % NSLOT, 0:CHUNKS[c][2]], raw(c), f32(WH[:, c % NSLOT, 0:CHUNKS[c][2]]),
                                  ALU.subtract).then_inc(w_lo, 1)

            def evict_lo(H, L, banks, hi, lo, kps=range(4), first=0):
                for n, kp in enumerate(kps):
                    eng.wait_ge(hi, first + n + 1)
                    eng.tensor_tensor(L[:, 2 * kp:2 * kp + 2, :].rearrange("p k t -> p (k t)"), PS[:, banks[kp], :],
                                      f32(H[:, 2 * kp:2 * kp + 2, :].rearrange("p k t -> p (k t)")),
                                      ALU.subtract).then_inc(lo, 1)

            def unit_max(u):
                g, qt, br = u >> 2, (u >> 1) & 1, u & 1
                eng.wait_ge(qk_done, u + 1)
                m = mx[:, 4 * (u % 2):4 * (u % 2) + 4]
                link(eng.tensor_reduce(m.rearrange("p (b r) -> p b r", b=2), s_view(2, qt), AX, ALU.max, negate=True))
                q = heads4(rq[:, NH * qt:NH * qt + NH], 4 * g)
                if u == 0:
                    eng.wait_ge(rq_ready, 1)
                eng.tensor_tensor(nb[:, 4 * (u % 2):4 * (u % 2) + 4].rearrange("p (b r) -> p b r", b=2),
                                  m.rearrange("p (b r) -> p b r", b=2), q, ALU.mult).then_inc(nb_ready, 1)

            def unit_weights(u):
                g, qt, br = u >> 2, (u >> 1) & 1, u & 1
                eng.wait_ge(exp_done, u + 1)
                o = 4 * (u % 2)
                link(eng.reciprocal(ri_[:, o:o + 4], rs[:, o:o + 4]))
                gate = gts[:, 48 * qt + 12 * g + br + 1:48 * qt + 12 * g + br + 11:3]
                if u >= 2:
                    eng.wait_ge(p_ready, u - 1)
                eng.tensor_tensor(wt[:, o:o + 4], ri_[:, o:o + 4], gate, ALU.mult).then_inc(wt_ready, 1)

            def unit_pt(u):
                if (u >> 1) & 1:
                    eng.wait_ge(t_done, u + 1)
                    if u >= 2:
                        eng.wait_ge(pv_done, u - 1)
                    eng.tensor_copy(PT[:, u % 2, 1, :, :].rearrange("p h q -> p (h q)"), PS[:, 5, :])\
                       .then_inc(pt1_copied, 1)

            def o_second(v):
                g, qt = v >> 1, v & 1
                eng.wait_ge(o_hi, v + 1)
                eng.tensor_tensor(CL[:, 2 * g:2 * g + 2, qt * P:(qt + 1) * P],
                                  PS[:, 6 + v % 2, 0:256].rearrange("p (k q) -> p k q", k=2),
                                  f32(CH[:, 2 * g:2 * g + 2, qt * P:(qt + 1) * P]), ALU.subtract).then_inc(o_lo, 1)

            def window(w):
                if w == 0:
                    eng.wait_ge(hgt_done, 2)
                    eng.wait_ge(hk_zero, 2)
                    for g in range(NKV):
                        last = eng.tensor_copy(HVX[:, 4 * g:4 * g + 4, 0:NC],
                                               PS[:, 3, P + CP * g:P + CP * g + NC].unsqueeze(1).broadcast_to([P, 4, NC]))
                    last.then_inc(hvx_ready, 1)
                    eng.wait_ge(kc_rstd, 1)
                    eng.tensor_tensor(KNC[:, :, :],
                                      PS[0:NKV * CP, 4, 0:HD].unsqueeze(1).broadcast_to([NKV * CP, 2, HD]),
                                      crs[0:NKV * CP, 0:1].unsqueeze(1).broadcast_to([NKV * CP, 2, HD]),
                                      ALU.mult).then_inc(knc_ready, 1)
                if w == 1:
                    eng.wait_ge(kc_done, 3)
                    for T in range(2):
                        last = eng.tensor_tensor(
                            VB[:, T, :, :], PS[:, 7, 64 * T:64 * T + 64].unsqueeze(1).broadcast_to([P, 8, HD]),
                            const("m8").unsqueeze(2).broadcast_to([P, 8, HD]), ALU.mult)
                        last.then_inc(vb_ready, 1)
                if w == 2:
                    eng.wait_ge(sc_done, 1)
                    eng.wait_ge(rq_ready, 1)
                    hs = [P, NH, CP]

                    def per_head(t, tt):
                        return t[:, NH * tt:NH * tt + NH].unsqueeze(2).broadcast_to(hs)

                    for tt in range(NT):
                        m = const("cadd")[:, CP * tt:CP * tt + CP].unsqueeze(1).broadcast_to(hs)
                        link(eng.tensor_tensor(SC[:, tt, :, :],
                                               PS[:, 5, 256 * tt:256 * tt + 256].rearrange("p (h c) -> p h c", h=NH),
                                               m, ALU.add))
                    link(eng.tensor_reduce(cmx[:, :], SC[:, :, :, :].rearrange("p a h c -> p (a h) c"), AX, ALU.max))
                    for tt in range(NT):
                        link(eng.tensor_tensor(SC[:, tt, :, :], SC[:, tt, :, :], per_head(cmx, tt), ALU.subtract))
                        ins = eng.tensor_tensor(SC[:, tt, :, :], SC[:, tt, :, :], per_head(rq, tt), ALU.mult)
                        if tt == 0:
                            link(ins)
                    ins.then_inc(sc_sub, 1)
                if w == 3:
                    eng.wait_ge(sc_exp, 1)
                    eng.wait_ge(gate_ready, 1)
                    link(eng.tensor_reduce(csm[:, :], SC[:, :, :, :].rearrange("p a h c -> p (a h) c"), AX, ALU.add))
                    link(eng.reciprocal(crw[:, :], csm[:, :]))
                    link(eng.tensor_tensor(crw[:, :], crw[:, :], gts[:, 0:NT * 3 * NH:3], ALU.mult))
                    hs = [P, NH, CP]
                    for tt in range(NT):
                        m = const("c01")[:, CP * tt:CP * tt + CP].unsqueeze(1).broadcast_to(hs)
                        link(eng.tensor_tensor(SC[:, tt, :, :], SC[:, tt, :, :], m, ALU.mult))
                        ins = eng.tensor_tensor(SC[:, tt, :, :], SC[:, tt, :, :],
                                                crw[:, NH * tt:NH * tt + NH].unsqueeze(2).broadcast_to(hs), ALU.mult)
                        if tt == 0:
                            link(ins)
                    ins.then_inc(pc_ready, 1)
                if 0 <= w - 4 < NU:
                    unit_pt(w - 4)
                if 0 <= w - 5 < NU and (w - 5) % 2:
                    o_second((w - 5) // 2)
                G = rg_group(w, RG_LOG_A)
                if G is not None:
                    eng.wait_ge(mb_act, MB_COUNTS[MB_NO[AT["ri", G]] + RG - 1])
                    if G == 0:
                        eng.wait_ge(c4_ready, 1)
                    eng.scalar_tensor_tensor(TR[:, :, :], TR[:, :, :], 1.0,
                                             c4[0:RP, RG * G:RG * G + RG].unsqueeze(2).broadcast_to([RP, RG, TOK]),
                                             ALU.add, ALU.mult).then_inc(la_ready, 1)
                    eng.scalar_tensor_tensor(TI[:, :, :], TI[:, :, :], 1.0, XC[:, G % 2, :, :], ALU.add, ALU.mult)\
                       .then_inc(ix_ready, 1)
                G = rg_group(w, RG_SQUARES)
                if G is not None:
                    eng.wait_ge(sq_ready, G + 1)
                    eng.scalar_tensor_tensor(TR[:, :, :], XC[:, G % 2, :, :], 1.0, TR[:, :, :], ALU.add, ALU.mult)\
                       .then_inc(w_ready, 1)
                    eng.memset(AA[:, :, 0:1], 0.0).then_inc(a_starts, 1)
                G = rg_group(w, RG_SCAN)
                if G is not None:
                    x = XC[:, G % 2, :, :]
                    eng.wait_ge(root_ready, 2 * G + 1)
                    eng.wait_ge(a_starts, G + 1)
                    link(eng.tensor_tensor(TI[:, :, :], x, TI[:, :, :], ALU.mult))
                    flat = [b.rearrange("p k t -> p (k t)") for b in (TR[:, :, :], AA[:, :, :], TI[:, :, :])]
                    eng.tensor_tensor_scan(flat[0], flat[1], flat[2], 0.0, ALU.mult, ALU.add).then_inc(h_ready, 1)

            def side(c):
                kind, i, _, _ = CHUNKS[c]
                if kind == "kv" and i % 2:
                    br = i // 2
                    for t in range(NT):
                        eng.wait_ge(k_sq, 2 * br + t + 1)
                        o = 8 * br + 4 * t
                        eng.tensor_reduce(kss[:, o:o + 4], KSQ[:, t, :].rearrange("p (g d) -> p g d", g=4), AX, ALU.add)\
                           .then_inc(k_ss, 1)
                    eng.wait_ge(k_rstd, br + 1)
                    for t in range(NT):
                        o = 8 * br + 4 * t
                        src = PS[:, 4 + 2 * br + t, 0:256].rearrange("p (g d) -> p g d", g=4)
                        eng.tensor_tensor(KN[:, br, t, :, :, :], src.unsqueeze(2).broadcast_to([P, 4, 2, HD]),
                                          krs[:, o:o + 4].unsqueeze(2).unsqueeze(2).broadcast_to([P, 4, 2, HD]),
                                          ALU.mult).then_inc(kn_ready, 1)
                if kind == "kv" and i == 0:
                    eng.wait_ge(col_in, 16)
                    for n, name in enumerate(("gkc", "gks", "gkw")):
                        last = eng.tensor_tensor(gk[:, n:n + 1], col(name), col("gq"), ALU.mult)
                    last.then_inc(gk_ready, 1)
                    eng.tensor_scalar(hba[:, :], col("ba", n=NR), 0.5, None, ALU.mult)
                    eng.tensor_scalar(hbx[:, :], col("bx", n=NR), 0.5, None, ALU.mult)
                    eng.scalar_tensor_tensor(l1[:, :], col("lam", n=NR), -1.0, col("lam", n=NR), ALU.mult, ALU.max)\
                       .then_inc(lam_abs, 1)
                if kind == "cmp" and i == 0:
                    eng.memset(HK[:, :, :, :], 0.0).then_inc(hk_zero, 1)
                    eng.memset(HVX[:, :, :], 0.0).then_inc(hk_zero, 1)
                    eng.memset(KCZ[:, :, :, :], 0.0).then_inc(hk_zero, 1)
                if kind == "cmp" and i == 1:
                    eng.wait_ge(lam_exp, 1)
                    z, s, p, q = (t[0:RP, :] for t in (l2, l1, l3, c4))
                    link(eng.tensor_scalar(s, z, 2.0, None, ALU.add))
                    link(eng.reciprocal(p, s))
                    link(eng.tensor_tensor(s, p, z, ALU.mult))
                    link(eng.tensor_tensor(z, s, s, ALU.mult))
                    link(eng.tensor_scalar(p, z, 1.0 / 17, None, ALU.mult))
                    for k in range(7, 0, -1):
                        link(eng.scalar_tensor_tensor(p, p, 1.0 / (2 * k + 1), z, ALU.add, ALU.mult))
                    link(eng.scalar_tensor_tensor(p, p, 1.0, s, ALU.add, ALU.mult))
                    link(eng.tensor_scalar(q, col("lam", n=NR, parts=RP), 4.0, 0.0, ALU.mult, ALU.min))
                    eng.scalar_tensor_tensor(q, p, -8.0, q, ALU.mult, ALU.add).then_inc(c4_ready, 1)
                if kind == "gate" or kind == "q" and i == 0:
                    n = 0 if kind == "gate" else 1
                    eng.wait_ge(mb_act, n + 1)
                    tokens = SK[:, n, :, :].rearrange("p g t -> p (g t)").rearrange("p (j l two) -> p l j two", l=8, two=2)
                    places = col(("pek", "pev")[n], n=16)
                    for half in range(2):
                        eng.tensor_tensor(XW[:, n, 8 * half:8 * half + 8, 0:NGC], tokens[:, :, half:half + NGC, 0],
                                          places[:, 8 * half:8 * half + 8].unsqueeze(2).broadcast_to([P, 8, NGC]),
                                          ALU.add).then_inc(xw_ready, 1)
                if kind == "q" and i == 0:
                    eng.wait_ge(gate_t_done, 1)
                    eng.tensor_scalar(gts[:, :], PS[:, 4, TOK:TOK + NT * 3 * NH], 0.5, 0.5, ALU.mult, ALU.add)\
                       .then_inc(gate_ready, 1)
                if kind == "cmp":
                    eng.wait_ge(kt_done, i + 1)
                    eng.wait_ge(gk_ready, 1)
                    bank = (2, 6)[i]
                    eng.tensor_scalar(KT[:, i, :, :], PS[:, bank:bank + 2, :].rearrange("p b (g t) -> p (b g) t", g=2),
                                      gk[:, 1 + i:2 + i], None, ALU.mult).then_inc(kt_copied, 1)
                if kind == "w1" and i == 1:
                    eng.wait_ge(qss_done, 4)
                    eng.tensor_copy(qss[:, :], PS[:, 5, 0:NT * NH]).then_inc(qss_copied, 1)
                if kind == "w1" and i == 1:
                    eng.wait_ge(hgt_done, 1)
                    eng.wait_ge(hk_zero, 1)
                    eng.tensor_copy(HK[:, 0, :, 0:NC], PS[:, 2, P:P + NKV * CP].rearrange("p (g c) -> p g c", g=NKV)[:, :, 0:NC])\
                       .then_inc(hk_ready, 1)
                if kind == "rnn":
                    bank = wait_mb(eng, c)
                    G, t = divmod(i, RG)
                    eng.wait_ge(rnn_g, i + 1)
                    for s in range(1, 4):
                        o = XC[:, G % 2, t, s:TOK]
                        ins = eng.scalar_tensor_tensor(o, PS[0:RP, bank, 0:TOK - s],
                                                       col("cw", (3 - s) * NR + i, parts=RP), o, ALU.mult, ALU.add)
                        if s < 3:
                            link(ins)
                    ins.then_inc(mb_dve, 1)
                if kind == "ao":
                    bank = wait_mb(eng, c)
                    t = MG[:, 8 + 2 * i:10 + 2 * i, :].rearrange("p k t -> p (k t)")
                    eng.scalar_tensor_tensor(t, t, 1.0, PS[:, bank, :], ALU.add, ALU.mult).then_inc(mb_dve, 1)
                if kind == "ro":
                    bank = wait_mb(eng, c)
                    t = MG[:, i, :]
                    link(eng.scalar_tensor_tensor(t, t, 1.0, PS[:, bank, 0:256], ALU.add, ALU.mult))
                    eng.tensor_tensor(t, t, MG[:, 8 + i, :], ALU.add).then_inc(m_ready, 1)
                    if i >= 1:
                        m_second(i - 1)
                    if i == 7:
                        m_second(7)
                if kind == "wo" and i % 2:
                    n = i // 2
                    if n == 0:
                        eng.wait_ge(x_again, 16)
                    for t in range(NT):
                        wait_tile(eng, c, t)
                        o = X1[:, t, 512 * n:512 * n + 512]
                        eng.scalar_tensor_tensor(o, PS[:, 2 + 2 * n + t, :], 0.5, o, ALU.mult, ALU.add)\
                           .then_inc(x1_ready, 1)
                        if i == 3:
                            eng.wait_ge(x1_sq, 3 + t)
                            eng.tensor_tensor(ss1s[:, t:t + 1], ss1[:, 2 * t:2 * t + 1], ss1[:, 2 * t + 1:2 * t + 2], ALU.add)\
                               .then_inc(x1_ss, 1)
                    if i == 3:
                        eng.wait_ge(g2_in, 16)
                        for t in range(NT):
                            eng.wait_ge(x1_rstd, t + 1)
                            for h in range(2):
                                half = slice(512 * h, 512 * h + 512)
                                eng.scalar_tensor_tensor(XN2[:, t, half], X1[:, t, half], rs1[:, t:t + 1], G2R[:, half],
                                                         ALU.mult, ALU.mult).then_inc(xn2_ready, 1)
                        evict_lo(CH, CL, XT_BANKS[2], xt2_hi, xt2_lo)
                        split(c + 2)
                if kind == "up":
                    up_taps_of(i)
                    if i >= 1:
                        up_product(i - 1)
                    if i >= 2:
                        up_second(i - 2)
                    if i == N_UP - 1:
                        up_product(i)
                        up_second(i - 1)
                        up_second(i)
                if kind == "dn" and i == N_UP // 2 - 1:
                    for t in range(NT):
                        wait_tile(eng, c, t)
                        for n in range(2):
                            o = X1[:, t, 512 * n:512 * n + 512]
                            ins = eng.tensor_tensor(o, PS[:, 2 + 2 * t + n, :], o, ALU.add)
                        ins.then_inc(x2_ready, 1)
                    evict_lo(BH, BL, XT_BANKS[3], xt3_hi, xt3_lo)
                    split(c + 2)
                if kind == "in2":
                    if i in (1, 3):
                        b = i // 2
                        for t in range(NT):
                            wait_tile(eng, c, t)
                            j = 2 * b + t
                            if j >= 2:
                                eng.wait_ge(roped, j - 1)
                            src = PS[:, IN2_BANKS[b] + t, :].rearrange("p (h d) -> p h d", h=8)
                            cos = const("cos")[:, HD * t:HD * t + HD].unsqueeze(1).broadcast_to([P, 8, HD])
                            sin = const("sin")[:, HD * t:HD * t + HD]
                            eng.tensor_tensor(RT[:, j % 2, 0, :].rearrange("p (h d) -> p h d", h=8), src, cos, ALU.mult)
                            o = RT[:, j % 2, 1, :].rearrange("p (h d) -> p h d", h=8)
                            hf = HD // 2
                            for a, z in ((0, hf), (hf, 0)):
                                ins = eng.tensor_tensor(o[:, :, a:a + hf], src[:, :, z:z + hf],
                                                        sin[:, a:a + hf].unsqueeze(1).broadcast_to([P, 8, hf]), ALU.mult)
                            ins.then_inc(rope_parts, 1)
                    if i == 5:
                        unit2_max(0)
                    if i == 6:
                        unit2_max(1)
                    if i == 7:
                        for t in range(NT):
                            eng.wait_ge(z_ready, t + 1)
                            z = Z2[:, t, :].rearrange("p (g d) -> p g d", g=8)
                            pm = pmean[:, 8 * t:8 * t + 8]
                            link(eng.tensor_reduce(pm, z, AX, ALU.add))
                            link(eng.tensor_scalar(pm, pm, 1.0 / HD, None, ALU.mult))
                            eng.tensor_tensor(ZT[:, t, :].rearrange("p (g d) -> p g d", g=8), z,
                                              pm.unsqueeze(2).broadcast_to([P, 8, HD]), ALU.subtract).then_inc(z_mean, 1)
                        unit2_pt(1)
                        unit2_max(2)
                        for t in range(NT):
                            eng.wait_ge(z_sq, t + 1)
                            ins = eng.tensor_reduce(zss[:, 8 * t:8 * t + 8], ZQ[:, t, :].rearrange("p (g d) -> p g d", g=8),
                                                    AX, ALU.add)
                        ins.then_inc(z_ss, 1)
                        eng.wait_ge(gln_in, 16)
                        for t in range(NT):
                            eng.tensor_tensor(ZT[:, t, :], ZT[:, t, :], GLN[:, 0, :], ALU.mult).then_inc(z_gain, 1)
                    if i == 8:
                        eng.wait_ge(z_rstd, 1)
                        eng.wait_ge(z_gain, NT)
                        for t in range(NT):
                            z = ZT[:, t, :].rearrange("p (g d) -> p g d", g=8)
                            link(eng.tensor_tensor(z, z, zrs[:, 8 * t:8 * t + 8].unsqueeze(2).broadcast_to([P, 8, HD]),
                                                   ALU.mult))
                            eng.tensor_tensor(ZT[:, t, :], ZT[:, t, :], GLN[:, 1, :], ALU.add).then_inc(zn_ready, 1)
                        unit2_max(3)
                    if i == 9:
                        unit2_pt(3)
                        eng.wait_ge(mix_done, 1)
                        for t in range(NT):
                            m = MR[:, t, AW:2 * AW].rearrange("p (b g d) -> p b g d", b=2, g=4)
                            mixed = PS[:, 0:2, :].rearrange("p b (g t d) -> p b g t d", g=4, t=NT)[:, :, :, t, :]
                            bias = col("bs", n=8).rearrange("p (b g) -> p b g", b=2).unsqueeze(3).broadcast_to([P, 2, 4, HD])
                            link(eng.tensor_tensor(m, mixed, bias, ALU.add))
                            eng.wait_ge(u_ready, t + 1)
                            eng.tensor_tensor(m, m, U2[:, t, :].rearrange("p (b g d) -> p b g d", b=2, g=4), ALU.mult)\
                               .then_inc(os_ready, 1)
                        for t in range(NT):
                            eng.wait_ge(exp2_done, NU2)
                            eng.wait_ge(pv2_done, NU2)
                            if t == 0:
                                link(eng.reciprocal(ri2[:, :], rs2[:, :]))
                            eng.tensor_tensor(MR[:, t, 0:AW].rearrange("p (h d) -> p h d", h=8),
                                              PS[:, 4 + t, :].rearrange("p (h d) -> p h d", h=8),
                                              ri2[:, 8 * t:8 * t + 8].unsqueeze(2).broadcast_to([P, 8, HD]),
                                              ALU.mult).then_inc(os_ready, 1)
                        eng.wait_ge(og_in, 16)
                        for part in (1, 0):
                            for t in range(NT):
                                eng.wait_ge(os_rstd, NT * (1 - part) + t + 1)
                                m = MR[:, t, AW * part:AW * part + AW]
                                eng.scalar_tensor_tensor(m, m, ors[:, 2 * part + t:2 * part + t + 1],
                                                         OGR[:, AW * part:AW * part + AW], ALU.mult, ALU.mult)\
                                   .then_inc(mr_ready, 1)
                        evict_lo(CH, CL, XT_BANKS["m"], mrt_hi, mrt_lo, kps=(2, 3))
                        split(c + 2)
                if kind == "wo2" and i == 1:
                    evict_lo(CH, CL, XT_BANKS["m"], mrt_hi, mrt_lo, kps=(0, 1), first=2)
                if kind == "wo2" and i == 0:
                    for t in range(NT):
                        residual_sum(0, t, 0)
                if kind == "wo2" and i == 2:
                    layer_norm(0)
                    evict_lo(BH, BL, XT_BANKS[4], xt4_hi, xt4_lo)
                    split(c + 2)
                if kind == "up2":
                    up2_product(i)
                    if i >= 1:
                        up2_second(i - 1)
                    if i == N_UP2 - 1:
                        up2_second(i)
                if kind == "dn2" and i == N_UP2 // 2 - 1:
                    layer_norm(1)

            def m_second(i):
                eng.wait_ge(m_hi, i + 1)
                eng.tensor_tensor(BL[:, i, :], MG[:, i, :], f32(BH[:, i, :]), ALU.subtract).then_inc(m_lo, 1)

            def up_taps_of(i):
                eng.wait_ge(up_taps, i + 1)
                for s in (1, 2):
                    for v in range(2):
                        f = N_UP * v + i
                        o = CG[:, i % 4, v, s:TOK]
                        ins = eng.scalar_tensor_tensor(o, PS[:, UP_BANKS[i % 4], 256 * v:256 * v + TOK - s],
                                                       col("fw", (2 - s) * 2 * N_UP + f), o, ALU.mult, ALU.add)
                        if s == 1:
                            link(ins)
                ins.then_inc(up_conv, 1)

            def up_product(i):
                eng.wait_ge(up_gelu, i + 1)
                eng.tensor_tensor(CG[:, i % 4, 0, :], CG[:, i % 4, 0, :], CG[:, i % 4, 1, :], ALU.mult)\
                   .then_inc(up_prod, 1)

            def up_second(i):
                eng.wait_ge(up_hi, i + 1)
                eng.tensor_tensor(AL[:, i % NR, :], CG[:, i % 4, 0, :], f32(AH[:, i % NR, :]), ALU.subtract)\
                   .then_inc(up_lo, 1)

            def up2_product(i):
                eng.wait_ge(up2_silu, i + 1)
                eng.tensor_tensor(SG[:, i % 4, :], PS[:, UP2_BANKS[i % 4], 256:512], SG[:, i % 4, :], ALU.mult)\
                   .then_inc(up2_prod, 1)

            def up2_second(i):
                eng.wait_ge(up2_hi, i + 1)
                eng.tensor_tensor(AL[:, i % NR, :], SG[:, i % 4, :], f32(AH[:, i % NR, :]), ALU.subtract)\
                   .then_inc(up2_lo, 1)

            def unit2_max(u):
                hg, qt = u >> 1, u & 1
                eng.wait_ge(qk2_done, u + 1)
                m = mx[:, 4 * (u % 2):4 * (u % 2) + 4]
                link(eng.tensor_reduce(m.rearrange("p (b r) -> p b r", b=2), s_view(0, qt), AX, ALU.max, negate=True))
                eng.tensor_scalar(nb[:, 4 * (u % 2):4 * (u % 2) + 4], m, HD ** -0.5, None, ALU.mult)\
                   .then_inc(nb2_ready, 1)

            def unit2_pt(u):
                if u & 1:
                    eng.wait_ge(t2_done, u + 1)
                    if u >= 2:
                        eng.wait_ge(pv2_done, u - 1)
                    eng.tensor_copy(PT2[:, u % 2, 1, :, :].rearrange("p h q -> p (h q)"), PS[:, 3, :])\
                       .then_inc(pt21_copied, 1)

            def residual_sum(n, t, h):
                wait_tile(eng, AT["wo2", 2 * h] if n == 0 else NCH - 1, t)
                o = (X1, X3)[n][:, t, 512 * h:512 * h + 512]
                k = 4 * n + 2 * t + h
                link(eng.scalar_tensor_tensor(o, o, ALPHA, PS[:, 2 * t + h, :], ALU.mult, ALU.add,
                                              accum_out=ysum[:, k:k + 1]))

            def layer_norm(n):
                y, gained = (X1, X3) if n == 0 else (X3, X1)
                gains, gains_in = ((LN1, ln1_in), (LN2, ln2_in))[n]

                def gain(t):
                    j = NT * n + t
                    eng.wait_ge(y_mean, j + 1)
                    eng.scalar_tensor_tensor(gained[:, t, :], y[:, t, :], ymean[:, j:j + 1], gains[:, 0, :],
                                             ALU.add, ALU.mult).then_inc(y_gain, 1)

                def finish(t):
                    j = NT * n + t
                    eng.wait_ge(y_rstd, j + 1)
                    eng.wait_ge(y_gain, j + 1)
                    for h in range(2):
                        half = slice(512 * h, 512 * h + 512)
                        eng.scalar_tensor_tensor(X3[:, t, half], gained[:, t, half], yrs[:, j:j + 1], gains[:, 1, half],
                                                 ALU.mult, ALU.add).then_inc(y_ln, 1)

                for t in range(NT):
                    j = NT * n + t
                    for h in range(n == 0, 2):
                        residual_sum(n, t, h)
                    m = ymean[:, j:j + 1]
                    k = 4 * n + 2 * t
                    eng.tensor_scalar(m, ysum[:, k:k + 1], ysum[:, k + 1:k + 2], -1.0 / DM, ALU.add, ALU.mult)\
                       .then_inc(y_mean, 1)
                    if t == 0:
                        eng.wait_ge(gains_in, 16)
                        gain(0)
                finish(0)
                gain(1)
                finish(1)

            eng.wait_ge(g1_in, 16)
            for t in range(NT):
                eng.wait_ge(x_rstd, t + 1)
                eng.scalar_tensor_tensor(XN[:, t, :], X0[:, t, :], rsx[:, t:t + 1], G1R[:, :], ALU.mult, ALU.mult)\
                   .then_inc(xn_ready, 1)
            evict_lo(BH, BL, XT_BANKS[0], xt_hi, xt_lo, kps=(0, 1))
            split(0)
            evict_lo(BH, BL, XT_BANKS[0], xt_hi, xt_lo, kps=(2, 3), first=2)
            split(1)
            for c in range(NCH):
                u = c - W0 - 3
                if 0 <= u < NU:
                    unit_max(u)
                if 0 <= u - 1 < NU:
                    unit_weights(u - 1)
                G = rg_group(c - W0, RG_SPLIT)
                if G is not None:
                    eng.wait_ge(h_ready, G + 1)
                    eng.wait_ge(root_ready, 2 * G + 2)
                    eng.tensor_tensor(XC[:, G % 2, :, :], TR[:, :, :], RGT[:, G % 2, :, :], ALU.mult)\
                       .then_inc(scan_ready, 1)
                if CHUNKS[c][:2] not in SUMS_FIRST:
                    split(c + 2)
                if G is not None:
                    eng.wait_ge(g_hi, G + 1)
                    eng.tensor_tensor(AL[0:RP, RG * G:RG * G + RG, :], XC[:, G % 2, :, :],
                                      f32(AH[0:RP, RG * G:RG * G + RG, :]), ALU.subtract).then_inc(g_lo, 1)
                side(c)
                if c >= W0:
                    window(c - W0)

        @block.tensor
        def _(eng):
            def transposes(src, banks, ready, done, kps=range(4), first=0, halves=False):
                for t in range(NT):
                    if not halves:
                        eng.wait_ge(ready, first + t + 1)
                    for kp in kps:
                        if halves and kp % 2 == 0:
                            eng.wait_ge(ready, 2 * t + kp // 2 + 1)
                        for kk in range(2):
                            k = 2 * kp + kk
                            o = PS[:, banks[kp], 256 * kk + P * t:256 * kk + P * t + P]
                            last = eng.transpose(o, src[:, t, P * k:P * k + P], ident)
                        if t == NT - 1:
                            last.then_inc(done, 1)

            def f_tile(out, c, col0, m, H, L, nk=KD, parts=P, lo_ready=None):
                s = c % NSLOT
                for k in range(nk):
                    if lo_ready is not None and k % 2 == 0:
                        eng.wait_ge(lo_ready, k // 2 + 1)
                    lo_, hi_ = col0 + k * m, col0 + k * m + m
                    wh, wl = WH[0:parts, s, lo_:hi_], WL[0:parts, s, lo_:hi_]
                    eng.matmul(out, wh, H[0:parts, k, :], start=(k == 0), stop=False)
                    eng.matmul(out, wh, L[0:parts, k, :], start=False, stop=False)
                    last = eng.matmul(out, wl, H[0:parts, k, :], start=False, stop=(k == nk - 1))
                return last

            def t_part(out, c, cols, ks, H, L, t, start, stop):
                s = c % NSLOT
                for n, (k, lo_) in enumerate(ks):
                    wh, wl = WH[:, s, lo_:lo_ + cols], WL[:, s, lo_:lo_ + cols]
                    h, l = H[:, k, P * t:P * t + P], L[:, k, P * t:P * t + P]
                    eng.matmul(out, h, wh, start=(start and n == 0), stop=False)
                    eng.matmul(out, h, wl, start=False, stop=False)
                    last = eng.matmul(out, l, wh, start=False, stop=(stop and n == len(ks) - 1))
                return last

            def t_half(c, banks, i, H, L, first_half=0):
                for t in range(NT):
                    last = t_part(PS[:, banks[t], :], c, 512, [(4 * (i % 2) + k, 512 * k) for k in range(4)], H, L, t,
                                  i % 2 == first_half, i % 2 != first_half)
                    if i % 2 != first_half and t == 0:
                        last.then_inc(tile0_done, 1)
                return last

            def mb_bank(m):
                if m >= 2:
                    reader, n = MB_USES[m - 2], MB_COUNTS[m - 2]
                    eng.wait_ge({"act": mb_act, "dve": mb_dve, "m": m_ready}[reader], n)
                return m % 2

            def scores(bank, qt, head_pair):
                nk = P * (qt + 1)
                for r in range(4):
                    q, k = head_pair(r, nk)
                    eng.matmul(PS[:, bank + r % 2, nk * (r // 2):nk * (r // 2) + nk], q, k, start=(r < 2), stop=False,
                               skip_group_check=True)
                for b in range(2):
                    out = PS[:, bank + b, 0:2 * nk].rearrange("p (r k) -> p r k", r=2)[:, :, P * qt:P * qt + P]
                    last = eng.matmul(out, IDR[:, :], MASKR[:, :].unsqueeze(1).broadcast_to([P, 2, P]), start=False,
                                      stop=True, skip_group_check=True)
                return last

            def unit_qk(u):
                g, qt, br = u >> 2, (u >> 1) & 1, u & 1
                if u == 0:
                    eng.wait_ge(masks_ready, 1)
                    eng.wait_ge(hk_ready, 1)
                    eng.wait_ge(hvx_ready, 1)
                else:
                    eng.wait_ge(exp_done, u)

                def head_pair(r, nk):
                    h = 4 * g + r
                    o = 64 * (h % 2)
                    return QT[o:o + 64, h // 2, P * qt:P * qt + P], KT[o:o + 64, br, g, 0:nk]

                scores(2, qt, head_pair).then_inc(qk_done, 1)

            def unit_t(u):
                qt = (u >> 1) & 1
                eng.wait_ge(p_ready, u + 1)
                if u >= 1:
                    eng.wait_ge(pt0_copied, u)
                    if n_tile1(u - 1):
                        eng.wait_ge(pt1_copied, n_tile1(u - 1))
                for kt in range(qt + 1):
                    for i in range(4):
                        last = eng.transpose(PS[:, 4 + kt, P * i:P * i + P], SM[:, u % 2, i, P * kt:P * kt + P], ident)
                last.then_inc(t_done, 1)

            def unit_pv(u):
                g, qt, br = u >> 2, (u >> 1) & 1, u & 1
                v = u >> 1
                bank = 6 + v % 2
                if br == 0:
                    if v == 0:
                        eng.wait_ge(pct_copied, 1)
                        eng.wait_ge(vb_ready, 2)
                    if v >= 2:
                        eng.wait_ge(o_lo, v - 1)
                    for pp in range(2):
                        j = 2 * (g % 2) + pp
                        eng.matmul(PS[:, bank, P * pp:P * pp + P],
                                   VB[:, g // 2, 2 * j:2 * j + 2, :].rearrange("p h d -> p (h d)"),
                                   PC[:, g // 2, P * qt:P * qt + P], start=(pp == 0), stop=False, skip_group_check=True)
                eng.wait_ge(pt0_copied, u + 1)
                if qt:
                    eng.wait_ge(pt1_copied, n_tile1(u))
                for kt in range(qt + 1):
                    for b in range(2):
                        last = eng.matmul(PS[64 * b:64 * b + 64, bank, 0:256], V[:, kt, br, HD * g:HD * g + HD],
                                          PT[:, u % 2, kt, 2 * b:2 * b + 2, :].rearrange("p r q -> p (r q)"),
                                          start=False, stop=(br == 1 and kt == qt), skip_group_check=True)
                last.then_inc(pv_done, 1)

            def window(w):
                if w == 0:
                    eng.wait_ge(hg_ready, 2)
                    eng.transpose(PS[:, 3, P:P + NGC], HG[0:NGC, 1, :], ident[0:NGC, 0:NGC])\
                       .then_inc(hgt_done, 1)
                    eng.wait_ge(hk_ready, 1)
                    eng.wait_ge(hk_zero, 1)
                    eng.wait_ge(gate_ready, 1)
                    eng.matmul(PS[0:NKV * CP, 4, 0:HD], HK[:, 0, :, :].rearrange("p g c -> p (g c)"), col("w2k", n=HD),
                               start=True, stop=True).then_inc(kc_done, 1)
                if w == 1:
                    eng.wait_ge(hvx_ready, 1)
                    eng.wait_ge(hk_zero, 2)
                    eng.wait_ge(kt_copied, 2)
                    for T in range(2):
                        eng.matmul(PS[:, 7, 64 * T:64 * T + 64], HVX[:, 8 * T:8 * T + 8, :].rearrange("p h c -> p (h c)"),
                                   col("w2v", n=HD), start=True, stop=True).then_inc(kc_done, 1)
                if w == 1:
                    eng.wait_ge(knc_ready, 1)
                    eng.wait_ge(qss_copied, 1)
                    eng.transpose(PS[:, 5, 0:NKV * CP], KNC[:, :, :].rearrange("p a d -> p (a d)"),
                                  ident[0:NKV * CP, 0:NKV * CP]).then_inc(kct_done, 1)
                if w == 2:
                    eng.wait_ge(kcz_ready, 1)
                    for tt in range(NT):
                        for j in range(KD):
                            last = eng.matmul(PS[:, 5, 256 * tt + 32 * j:256 * tt + 32 * j + 32],
                                              QT[:, j, P * tt:P * tt + P],
                                              KCZ[:, j // 2, :, :].rearrange("p a c -> p (a c)"), start=True, stop=True)
                    last.then_inc(sc_done, 1)
                if w == 4:
                    eng.wait_ge(pc_ready, 1)
                    for T in range(2):
                        for tt in range(NT):
                            last = eng.transpose(PS[:, 6, 256 * T + P * tt:256 * T + P * tt + P],
                                                 SC[:, tt, 8 * T:8 * T + 8, :].rearrange("p h c -> p (h c)"), ident)
                    last.then_inc(pct_done, 1)
                if 0 <= w - 4 < NU:
                    unit_t(w - 4)
                if 0 <= w - 5 < NU:
                    unit_pv(w - 5)

            def unit2_qk(u):
                hg, qt = u >> 1, u & 1
                if u == 0:
                    eng.wait_ge(qkt_copied, 2)
                else:
                    eng.wait_ge(exp2_done, u)

                def head_pair(r, nk):
                    h = 4 * hg + r
                    o = 64 * (h % 2)
                    return QK2[o:o + 64, 0, h // 2, P * qt:P * qt + P], QK2[o:o + 64, 1, h // 2, 0:nk]

                scores(0, qt, head_pair).then_inc(qk2_done, 1)

            def unit2_t(u):
                qt = u & 1
                eng.wait_ge(exp2_done, u + 1)
                if u >= 1:
                    eng.wait_ge(pt20_copied, u)
                if u // 2:
                    eng.wait_ge(pt21_copied, u // 2)
                for kt in range(qt + 1):
                    for i in range(4):
                        last = eng.transpose(PS[:, 2 + kt, P * i:P * i + P], SM2[:, u % 2, i, P * kt:P * kt + P], ident)
                last.then_inc(t2_done, 1)

            def unit2_pv(u):
                hg, qt = u >> 1, u & 1
                eng.wait_ge(pt20_copied, u + 1)
                if qt:
                    eng.wait_ge(pt21_copied, u // 2 + 1)
                if u == 0:
                    eng.wait_ge(z_ready, NT)
                    eng.wait_ge(v2_copied, NT)
                for i in range(4):
                    h = 4 * hg + 2 * (i % 2) + i // 2
                    for kt in range(qt + 1):
                        last = eng.matmul(PS[:, 4 + qt, HD * h:HD * h + HD], PT2[:, u % 2, kt, i, :],
                                          V2[:, kt, HD * h:HD * h + HD], start=(kt == 0), stop=(kt == qt))
                last.then_inc(pv2_done, 1)

            def transpose_heads(b, bank):
                for j in range(4):
                    for t in range(NT):
                        eng.wait_ge(roped, NT * b + t + 1)
                        last = eng.transpose(PS[:, bank + j // 2, 256 * (j % 2) + P * t:256 * (j % 2) + P * t + P],
                                             RQK[:, b, t, P * j:P * j + P], ident)
                last.then_inc(qkt_done, 1)

            def main(c):
                kind, i, _, is_split = CHUNKS[c]
                if is_split:
                    eng.wait_ge(w_lo, SPLIT_NO[c] + 1)
                else:
                    n = PLAIN.index(c)
                    eng.wait_ge(plain_in[n % 2], 16 * (n // 2 + 1))
                if kind == "kv":
                    eng.wait_ge(xt_lo, (2, 4)[i > 0])
                    b = 4 + 2 * (i // 2)
                    last = t_half(c, (b, b + 1), i, BH, BL)
                if kind == "cmp":
                    m = MB_NO[c]
                    bank = mb_bank(m)
                    for j in range(2):
                        last = f_tile(PS[:, bank, 256 * j:256 * j + 256], c, 1024 * j, P, BH, BL)
                if kind == "gate":
                    eng.wait_ge(kn_ready, 2)
                    eng.wait_ge(k_sq, 2)
                    last = f_tile(PS[0:3 * NH, 4, 0:TOK], c, 0, 3 * NH, BH, BL)
                if kind == "q":
                    bank = mb_bank(MB_NO[c])
                    for j in range(2):
                        last = f_tile(PS[:, bank, 256 * j:256 * j + 256], c, 1024 * j, P, BH, BL)
                if kind == "w1":
                    if i == 0:
                        eng.wait_ge(kt_copied, 1)
                    w = plain(c).rearrange("p (l n) -> p l n", l=16)
                    eng.wait_ge(xw_ready, 2 * i + 2)
                    for l in range(16):
                        last = eng.matmul(PS[0:NGC, 2 + i, 0:P], XW[:, i, l, 0:NGC], w[:, l, :], start=(l == 0),
                                          stop=(l == 15))
                if kind == "rnn":
                    bank = mb_bank(MB_NO[c])
                    for j in range(2):
                        last = f_tile(PS[0:RP, bank, 256 * j:256 * j + 256], c, KD * RP * j, RP, BH, BL)
                if kind == "mg":
                    bank = mb_bank(MB_NO[c])
                    for j in range(2):
                        last = f_tile(PS[:, bank, 256 * j:256 * j + 256], c, 1024 * j, P, BH, BL)
                if kind == "ri":
                    eng.wait_ge(mb_dve, RG * (i + 1))
                    for t in range(RG):
                        bank = mb_bank(MB_NO[c] + t)
                        for which in range(2):
                            for n, ti in enumerate(ADJ[t]):
                                e = len(ADJ_LIST) * which + ADJ_LIST.index((t, ti))
                                last = eng.matmul(PS[0:RP, bank, 256 * which:256 * which + 256],
                                                  plain(c)[0:RP, RP * e:RP * e + RP], XC[:, i % 2, ti, :],
                                                  start=(n == 0), stop=(n == len(ADJ[t]) - 1))
                        if t < RG - 1:
                            last.then_inc(ri_part, 1)
                if kind == "ao":
                    if i == 0:
                        eng.wait_ge(o_lo, 8)
                    bank = mb_bank(MB_NO[c])
                    for j in range(2):
                        last = f_tile(PS[:, bank, 256 * j:256 * j + 256], c, 1024 * j, P, CH, CL)
                if kind == "ro":
                    if i == 0:
                        eng.wait_ge(g_lo, NG)
                    bank = mb_bank(MB_NO[c])
                    last = f_tile(PS[:, bank, 0:256], c, 0, P, AH, AL, nk=NR, parts=RP)
                if kind == "wo":
                    if i % 2 == 0:
                        eng.wait_ge(m_lo, 4)
                    else:
                        eng.wait_ge(m_lo, 8)
                    b = 2 + 2 * (i // 2)
                    last = t_half(c, (b, b + 1), i, BH, BL)
                if kind == "up":
                    if i >= 4:
                        eng.wait_ge(up_conv, i - 3)
                    for v in range(2):
                        last = f_tile(PS[:, UP_BANKS[i % 4], 256 * v:256 * v + 256], c, 1024 * v, P, CH, CL,
                                      lo_ready=xt2_lo if i == 0 and v == 0 else None)
                if kind in ("dn", "dn2"):
                    first_bank, lo_s, n_all = (2, up_lo, N_UP // 2) if kind == "dn" else (0, up2_lo, N_UP2 // 2)
                    eng.wait_ge(lo_s, 2 * i + 2)
                    for t in range(NT):
                        for n in range(2):
                            last = t_part(PS[:, first_bank + 2 * t + n, :], c, 512,
                                          [((2 * i + k) % NR, 1024 * k + 512 * n) for k in range(2)], AH, AL, t,
                                          i == 0, i == n_all - 1)
                        if i == n_all - 1 and t == 0:
                            last.then_inc(tile0_done, 1)
                if kind == "in2":
                    b = i // 2
                    eng.wait_ge(xt3_lo, (2, 4)[i > 0])
                    if i == 0:
                        eng.wait_ge(x2_ready, NT)
                    if i == 6:
                        eng.wait_ge(rope_parts, 4)
                    if i == 8:
                        eng.wait_ge(v2_copied, NT)
                    last = t_half(c, (IN2_BANKS[b], IN2_BANKS[b] + 1), i, BH, BL)
                if kind == "wo2":
                    if i == 1:
                        eng.wait_ge(mrt_lo, 2)
                        eng.wait_ge(pt21_copied, NU2 // 2)
                    if i == 0:
                        eng.wait_ge(mrt_lo, 4)
                    last = t_half(c, (i // 2, 2 + i // 2), i, CH, CL, first_half=1)
                if kind == "up2":
                    if i >= 4:
                        eng.wait_ge(up2_prod, i - 3)
                    for v in range(2):
                        last = f_tile(PS[:, UP2_BANKS[i % 4], 256 * v:256 * v + 256], c, 1024 * v, P, BH, BL,
                                      lo_ready=xt4_lo if i == 0 and v == 0 else None)

                last.then_inc(chunk_done, 1)

            def keep_clock(n, bank, held):
                for _ in range(n):
                    eng.matmul(PS[:, bank, :], IDR[:, :], held[:, 0:2, :].rearrange("p k t -> p (k t)"), start=True, stop=True)

            def q_sums(i):
                eng.wait_ge(mb_act, MB_COUNTS[MB_NO[AT["q", i]]])
                for j in range(2):
                    for tt in range(NT):
                        h = 2 * (2 * i + j)
                        last = eng.matmul(PS[:, 5, NH * tt + h:NH * tt + h + 2], QSQ[:, j, P * tt:P * tt + P],
                                          const("ind2"), start=True, stop=True)
                last.then_inc(qss_done, 1)

            def after(c):
                kind, i, _, _ = CHUNKS[c]
                if kind == "cmp":
                    eng.wait_ge(kn_ready, 2 * i + 2)
                    for g in range(NKV):
                        for t in range(NT):
                            o = 256 * (g % 2) + P * t
                            last = eng.transpose(PS[:, (2, 6)[i] + g // 2, o:o + P],
                                                 KN[:, i, t, g, :, :].rearrange("p a d -> p (a d)"), ident)
                    last.then_inc(kt_done, 1)
                if kind == "q" and i == 0:
                    eng.wait_ge(gate_tanh, 1)
                    for t in range(NT):
                        last = eng.transpose(PS[:, 4, TOK + 3 * NH * t:TOK + 3 * NH * t + 3 * NH], GTT[:, P * t:P * t + P],
                                             ident[0:3 * NH, 0:3 * NH])
                    last.then_inc(gate_t_done, 1)
                if kind == "q" and i:
                    q_sums(i - 1)
                if kind == "w1" and i == 0:
                    q_sums(3)
                if kind == "w1" and i == 1:
                    eng.wait_ge(hg_ready, 1)
                    eng.transpose(PS[:, 2, P:P + NGC], HG[0:NGC, 0, :], ident[0:NGC, 0:NGC])\
                       .then_inc(hgt_done, 1)
                if kind == "wo" and i == 3:
                    keep_clock(12, 6, BH)
                    transposes(XN2, XT_BANKS[2], xn2_ready, xt2_done, halves=True)
                    keep_clock(2, 2, BH)
                if kind == "dn" and i == N_UP // 2 - 1:
                    transposes(X1, XT_BANKS[3], x2_ready, xt3_done)
                    keep_clock(5, 2, CH)
                if kind == "in2":
                    if i == 3:
                        transpose_heads(0, 0)
                    if i == 4:
                        eng.wait_ge(rope_parts, 2)
                        transpose_heads(1, 2)
                    if i == 5:
                        unit2_qk(0)
                    if i == 6:
                        unit2_t(0)
                        unit2_qk(1)
                    if i == 7:
                        unit2_t(1)
                        unit2_qk(2)
                    if i == 8:
                        unit2_pv(0)
                        unit2_pv(1)
                        unit2_t(2)
                        unit2_qk(3)
                    if i == 9:
                        unit2_t(3)
                        eng.wait_ge(zn_ready, NT)
                        eng.wait_ge(ws_ready, 1)
                        for g in range(8):
                            last = eng.matmul(PS[:, g // 4, P * (g % 4):P * (g % 4) + P], WS[:, g, :],
                                              ZT[:, :, HD * g:HD * g + HD], start=True, stop=True)
                        last.then_inc(mix_done, 1)
                        unit2_pv(2)
                        unit2_pv(3)
                        keep_clock(6, 2, BH)
                        transposes(MR, XT_BANKS["m"], mr_ready, mrt_done, kps=(2, 3))
                        keep_clock(5, 0, BH)
                if kind == "wo2" and i == 1:
                    transposes(MR, XT_BANKS["m"], mr_ready, mrt_done, kps=(0, 1), first=NT)
                if kind == "wo2" and i == 2:
                    keep_clock(8, 4, CH)
                    transposes(X3, XT_BANKS[4], y_ln, xt4_done, halves=True)
                    keep_clock(2, 0, CH)

            eng.wait_ge(const_in, 16)
            transposes(XN, XT_BANKS[0], xn_ready, xt_done)
            for _ in range(8):
                eng.matmul(PS[:, 4, 0:TOK], ident, XN[:, 0, 0:TOK], start=True, stop=True)
            for c in range(NCH):
                if 0 <= c - W0 - 3 < NU:
                    unit_qk(c - W0 - 3)
                main(c)
                after(c)
                if c >= W0:
                    window(c - W0)


def _f(w):
    return w.reshape(-1, P, w.shape[1]).transpose(1, 0, 2)


def kernel(**inputs):
    import numpy as np
    import concourse.bacc as bacc
    from concourse.bass_utils import run_bass_kernel_spmd as run

    a = {k: np.asarray(v) for k, v in inputs.items()}
    w_in = a["w_in"]
    kvw = NKV * HD
    sizes = [D_RNN, D_RNN, DM] + [kvw] * 6 + [3 * NH, DM, DM]
    offs = np.concatenate([[0], np.cumsum(sizes)])
    (rx, rgate, q, kc, vc, ks, vs, kw, vw, gates, mg_rnn, mg_attn) = (
        w_in[:, offs[n]:offs[n + 1]] for n in range(len(sizes)))
    mgs = np.concatenate([mg_rnn, mg_attn], 1)
    rows = []

    def f_pair(w0, w1):
        return np.concatenate([_f(w0).reshape(P, -1), _f(w1).reshape(P, -1)], 1)

    def t_half(w, i):
        n, kh = divmod(i, 2)
        return _f(w[512 * kh:512 * kh + 512, 512 * n:512 * n + 512]).reshape(P, -1)

    def tile(w, m, width=P):
        return w[:, width * m:width * m + width]

    def gates_blocks(g):
        out = np.zeros((P, 2, len(ADJ_LIST), RP), np.float32)
        span = RG * RP
        for which, w in enumerate((a["rg_w_a"], a["rg_w_x"])):
            dense = np.zeros((span, span), np.float32)
            for b in range(span // RB):
                dense[RB * b:RB * b + RB, RB * b:RB * b + RB] = w[g * (span // RB) + b]
            for e, (to, ti) in enumerate(ADJ_LIST):
                out[0:RP, which, e] = dense[RP * ti:RP * ti + RP, RP * to:RP * to + RP]
        return out.reshape(P, -1)

    for kind, i, width, _ in CHUNKS:
        if kind == "kv":
            r = t_half(np.concatenate([ks, vs, kw, vw], 1), i)
        elif kind == "cmp":
            w = (kc, vc)[i]
            r = f_pair(tile(w, 0), tile(w, 1))
        elif kind == "gate":
            r = _f(gates).reshape(P, -1)
        elif kind == "q":
            r = f_pair(tile(q, 2 * i), tile(q, 2 * i + 1))
        elif kind == "w1":
            r = _f(a[("cmp_w1_k", "cmp_w1_v")[i]]).reshape(P, -1)
        elif kind == "rnn":
            r = f_pair(tile(rx, i, RP), tile(rgate, i, RP))
        elif kind == "mg":
            r = f_pair(tile(mgs, 2 * i), tile(mgs, 2 * i + 1))
        elif kind == "ri":
            r = gates_blocks(i)
        elif kind == "ao":
            r = f_pair(tile(a["w_attn_out"], 2 * i), tile(a["w_attn_out"], 2 * i + 1))
        elif kind == "ro":
            r = np.zeros((P, NR, P), np.float32)
            r[0:RP] = tile(a["w_rnn_out"], i).reshape(NR, RP, P).transpose(1, 0, 2)
            r = r.reshape(P, -1)
        elif kind == "wo":
            r = t_half(a["w_out"], i)
        elif kind == "up":
            r = f_pair(tile(a["w_up"], i), tile(a["w_up"], N_UP + i))
        elif kind == "dn":
            r = _f(a["w_down"][256 * i:256 * i + 256]).reshape(P, -1)
        elif kind == "in2":
            r = t_half(a["w_in_2"][0], (i, i + 2 if i < 8 else i - 2)[i >= 6])
        elif kind == "wo2":
            r = t_half(a["w_out_2"][0], i)
        elif kind == "up2":
            r = f_pair(tile(a["w_gate_2"][0], i), tile(a["w_up_2"][0], i))
        elif kind == "dn2":
            r = _f(a["w_down_2"][0][256 * i:256 * i + 256]).reshape(P, -1)
        assert r.shape == (P, width), (kind, r.shape)
        rows.append(np.ascontiguousarray(r).reshape(-1))
    stream = np.concatenate(rows)

    cols = np.zeros((P, NCOLS), np.float32)

    def place(name, block):
        cols[0:block.shape[0], COLS[name][0]:COLS[name][0] + block.shape[1]] = block

    place("cw", a["rnn_conv_w"].reshape(4 * NR, RP).T)
    for name, key in (("cb", "rnn_conv_b"), ("ba", "rg_b_a"), ("bx", "rg_b_x"), ("lam", "lru_lambda")):
        place(name, a[key].reshape(NR, RP).T)
    place("fw", a["ffn_conv_w"].reshape(3 * 2 * N_UP, P).T)
    place("fb", a["ffn_conv_b"].reshape(2 * N_UP, P).T)
    for name, key in (("gq", "q_norm_g"), ("gkc", "k_cmp_norm_g"), ("gks", "k_slc_norm_g"), ("gkw", "k_win_norm_g")):
        place(name, np.concatenate([a[key], a[key]])[:, None])
    place("bs", a["b_spatial_2"][0].T)
    place("pek", a["cmp_pe_k"].reshape(16, P).T)
    place("pev", a["cmp_pe_v"].reshape(16, P).T)
    place("w2k", a["cmp_w2_k"])
    place("w2v", a["cmp_w2_v"])

    consts = np.zeros((P, NCONST), np.float32)

    def fixed(name, block):
        consts[:, CONSTS[name][0]:CONSTS[name][1]] = block

    pos = np.arange(TOK)
    fixed("ident", np.eye(P))
    fixed("mask", np.where(pos[None, :P] <= pos[:P, None], 0.0, NEG))
    ends = np.arange(CP) * CMP_STRIDE + 31
    seen = (ends[None, :] <= pos[:, None]) & (np.arange(CP) < NC)[None, :]
    seen = seen.reshape(NT, P, CP).transpose(1, 0, 2).reshape(P, -1)
    fixed("cadd", np.where(seen, 0.0, NEG))
    fixed("c01", seen.astype(np.float32))
    fixed("m8", (np.arange(P)[:, None] // CP == np.arange(8)[None, :]))
    fixed("ind2", (np.arange(P)[:, None] // HD == np.arange(2)[None, :]))
    inv = (np.float32(10000.0) ** (-np.arange(0, HD, 2, dtype=np.float32) / np.float32(HD))).astype(np.float32)
    ang = pos.astype(np.float32)[:, None] * inv[None, :]
    cos, sin = np.cos(ang).astype(np.float32), np.sin(ang).astype(np.float32)
    for name, t in (("cos", np.concatenate([cos, cos], 1)), ("sin", np.concatenate([-sin, sin], 1))):
        fixed(name, t.reshape(NT, P, HD).transpose(1, 0, 2).reshape(P, -1))

    def row(*keys):
        return np.concatenate([a[k].reshape(-1) for k in keys])

    arrays = {
        "w_stream": stream,
        "x": np.ascontiguousarray(a["x"].reshape(TOK, DM)),
        "cols": cols,
        "consts": consts,
        "g1": row("norm1_g"),
        "g2": row("norm2_g"),
        "og": row("attn_out_g_2", "gmlp_out_g_2"),
        "gln": row("gmlp_ln_g_2", "gmlp_ln_b_2"),
        "ln1": row("ln1_g_2", "ln1_b_2"),
        "ln2": row("ln2_g_2", "ln2_b_2"),
        "ws": np.ascontiguousarray(a["w_spatial_2"][0].transpose(2, 0, 1)),
    }
    nc = bacc.Bacc("TRN2", target_bir_lowering=False, num_devices=1)
    aps = [nc.dram_tensor("in_" + k, v.shape, F32, kind="ExternalInput").ap() for k, v in arrays.items()]
    out = nc.dram_tensor("out_y", (TOK, DM), F32, kind="ExternalOutput").ap()
    two_block_program(nc, *aps, out)
    r = run(nc, [{"in_" + k: v for k, v in arrays.items()}], core_ids=[0])
    return r.results[0]["out_y"].reshape(1, TOK, DM)
```
